# Optimizing a Trainium2 kernel written in Bass

```python
import jax, jax.numpy as jnp
from jax import lax
import numpy as np

D_MODEL = 1024
BATCH = 1
SEQ = 256
DEPTH = 2

N_HEADS = 16
HEAD_DIM = D_MODEL // N_HEADS
N_A_LAYERS = DEPTH // 2
N_B_LAYERS = DEPTH - N_A_LAYERS
SB_Q_BLOCK = 128
MOBA_BLOCK = 256
MOBA_TOPK = 3
MOBA_Q_CHUNK = 64
N_GROUPS = 4
EXPERTS_PER_GROUP = 4
N_EXPERTS = N_GROUPS * EXPERTS_PER_GROUP
TOPK_IN_GROUP = 2
EXPERT_FF = 256
RMS_EPS = 1e-6
ALIBI_MAX_BIAS = 8.0

kernel_name = 'hybrid_yoco_stickbreak_moba_hmoe'

def rmsnorm(x, g):
    xf = x.astype(jnp.float32)
    y = xf * lax.rsqrt(jnp.mean(xf * xf, axis=-1, keepdims=True) + RMS_EPS)
    return (y * g.astype(jnp.float32)).astype(x.dtype)

def modulate(h, shift, scale):
    return h * (1.0 + scale[:, None, :]) + shift[:, None, :]

def split_heads(t):
    b, s, _ = t.shape
    return t.reshape(b, s, N_HEADS, HEAD_DIM).transpose(0, 2, 1, 3)

def merge_heads(t):
    b, h, s, d = t.shape
    return t.transpose(0, 2, 1, 3).reshape(b, s, h * d)

def alibi_slopes():
    return jnp.exp2(-ALIBI_MAX_BIAS * jnp.arange(1, N_HEADS + 1, dtype=jnp.float32) / N_HEADS)

def stick_breaking_attention(q, k, v):
    b, h, s, dh = q.shape
    nq = s // SB_Q_BLOCK
    scale = dh ** -0.5
    kpos = jnp.arange(s)
    qb = q.reshape(b, h, nq, SB_Q_BLOCK, dh).transpose(2, 0, 1, 3, 4)

    def block(args):
        qblk, i = args
        qpos = i * SB_Q_BLOCK + jnp.arange(SB_Q_BLOCK)
        z = jnp.einsum('bhqd,bhkd->bhqk', qblk, k).astype(jnp.float32) * scale
        past = kpos[None, :] < qpos[:, None]
        log_keep = jnp.where(past, jax.nn.log_sigmoid(-z), 0.0)
        suffix = lax.cumsum(log_keep, axis=3, reverse=True) - log_keep
        w = jnp.where(past, jnp.exp(jax.nn.log_sigmoid(z) + suffix), 0.0)
        return jnp.einsum('bhqk,bhkd->bhqd', w.astype(v.dtype), v)

    out = lax.map(block, (qb, jnp.arange(nq)))
    return out.transpose(1, 2, 0, 3, 4).reshape(b, h, s, dh)

def moba_attention(q, k_blocks, v_blocks, k_means, slopes):
    b, h, s, dh = q.shape
    nb = k_blocks.shape[2]
    topk = min(MOBA_TOPK, nb)
    nc = s // MOBA_Q_CHUNK
    scale = dh ** -0.5
    qc = q.reshape(b, h, nc, MOBA_Q_CHUNK, dh).transpose(2, 0, 1, 3, 4)
    blk_ids = jnp.arange(nb)
    in_blk = jnp.arange(MOBA_BLOCK)
    gather = jax.vmap(jax.vmap(lambda blocks, idx: blocks[idx]))

    def chunk(args):
        qblk, i = args
        qpos = i * MOBA_Q_CHUNK + jnp.arange(MOBA_Q_CHUNK)
        own = (i * MOBA_Q_CHUNK) // MOBA_BLOCK
        gate = jnp.einsum('bhqd,bhnd->bhqn', qblk, k_means).astype(jnp.float32)
        gate = jnp.where(blk_ids < own, gate, -jnp.inf)
        _, gidx = lax.top_k(gate, topk)
        valid = gidx < own
        ks = gather(k_blocks, gidx)
        vs = gather(v_blocks, gidx)
        ls = jnp.einsum('bhqd,bhqnkd->bhqnk', qblk, ks).astype(jnp.float32) * scale
        kpos_sel = gidx[..., None] * MOBA_BLOCK + in_blk
        dist_sel = (qpos[:, None, None] - kpos_sel).astype(jnp.float32)
        ls = ls - slopes[None, :, None, None, None] * dist_sel
        ls = jnp.where(valid[..., None], ls, -jnp.inf).reshape(b, h, MOBA_Q_CHUNK, topk * MOBA_BLOCK)
        k_own = lax.dynamic_index_in_dim(k_blocks, own, axis=2, keepdims=False)
        v_own = lax.dynamic_index_in_dim(v_blocks, own, axis=2, keepdims=False)
        lo = jnp.einsum('bhqd,bhkd->bhqk', qblk, k_own).astype(jnp.float32) * scale
        dist_own = qpos[:, None] - (own * MOBA_BLOCK + in_blk)[None, :]
        lo = jnp.where(dist_own >= 0,
                       lo - slopes[None, :, None, None] * dist_own.astype(jnp.float32),
                       -jnp.inf)
        p = jax.nn.softmax(jnp.concatenate([ls, lo], axis=-1), axis=-1)
        p_sel = p[..., :topk * MOBA_BLOCK].reshape(b, h, MOBA_Q_CHUNK, topk, MOBA_BLOCK)
        p_own = p[..., topk * MOBA_BLOCK:]
        return (jnp.einsum('bhqnk,bhqnkd->bhqd', p_sel.astype(vs.dtype), vs)
                + jnp.einsum('bhqk,bhkd->bhqd', p_own.astype(v_own.dtype), v_own))

    out = lax.map(chunk, (qc, jnp.arange(nc)))
    return out.transpose(1, 2, 0, 3, 4).reshape(b, h, s, dh)

def shared_kv(x, c, w_ada_kv, b_ada_kv, g_kv, w_kv):
    b, s, d = x.shape
    shift, scale = jnp.split(c @ w_ada_kv + b_ada_kv, 2, axis=-1)
    hkv = modulate(rmsnorm(x, g_kv), shift, scale)
    kv = hkv @ w_kv
    k = split_heads(kv[..., :d])
    v = split_heads(kv[..., d:])
    n_blocks = -(-s // MOBA_BLOCK)
    pad = n_blocks * MOBA_BLOCK - s
    k = jnp.pad(k, ((0, 0), (0, 0), (0, pad), (0, 0)))
    v = jnp.pad(v, ((0, 0), (0, 0), (0, pad), (0, 0)))
    k_blocks = k.reshape(b, N_HEADS, n_blocks, MOBA_BLOCK, HEAD_DIM)
    v_blocks = v.reshape(b, N_HEADS, n_blocks, MOBA_BLOCK, HEAD_DIM)
    k_means = jnp.mean(k_blocks.astype(jnp.float32), axis=3).astype(k.dtype)
    return k_blocks, v_blocks, k_means

def hier_moe(h, w_rg, b_rg, w_re, b_re, w_gate, w_up, w_down):
    b, s, d = h.shape
    t = h.reshape(b * s, d)
    n_tok = t.shape[0]
    tok = jnp.arange(n_tok)
    lg = (t @ w_rg + b_rg).astype(jnp.float32)
    pg = jax.nn.softmax(lg, axis=-1)
    g_sel = jnp.argmax(lg, axis=-1)
    p_g = pg[tok, g_sel][:, None]
    le = (t @ w_re + b_re).astype(jnp.float32).reshape(n_tok, N_GROUPS, EXPERTS_PER_GROUP)
    le_g = le[tok, g_sel]
    ve, ie = lax.top_k(le_g, TOPK_IN_GROUP)
    pe = jax.nn.softmax(ve, axis=-1) * p_g
    eid = g_sel[:, None] * EXPERTS_PER_GROUP + ie
    combine = jnp.sum(jax.nn.one_hot(eid, N_EXPERTS, dtype=jnp.float32) * pe[..., None], axis=1)
    hg = jnp.einsum('td,edf->tef', t, w_gate)
    hu = jnp.einsum('td,edf->tef', t, w_up)
    hid = jax.nn.silu(hg) * hu * combine[:, :, None].astype(t.dtype)
    out = jnp.einsum('tef,efd->td', hid, w_down)
    return out.reshape(b, s, d)

def setup_inputs(seed: int = 0) -> dict:
    key = jax.random.key(seed)
    ks = jax.random.split(key, 24)
    D = D_MODEL
    nA = max(N_A_LAYERS, 1)
    nB = max(N_B_LAYERS, 1)

    def nrm(k, shape, fan_in, gain=1.0):
        return jax.random.normal(k, shape, jnp.float32) * (gain * fan_in ** -0.5)

    def gain(k, shape):
        return 1.0 + 0.02 * jax.random.normal(k, shape, jnp.float32)

    def small(k, shape, s=0.01):
        return s * jax.random.normal(k, shape, jnp.float32)

    return {
        'x': jax.random.normal(ks[0], (BATCH, SEQ, D), jnp.float32),
        'c': jax.random.normal(ks[1], (BATCH, D), jnp.float32),
        'w_ada': nrm(ks[2], (DEPTH, D, 6 * D), D, 0.1),
        'b_ada': small(ks[3], (DEPTH, 6 * D)),
        'g_attn': gain(ks[4], (DEPTH, D)),
        'g_ffn': gain(ks[5], (DEPTH, D)),
        'w_qkv_a': nrm(ks[6], (nA, D, 3 * D), D),
        'w_o_a': nrm(ks[7], (nA, D, D), D),
        'w_ada_kv': nrm(ks[8], (D, 2 * D), D, 0.1),
        'b_ada_kv': small(ks[9], (2 * D,)),
        'g_kv': gain(ks[10], (D,)),
        'w_kv': nrm(ks[11], (D, 2 * D), D),
        'w_q_b': nrm(ks[12], (nB, D, D), D),
        'w_o_b': nrm(ks[13], (nB, D, D), D),
        'w_rg': nrm(ks[14], (DEPTH, D, N_GROUPS), D),
        'b_rg': small(ks[15], (DEPTH, N_GROUPS)),
        'w_re': nrm(ks[16], (DEPTH, D, N_EXPERTS), D),
        'b_re': small(ks[17], (DEPTH, N_EXPERTS)),
        'w_gate': nrm(ks[18], (DEPTH, N_EXPERTS, D, EXPERT_FF), D),
        'w_up': nrm(ks[19], (DEPTH, N_EXPERTS, D, EXPERT_FF), D),
        'w_down': nrm(ks[20], (DEPTH, N_EXPERTS, EXPERT_FF, D), EXPERT_FF),
        'g_final': gain(ks[21], (D,)),
    }

def reference(x, c, w_ada, b_ada, g_attn, g_ffn, w_qkv_a, w_o_a, w_ada_kv, b_ada_kv, g_kv, w_kv,
              w_q_b, w_o_b, w_rg, b_rg, w_re, b_re, w_gate, w_up, w_down, g_final):
    b, s, d = x.shape
    slopes = alibi_slopes()
    k_blocks = v_blocks = k_means = None
    for l in range(DEPTH):
        mod = c @ w_ada[l] + b_ada[l]
        sh_m, sc_m, gt_m, sh_f, sc_f, gt_f = jnp.split(mod, 6, axis=-1)
        h = modulate(rmsnorm(x, g_attn[l]), sh_m, sc_m)
        if l < N_A_LAYERS:
            qkv = (h @ w_qkv_a[l]).reshape(b, s, 3, N_HEADS, HEAD_DIM).transpose(2, 0, 3, 1, 4)
            o = merge_heads(stick_breaking_attention(qkv[0], qkv[1], qkv[2])) @ w_o_a[l]
        else:
            j = l - N_A_LAYERS
            q = split_heads(h @ w_q_b[j])
            o = merge_heads(moba_attention(q, k_blocks, v_blocks, k_means, slopes)) @ w_o_b[j]
        x = x + (1.0 + gt_m)[:, None, :] * o
        h = modulate(rmsnorm(x, g_ffn[l]), sh_f, sc_f)
        x = x + (1.0 + gt_f)[:, None, :] * hier_moe(h, w_rg[l], b_rg[l], w_re[l], b_re[l],
                                                   w_gate[l], w_up[l], w_down[l])
        if l == N_A_LAYERS - 1:
            k_blocks, v_blocks, k_means = shared_kv(x, c, w_ada_kv, b_ada_kv, g_kv, w_kv)
    return rmsnorm(x, g_final)


_drawn_inputs = setup_inputs


def setup_inputs(seed=0):
    import zlib

    import numpy as np

    out = dict(_drawn_inputs(seed))
    spreads = {}
    factors = {'b_ada_kv': 3.217, 'g_kv': 3.632, 'b_rg': 8.0, 'b_re': 5.717, 'g_final': 2.744}
    for name, (base, spread) in spreads.items():
        noise = np.random.default_rng([zlib.crc32(name.encode()), seed]).standard_normal(out[name].shape)
        drawn = base * np.exp(spread * noise) if base else spread * noise
        out[name] = __import__('jax').numpy.asarray(drawn.astype(out[name].dtype))
    for name, factor in factors.items():
        out[name] = (out[name] * factor).astype(out[name].dtype)
    return out
```

```python
from contextlib import ExitStack

import concourse.bass as bass
from concourse import mybir

F32 = mybir.dt.float32
I32 = mybir.dt.int32
ALU = mybir.AluOpType
ACT = mybir.ActivationFunctionType
AX_X = mybir.AxisListType.X

P = 128
D = 1024
T = 256
TT = T // P
KC = D // P
HEADS = 16
HD = D // HEADS
PAIRS = HEADS // 2
GROUPS = 4
PER_GROUP = 4
EXPERTS = GROUPS * PER_GROUP
FF = 256
FC = FF // P
EPS = 1e-6
SCALE = HD ** -0.5
NEG = -1.0e30
CAUSAL = T + P
COLS = 256
UNITS = D // COLS
WSLOTS = 12
ASLOTS = 3
VECS = 14
PARTS = 4
ROWS = KC // PARTS
DEPTH = 2

SHIFT_M, SCALE_M, GATE_M, SHIFT_F, SCALE_F, GATE_F = range(6)
KV_SHIFT, KV_SCALE = 6, 7


def vec(layer, which):
    return which if layer == 0 else 8 + which


def is_gate(v):
    return v in (vec(0, GATE_M), vec(0, GATE_F), vec(1, GATE_M), vec(1, GATE_F))


def is_scale(v):
    return v in (vec(0, SCALE_M), vec(0, SCALE_F), KV_SCALE, vec(1, SCALE_M), vec(1, SCALE_F))


GROUP_LOADS = [("gate", 0), ("up", 0), ("gate", 1), ("up", 1), ("down", 0), ("gate", 2), ("up", 2), ("down", 1),
               ("gate", 3), ("up", 3), ("down", 2), ("down", 3)]
assert len(GROUP_LOADS) == WSLOTS

QKV0 = [("qkv", u) for u in range(12)]
O0 = [("o0", u) for u in range(4)]
KVQ1 = [("kvq", u) for u in range(12)]
O1 = [("o1", u) for u in range(4)]


def sum_items(v):
    return [("sum", v, 0), ("sum", v, 1)] if is_gate(v) else [("sum", v, 0)]


SUM_AFTER_QKV0 = {6: 2, 10: 3}
SUM_AFTER_HEAD0 = {0: 4, 5: 5, 9: 6, 13: 7}
SUM_AFTER_KVQ1 = {6: 10, 10: 11}
SUM_AFTER_HEAD1 = {0: 12, 12: 13}


def out_items():
    items = sum_items(0) + sum_items(1)
    for u, item in enumerate(QKV0):
        items.append(item)
        if u in SUM_AFTER_QKV0:
            items += sum_items(SUM_AFTER_QKV0[u])
    for h in range(HEADS):
        if h in SUM_AFTER_HEAD0:
            items += sum_items(SUM_AFTER_HEAD0[h])
    items += sum_items(8)
    items += O0
    items += sum_items(9)
    items.append(("route", 0))
    for u, item in enumerate(KVQ1):
        items.append(item)
        if u in SUM_AFTER_KVQ1:
            items += sum_items(SUM_AFTER_KVQ1[u])
    for h in range(HEADS):
        if h in SUM_AFTER_HEAD1:
            items += sum_items(SUM_AFTER_HEAD1[h])
    items += O1
    items.append(("route", 1))
    return items


ITEMS = out_items()
OUT = {item: i for i, item in enumerate(ITEMS)}
VEC_ORDER = [vv for vv in range(VECS) if not is_gate(vv)]
GATE_ORDER = [vv for vv in range(VECS) if is_gate(vv)]
R_EXP1, R_EXP2, R_STEPS = 7, 21, 31
Y_GROUP = 1 + 4 * PER_GROUP
O_STEPS = 2 * UNITS
assert sorted(v for k in OUT if k[0] == "sum" for v in [k[1]] if k[2] == 0) == list(range(VECS))

FIXED_LOADS = {0: QKV0 + O0, 1: KVQ1 + O1}
MOE_LOADS = GROUPS * WSLOTS
LOAD_BASE = {0: 0, 1: len(QKV0 + O0) + MOE_LOADS}
MOE_BASE = {l: LOAD_BASE[l] + len(FIXED_LOADS[l]) for l in range(DEPTH)}
LOAD = {}
for _l in range(DEPTH):
    for _i, _item in enumerate(FIXED_LOADS[_l]):
        LOAD[_item] = LOAD_BASE[_l] + _i


def program(nc, x_in, c_in, w_ada, b_ada, g_attn, g_ffn, w_qkv_a, w_o_a, w_ada_kv, b_ada_kv, g_kv, w_kv,
            w_q_b, w_o_b, w_rg, b_rg, w_re, b_re, w_gate, w_up, w_down, g_final, out):
    ctx = ExitStack()
    with ctx:
        def sb(name, shape, dt=F32):
            return ctx.enter_context(nc.sbuf_tensor(name, shape, dt))

        def sem(name):
            return ctx.enter_context(nc.semaphore(name))

        bank = [ctx.enter_context(nc.psum_tensor(f"bank{i}", [P, 512], F32)) for i in range(8)]
        out_bank = bank[0:2]
        av_bank = bank[2:4]
        z_bank = bank[4:6]
        s_bank = bank[6:8]
        turn_bank = bank[4:8]
        gu_bank = [bank[0:2], bank[6:8]]
        y_bank = bank[2:6]

        wring = sb("wring", [P, WSLOTS, 2048])
        aring = sb("aring", [P, ASLOTS, ROWS, D])
        x = sb("x", [P, TT, D])
        xn = sb("xn", [P, TT, D])
        hT = sb("hT", [P, KC, T])
        qT = sb("qT", [P, PAIRS, T])
        kT = sb("kT", [P, PAIRS, T])
        v = sb("v", [P, TT, D])
        attnT = sb("attnT", [P, PAIRS, T])
        hkvT = attnT
        cT = sb("cT", [P, KC])
        acc = sb("acc", [P, 2, D])
        bias14 = sb("bias14", [VECS, D])
        shift = sb("shift", [P, VECS, KC])
        gains = sb("gains", [P, VECS, KC])
        gate_m = sb("gate_m", [P, D])
        gate_f = sb("gate_f", [P, D])
        gfin = gate_m
        ident = sb("ident", [P, P])
        ones = sb("ones", [P, P])
        negones = sb("negones", [P, P])
        negtri = sb("negtri", [P, P])
        maskA = sb("maskA", [P, CAUSAL])
        distB = sb("distB", [P, CAUSAL])
        distI = kT[:, 0:2, :].rearrange("p a t -> p (a t)")[:, 0:CAUSAL].bitcast(I32)
        desc = sb("desc", [P, GROUPS])
        zm = hT[:, :, :].rearrange("p k t -> p (k t)")[:, 0:4 * CAUSAL].rearrange("p (i n) -> p i n", i=4)
        xn_flat = xn[:, :, :].rearrange("p t n -> p (t n)")
        soft = xn_flat[:, 0:2 * CAUSAL].rearrange("p (i n) -> p i n", i=2)
        sp = xn_flat[:, D:D + 2 * CAUSAL].rearrange("p (i n) -> p i n", i=2)
        prob = sb("prob", [P, 2, CAUSAL])
        mx = sb("mx", [P, 2, TT])
        nmx = sb("nmx", [P, 2, TT])
        den = sb("den", [P, 2, TT])
        rden = sb("rden", [P, 2, TT])
        ss = sb("ss", [P, TT])
        ms = sb("ms", [P, TT])
        rstd = sb("rstd", [P, TT])
        rtmp = sb("rtmp", [P, 4, TT])
        otmp = v[:, :, :].rearrange("p t n -> p (t n)")[:, 0:4 * COLS].rearrange("p (i t n) -> p i t n", i=2, t=TT)
        w_r = sb("w_r", [P, DEPTH, KC, GROUPS + EXPERTS])
        b_r = sb("b_r", [P, DEPTH, GROUPS + EXPERTS])
        lg = sb("lg", [P, TT, GROUPS + EXPERTS])
        rt = sb("rt", [P, 16, TT, 4])
        r1 = sb("r1", [P, 12, TT])
        le_sel = sb("le_sel", [P, TT, EXPERTS])
        comb = sb("comb", [P, TT, EXPERTS])
        comb_g = sb("comb_g", [P, TT, PER_GROUP])
        q_flat = qT[:, :, :].rearrange("p c t -> p (c t)")
        sg = q_flat[:, 0:2 * FC * T].rearrange("p (i n) -> p i n", i=2)
        hid = q_flat[:, 2 * FC * T:4 * FC * T].rearrange("p (i n) -> p i n", i=2)
        ytmp = kT[:, :, :].rearrange("p c t -> p (c t)").rearrange("p (q n) -> p q n", q=4)

        s_x = sem("s_x")
        s_c = sem("s_c")
        s_small = sem("s_small")
        s_gfin = sem("s_gfin")
        s_const = sem("s_const")
        w_landed = [sem(f"w_landed{i}") for i in range(WSLOTS)]
        a_landed = [sem(f"a_landed{i}") for i in range(ASLOTS)]
        ada_rows = sem("ada_rows")
        out_full = sem("out_full")
        vec_ready = sem("vec_ready")
        gate_ready = sem("gate_ready")
        ss_ready = sem("ss_ready")
        rsqrt_ready = sem("rsqrt_ready")
        nrm = sem("nrm")
        turned = sem("turned")
        hT_dve = sem("hT_dve")
        hT_act = sem("hT_act")
        qkv_ready = sem("qkv_ready")
        z_full = sem("z_full")
        zm_ready = sem("zm_ready")
        act_step = sem("act_step")
        soft_ready = sem("soft_ready")
        sp_ready = sem("sp_ready")
        s_full = sem("s_full")
        t_ready = sem("t_ready")
        w_ready = sem("w_ready")
        av_full = sem("av_full")
        attn_ready = sem("attn_ready")
        b_max = sem("b_max")
        p_ready = sem("p_ready")
        b_norm = sem("b_norm")
        pT_ready = sem("pT_ready")
        o_step = sem("o_step")
        route = sem("route")
        route_exp = sem("route_exp")
        gu_full = sem("gu_full")
        silu_done = sem("silu_done")
        gu_free = sem("gu_free")
        y_full = sem("y_full")
        y_free = sem("y_free")
        y_sum = sem("y_sum")
        s_out = sem("s_out")

        wslot = [wring[:, i, :] for i in range(WSLOTS)]

        def w_cols(slot):
            return wslot[slot].rearrange("p (k n) -> p k n", k=KC)

        def w_rows(slot):
            return wslot[slot].rearrange("p (k n) -> p k n", k=FC)

        def wait_weights(eng, load, extra=0):
            eng.wait_ge(w_landed[load % WSLOTS], (extra + load // WSLOTS + 1) * 16)

        def wait_out_read(eng, i):
            kind, n = ITEMS[i][0:2]
            if kind in ("qkv", "kvq"):
                eng.wait_ge(qkv_ready, n + 1 + 12 * (kind == "kvq"))
            elif kind in ("o0", "o1"):
                eng.wait_ge(o_step, 2 * (n + UNITS * (kind == "o1")) + 1)
            elif kind == "route":
                eng.wait_ge(route, R_STEPS * n + 1)
            elif is_gate(n):
                eng.wait_ge(gate_ready, 2 * GATE_ORDER.index(n) + ITEMS[i][2] + 1)
            else:
                eng.wait_ge(vec_ready, VEC_ORDER.index(n) + 1)

        def wait_out_free(pe, i):
            if i >= 2:
                wait_out_read(pe, i - 2)

        def pk(w):
            return w.rearrange("(p k) n -> p k n", k=KC)

        def cp(w):
            return w.rearrange("(c p) n -> p c n", p=P)

        def unit_source(item):
            kind, u = item
            cols = slice(u * COLS, (u + 1) * COLS)
            if kind == "qkv":
                return pk(w_qkv_a[0])[:, :, cols]
            if kind == "o0":
                return cp(w_o_a[0])[:, :, cols]
            if kind == "kvq" and u < 2 * UNITS:
                return pk(w_kv)[:, :, cols]
            if kind == "kvq":
                cols = slice((u - 2 * UNITS) * COLS, (u - 2 * UNITS + 1) * COLS)
                return pk(w_q_b[0])[:, :, cols]
            return cp(w_o_b[0])[:, :, cols]

        def ada_source(n):
            vv, part = n // PARTS, n % PARTS
            if vv in (KV_SHIFT, KV_SCALE):
                w, j = w_ada_kv, vv - KV_SHIFT
            else:
                l, j = (0, vv) if vv < 6 else (1, vv - 8)
                w = w_ada[l]
            return pk(w)[:, part * ROWS:(part + 1) * ROWS, j * D:(j + 1) * D]

        HT_COUNT = {0: 4, 1: 8, 2: 16, 3: 20}

        def modulated(norm):
            if norm == 2:
                return [(hkvT, KV_SHIFT, KV_SCALE), (hT, vec(1, SHIFT_M), vec(1, SCALE_M))]
            return [(hT, *{0: (vec(0, SHIFT_M), vec(0, SCALE_M)), 1: (vec(0, SHIFT_F), vec(0, SCALE_F)),
                           3: (vec(1, SHIFT_F), vec(1, SCALE_F))}[norm])]

        CONSTS = 18
        SMALL = 16 * (3 + 5 + 4 * DEPTH)

        block = ctx.enter_context(nc.Block())

        @block.sync
        def _(sp_eng):
            sp_eng.dma_start(cT[:, :], c_in[0].rearrange("(p k) -> p k", k=KC)).then_inc(s_c, 16)
            for t in range(TT):
                sp_eng.dma_start(x[:, t, :], x_in[0, t * P:(t + 1) * P, :]).then_inc(s_x, 16)

            def released(load):
                for item, i in LOAD.items():
                    if i == load:
                        sp_eng.wait_ge(out_full, OUT[item] + 1)
                        return
                layer = 0 if load < LOAD_BASE[1] else 1
                g, j = divmod(load - MOE_BASE[layer], WSLOTS)
                moe_released(layer, j, g)

            def moe_released(layer, j, g):
                kind, e = GROUP_LOADS[j]
                if kind == "down":
                    sp_eng.wait_ge(y_full, g * 4 * PER_GROUP + (layer * EXPERTS + e) * 4 + 4)
                else:
                    sp_eng.wait_ge(gu_full, g * 2 * PER_GROUP + (layer * EXPERTS + e) * 2 + 1 + (kind == "up"))

            def expert_load(layer, j, g):
                kind, e = GROUP_LOADS[j]
                load = MOE_BASE[layer] + j
                src = {"gate": w_gate, "up": w_up, "down": w_down}[kind]
                one = src[layer, bass.ds(g * PER_GROUP + e, 1)].rearrange("o r n -> (o r) n")
                slot = load % WSLOTS
                if kind == "down":
                    sp_eng.dma_start(w_rows(slot), cp(one)).then_inc(w_landed[slot], 16)
                else:
                    sp_eng.dma_start(w_cols(slot), pk(one)).then_inc(w_landed[slot], 16)

            for layer in range(DEPTH):
                for item in FIXED_LOADS[layer]:
                    load = LOAD[item]
                    if load >= WSLOTS:
                        released(load - WSLOTS)
                    sp_eng.dma_start(w_cols(load % WSLOTS), unit_source(item)).then_inc(w_landed[load % WSLOTS], 16)
                for j in range(WSLOTS):
                    released(MOE_BASE[layer] + j - WSLOTS)
                    expert_load(layer, j, 0)
                with sp_eng.Fori(1, GROUPS) as g:
                    for j in range(WSLOTS):
                        moe_released(layer, j, g - 1)
                        expert_load(layer, j, g)

            for t in range(TT):
                sp_eng.wait_ge(o_step, DEPTH * O_STEPS + t + 1)
                sp_eng.dma_start(out[0, t * P:(t + 1) * P, :], xn[:, t, :]).then_inc(s_out, 16)
            sp_eng.wait_ge(s_out, 16 * TT)

        @block.gpsimd
        def _(pool):
            def load_ada(n):
                if n >= ASLOTS:
                    pool.wait_ge(ada_rows, ROWS * (n - ASLOTS + 1))
                pool.dma_start(aring[:, n % ASLOTS, :, :], ada_source(n)).then_inc(a_landed[n % ASLOTS], 16)

            for n in range(ASLOTS):
                load_ada(n)
            pool.dma_start(bias14[0:6, :], b_ada[0].rearrange("(j n) -> j n", n=D)).then_inc(s_small, 16)
            pool.dma_start(bias14[6:8, :], b_ada_kv.rearrange("(j n) -> j n", n=D)).then_inc(s_small, 16)
            pool.dma_start(bias14[8:14, :], b_ada[1].rearrange("(j n) -> j n", n=D)).then_inc(s_small, 16)
            for vv, g_ap in ((vec(0, SCALE_M), g_attn[0]), (vec(0, SCALE_F), g_ffn[0]), (KV_SCALE, g_kv),
                             (vec(1, SCALE_M), g_attn[1]), (vec(1, SCALE_F), g_ffn[1])):
                pool.dma_start(gains[:, vv, :], g_ap.rearrange("(p k) -> p k", k=KC)).then_inc(s_small, 16)
            for l in range(DEPTH):
                pool.dma_start(w_r[:, l, :, 0:GROUPS], pk(w_rg[l])).then_inc(s_small, 16)
                pool.dma_start(w_r[:, l, :, GROUPS:], pk(w_re[l])).then_inc(s_small, 16)
                pool.dma_start(b_r[:, l, 0:GROUPS], b_rg[l:l + 1, :].broadcast_to([P, GROUPS])).then_inc(s_small, 16)
                pool.dma_start(b_r[:, l, GROUPS:], b_re[l:l + 1, :].broadcast_to([P, EXPERTS])).then_inc(s_small, 16)

            pool.memset(ident[:, :], 0.0).then_inc(s_const, 1)
            pool.memset(ones[:, :], 1.0).then_inc(s_const, 1)
            pool.memset(negones[:, :], -1.0).then_inc(s_const, 1)
            pool.memset(negtri[:, :], -1.0).then_inc(s_const, 1)
            pool.memset(maskA[:, :], 0.0).then_inc(s_const, 1)
            for j in range(GROUPS):
                pool.memset(desc[:, j:j + 1], float(GROUPS - j)).then_inc(s_const, 1)
            pool.iota(distI[:, 0:P], pattern=[[1, P]], base=0, channel_multiplier=-1).then_inc(s_const, 1)
            pool.iota(distI[:, P:], pattern=[[1, T]], base=-P, channel_multiplier=-1).then_inc(s_const, 1)
            pool.wait_ge(s_const, 11)
            pool.affine_select(out=ident[:, :], in_=ident[:, :], compare_op=ALU.not_equal, fill=1.0, base=0,
                               pattern=[[-1, P]], channel_multiplier=1).then_inc(s_const, 1)
            pool.affine_select(out=negtri[:, :], in_=negtri[:, :], compare_op=ALU.is_ge, fill=0.0, base=0,
                               pattern=[[-1, P]], channel_multiplier=1).then_inc(s_const, 1)
            for lo, n in ((0, T), (T, P)):
                pool.affine_select(out=maskA[:, lo:lo + n], in_=maskA[:, lo:lo + n], compare_op=ALU.is_ge, fill=NEG,
                                   base=-1, pattern=[[1, n]], channel_multiplier=-1).then_inc(s_const, 1)
            pool.tensor_copy(distB[:, :], distI[:, :]).then_inc(s_const, 1)
            pool.wait_ge(s_const, 16)
            for lo, n, off in ((0, P, 0), (P, T, P)):
                pool.affine_select(out=distB[:, lo:lo + n], in_=distB[:, lo:lo + n], compare_op=ALU.is_ge, fill=NEG,
                                   base=off, pattern=[[-1, n]], channel_multiplier=1).then_inc(s_const, 1)
            for n in range(ASLOTS, VECS * PARTS):
                load_ada(n)
            pool.wait_ge(o_step, DEPTH * O_STEPS)
            pool.dma_start(gfin[:, :], g_final.rearrange("(o n) -> o n", o=1).broadcast_to([P, D])).then_inc(s_gfin, 16)

        @block.tensor
        def _(pe):
            mm = pe.matmul

            def sum_vector(vv):
                pe.wait_ge(ada_rows, KC * (vv + 1))
                rows = acc[:, vv % 2, :]
                if not is_gate(vv):
                    i = OUT[("sum", vv, 0)]
                    wait_out_free(pe, i)
                    b = out_bank[i % 2]
                    by_chunk = rows.rearrange("p (q k) -> p k q", k=KC)
                    bias_by_chunk = bias14[:, :].rearrange("p (q k) -> p k q", k=KC)
                    for k in range(KC):
                        mm(b[:, k:k + 1], by_chunk[:, k, :], ones[:, 0:1], start=True, stop=False)
                        last = mm(b[:, k:k + 1], bias_by_chunk[:, k, :], ident[0:VECS, vv:vv + 1],
                                  start=False, stop=True)
                    last.then_inc(out_full, 1)
                    return
                for half in range(2):
                    i = OUT[("sum", vv, half)]
                    wait_out_free(pe, i)
                    cols = slice(half * 512, half * 512 + 512)
                    mm(out_bank[i % 2][:, :], ones[:, :], rows[:, cols], start=True, stop=False)
                    mm(out_bank[i % 2][:, :], ident[0:VECS, vv:vv + 1].broadcast_to([VECS, P]), bias14[:, cols],
                       start=False, stop=True).then_inc(out_full, 1)

            def turn(norm):
                by_chunk = xn[:, :, :].rearrange("p t (q k) -> p t k q", k=KC)
                for j in range(4):
                    for a in range(2):
                        for t in range(TT):
                            pe.wait_ge(nrm, 7 * norm + 6 + t)
                            col = a * T + t * P
                            last = pe.transpose(turn_bank[j][:, col:col + P], by_chunk[:, t, 2 * j + a, :], ident[:, :])
                    last.then_inc(turned, 1)

            def feature_unit(item, rhsT):
                i, load = OUT[item], LOAD[item]
                wait_out_free(pe, i)
                wait_weights(pe, load)
                w = w_cols(load % WSLOTS)
                for half in range(2):
                    for k in range(KC):
                        last = mm(out_bank[i % 2][:, half * T:(half + 1) * T], w[:, k, half * P:(half + 1) * P],
                                  rhsT[:, k, :], start=(k == 0), stop=(k == KC - 1))
                last.then_inc(out_full, 1)

            def token_unit(item, lhsT):
                i, load = OUT[item], LOAD[item]
                wait_out_free(pe, i)
                wait_weights(pe, load)
                w = w_cols(load % WSLOTS)
                for t in range(TT):
                    for k in range(KC):
                        last = mm(out_bank[i % 2][:, t * COLS:(t + 1) * COLS], lhsT[:, k, t * P:(t + 1) * P],
                                  w[:, k, :], start=(k == 0), stop=(k == KC - 1))
                last.then_inc(out_full, 1)

            def head_rows(h):
                return slice(HD * (h % 2), HD * (h % 2) + HD), h // 2

            def scores_a(h):
                if h >= 2:
                    pe.wait_ge(zm_ready, h - 1)
                r, c = head_rows(h)
                z = z_bank[h % 2]
                mm(z[:, 0:T], kT[r, c, 0:P], qT[r, c, :], start=True, stop=True)
                mm(z[:, T:CAUSAL], kT[r, c, P:T], qT[r, c, P:T], start=True, stop=True).then_inc(z_full, 1)

            def suffix_a(h):
                pe.wait_ge(sp_ready, h + 1)
                if h >= 2:
                    pe.wait_ge(t_ready, h - 1)
                s, w = s_bank[h % 2], sp[:, h % 2, :]
                mm(s[:, 0:P], negtri[:, :], w[:, 0:P], start=True, stop=True)
                mm(s[:, P:T], negtri[:, :], w[:, P:T], start=True, stop=False)
                mm(s[:, P:T], negones[:, :], w[:, T:CAUSAL], start=False, stop=True)
                mm(s[:, T:CAUSAL], negtri[:, :], w[:, T:CAUSAL], start=True, stop=True).then_inc(s_full, 1)

            def values(h, ready, count, layer):
                pe.wait_ge(ready, count)
                r, c = head_rows(h)
                if h % 2 == 0 and c + layer * PAIRS >= 2:
                    pe.wait_ge(attn_ready, c + layer * PAIRS - 1)
                o, w = av_bank[c % 2], prob[:, h % 2, :]
                vh = v[:, :, h * HD:(h + 1) * HD]
                mm(o[r, 0:P], vh[:, 0, :], w[:, 0:P], start=True, stop=True)
                mm(o[r, P:T], vh[:, 0, :], w[:, P:T], start=True, stop=False)
                mm(o[r, P:T], vh[:, 1, :], w[:, T:CAUSAL], start=False, stop=True).then_inc(av_full, 1)

            def scores_b(h):
                if h >= 2:
                    pe.wait_ge(b_max, 3 * (h - 2) + 1)
                r, c = head_rows(h)
                z = z_bank[h % 2]
                mm(z[:, 0:P], qT[r, c, 0:P], kT[r, c, 0:P], start=True, stop=True)
                mm(z[:, P:CAUSAL], qT[r, c, P:T], kT[r, c, :], start=True, stop=True).then_inc(z_full, 1)

            def turn_b(h):
                pe.wait_ge(b_norm, 3 * h + 3)
                if h >= 2:
                    pe.wait_ge(pT_ready, h - 1)
                s, p = s_bank[h % 2], zm[:, h % 4, :]
                pe.transpose(s[:, 0:P], p[:, 0:P], ident[:, :])
                pe.transpose(s[:, P:T], p[:, P:T], ident[:, :])
                pe.transpose(s[:, T:CAUSAL], p[:, T:CAUSAL], ident[:, :]).then_inc(s_full, 1)

            def router(layer):
                i = OUT[("route", layer)]
                wait_out_free(pe, i)
                for t in range(TT):
                    for k in range(KC):
                        last = mm(out_bank[i % 2][:, t * 32:t * 32 + GROUPS + EXPERTS], hT[:, k, t * P:(t + 1) * P],
                                  w_r[:, layer, k, :], start=(k == 0), stop=(k == KC - 1))
                last.then_inc(out_full, 1)

            def gate_up(layer, j, g):
                e = layer * EXPERTS + j
                pe.wait_ge(gu_free, g * PER_GROUP + e + 1)
                for n, kind in enumerate(("gate", "up")):
                    load = MOE_BASE[layer] + GROUP_LOADS.index((kind, j))
                    wait_weights(pe, load, g)
                    w = w_cols(load % WSLOTS)
                    b = gu_bank[j % 2][n]
                    for f in range(FC):
                        for k in range(KC):
                            last = mm(b[:, f * T:(f + 1) * T], w[:, k, f * P:(f + 1) * P], hT[:, k, :],
                                      start=(k == 0), stop=(k == KC - 1))
                    last.then_inc(gu_full, 1)

            def down(layer, j, g):
                e = layer * EXPERTS + j
                load = MOE_BASE[layer] + GROUP_LOADS.index(("down", j))
                wait_weights(pe, load, g)
                pe.wait_ge(gu_free, g * PER_GROUP + e + 3)
                w = w_rows(load % WSLOTS)
                hT_e = hid[:, j % 2, :].rearrange("p (f t) -> p f t", f=FC)
                for q in range(4):
                    t, half = divmod(q, 2)
                    pe.wait_ge(y_free, g * 4 * PER_GROUP + 4 * e + q + 1)
                    for f in range(FC):
                        last = mm(y_bank[q][:, :], hT_e[:, f, t * P:(t + 1) * P], w[:, f, half * 512:half * 512 + 512],
                                  start=(f == 0), stop=(f == FC - 1))
                    last.then_inc(y_full, 1)

            def experts(layer):
                with pe.Fori(0, GROUPS) as g:
                    gate_up(layer, 0, g)
                    for j in range(PER_GROUP):
                        if j + 1 < PER_GROUP:
                            gate_up(layer, j + 1, g)
                        down(layer, j, g)

            def wait_hT(norm):
                pe.wait_ge(hT_dve, HT_COUNT[norm])
                pe.wait_ge(hT_act, HT_COUNT[norm])

            pe.wait_ge(s_const, CONSTS)
            pe.wait_ge(s_small, SMALL)
            sum_vector(0)
            sum_vector(1)
            turn(0)
            wait_hT(0)
            for u in range(12):
                if u < 2 * UNITS:
                    feature_unit(("qkv", u), hT)
                else:
                    token_unit(("qkv", u), hT)
                if u in SUM_AFTER_QKV0:
                    sum_vector(SUM_AFTER_QKV0[u])
            pe.wait_ge(qkv_ready, 12)
            for i in range(HEADS + 3):
                if i < HEADS:
                    scores_a(i)
                if 1 <= i <= HEADS:
                    suffix_a(i - 1)
                if i in SUM_AFTER_HEAD0:
                    sum_vector(SUM_AFTER_HEAD0[i])
                if i >= 3:
                    values(i - 3, w_ready, i - 2, 0)
            sum_vector(8)
            pe.wait_ge(attn_ready, PAIRS)
            for u in range(UNITS):
                token_unit(("o0", u), attnT)
            sum_vector(9)
            turn(1)
            wait_hT(1)
            router(0)
            for n in (OUT[("route", 0)], OUT[("route", 0)] - 1):
                wait_out_read(pe, n)
            experts(0)

            turn(2)
            wait_hT(2)
            for u in range(12):
                if u < UNITS:
                    feature_unit(("kvq", u), hkvT)
                elif u < 2 * UNITS:
                    token_unit(("kvq", u), hkvT)
                else:
                    feature_unit(("kvq", u), hT)
                if u in SUM_AFTER_KVQ1:
                    sum_vector(SUM_AFTER_KVQ1[u])
            pe.wait_ge(qkv_ready, 24)
            for i in range(HEADS + 3):
                if i < HEADS:
                    scores_b(i)
                if 2 <= i < HEADS + 2:
                    turn_b(i - 2)
                if i in SUM_AFTER_HEAD1:
                    sum_vector(SUM_AFTER_HEAD1[i])
                if i >= 3:
                    values(i - 3, pT_ready, i - 2, 1)
            pe.wait_ge(attn_ready, 2 * PAIRS)
            for u in range(UNITS):
                token_unit(("o1", u), attnT)
            turn(3)
            wait_hT(3)
            router(1)
            for n in (OUT[("route", 1)], OUT[("route", 1)] - 1):
                wait_out_read(pe, n)
            experts(1)

        @block.scalar
        def _(act):
            steps = [0]

            def own(ins):
                ins.then_inc(act_step, 1)
                steps[0] += 1
                act.wait_ge(act_step, steps[0])

            def squares(norm):
                for t in range(TT):
                    if norm == 0:
                        act.wait_ge(s_x, 16 * TT)
                    elif norm in (1, 3):
                        act.wait_ge(o_step, O_STEPS * (norm // 2 + 1))
                    else:
                        act.wait_ge(y_sum, Y_GROUP * GROUPS * (norm // 2))
                    act.activation(xn[:, t, :], x[:, t, :], ACT.Square, accum_out=ss[:, t:t + 1]).then_inc(ss_ready, 1)

            def rsqrt(norm):
                act.wait_ge(nrm, 7 * norm + 1)
                act.activation(rtmp[:, 0, :], ms[:, :], ACT.Ln).then_inc(rsqrt_ready, 1)
                act.wait_ge(rsqrt_ready, 2 * norm + 1)
                act.activation(rtmp[:, 0, :], rtmp[:, 0, :], ACT.Exp, scale=-0.5).then_inc(rsqrt_ready, 1)

            def modulate(norm):
                act.wait_ge(vec_ready, 1 + max(VEC_ORDER.index(a) for _, sh, a in modulated(norm)))
                for j in (1, 3):
                    act.wait_ge(turned, 4 * norm + j + 1)
                    for dst, sh, a in modulated(norm):
                        for n in range(2):
                            k = 2 * j + n
                            act.activation(dst[:, k, :], turn_bank[j][:, n * T:(n + 1) * T], ACT.Identity,
                                           bias=shift[:, sh, k:k + 1], scale=shift[:, a, k:k + 1]).then_inc(hT_act, 1)

            def take(item, dst):
                i = OUT[item]
                act.wait_ge(out_full, i + 1)
                act.activation(dst, out_bank[i % 2][:, :].rearrange("p (a n) -> p a n", a=2), ACT.Copy)\
                   .then_inc(qkv_ready, 1)

            def gate(vv, dst):
                for half in range(2):
                    i = OUT[("sum", vv, half)]
                    act.wait_ge(out_full, i + 1)
                    act.activation(dst[:, half * 512:half * 512 + 512], out_bank[i % 2][:, :], ACT.Copy, bias=1.0)\
                       .then_inc(gate_ready, 1)

            def attn_out(c, layer):
                act.wait_ge(av_full, 2 * (c + 1) + layer * HEADS)
                act.activation(attnT[:, c, :], av_bank[c % 2][:, 0:T], ACT.Copy).then_inc(attn_ready, 1)

            def soft_a(h):
                act.wait_ge(zm_ready, h + 1)
                if h >= 2:
                    act.wait_ge(sp_ready, h - 1)
                s = soft[:, h % 2, :]
                own(act.activation(s, zm[:, h % 4, :], ACT.Abs))
                own(act.activation(s, s, ACT.Exp, scale=-1.0))
                act.activation(s, s, ACT.Ln, bias=1.0).then_inc(soft_ready, 1)

            def weights_a(h):
                act.wait_ge(t_ready, h + 1)
                if h >= 2:
                    act.wait_ge(av_full, h - 1)
                act.activation(prob[:, h % 2, :], zm[:, h % 4, :], ACT.Exp).then_inc(w_ready, 1)

            def exps_b(h):
                act.wait_ge(b_max, 3 * h + 3)
                for t, cols in ((0, slice(0, P)), (1, slice(P, CAUSAL))):
                    act.activation(zm[:, h % 4, cols], zm[:, h % 4, cols], ACT.Exp, scale=SCALE,
                                   bias=nmx[:, h % 2, t:t + 1], accum_out=den[:, h % 2, t:t + 1]).then_inc(p_ready, 1)

            def probs_b(h):
                act.wait_ge(s_full, HEADS + h + 1)
                if h >= 2:
                    act.wait_ge(av_full, HEADS + h - 1)
                act.activation(prob[:, h % 2, :], s_bank[h % 2][:, 0:CAUSAL], ACT.Copy).then_inc(pT_ready, 1)

            def router(layer):
                act.wait_ge(route, R_STEPS * layer + R_EXP1)
                act.activation(rt[:, 4, :, :], rt[:, 4, :, :], ACT.Exp).then_inc(route_exp, 1)
                act.wait_ge(route, R_STEPS * layer + R_EXP2)
                act.activation(r1[:, 6, :], r1[:, 6, :], ACT.Exp).then_inc(route_exp, 1)

            def experts(layer):
                with act.Fori(0, GROUPS) as g:
                    for j in range(PER_GROUP):
                        e = layer * EXPERTS + j
                        act.wait_ge(gu_full, g * 2 * PER_GROUP + 2 * e + 1)
                        act.wait_ge(gu_free, g * PER_GROUP + e + 1)
                        act.activation(sg[:, j % 2, :], gu_bank[j % 2][0][:, :], ACT.Silu).then_inc(silu_done, 1)

            squares(0)
            rsqrt(0)
            modulate(0)
            for u in range(12):
                if u < 2 * UNITS:
                    dst = qT if u < UNITS else kT
                    take(("qkv", u), dst[:, 2 * (u % UNITS):2 * (u % UNITS) + 2, :])
                else:
                    take(("qkv", u), v[:, :, (u - 2 * UNITS) * COLS:(u - 2 * UNITS + 1) * COLS])
                if SUM_AFTER_QKV0.get(u) == vec(0, GATE_M):
                    gate(vec(0, GATE_M), gate_m)
            for i in range(HEADS + 4):
                if i < HEADS:
                    soft_a(i)
                if 2 <= i < HEADS + 2:
                    weights_a(i - 2)
                if SUM_AFTER_HEAD0.get(i) == vec(0, GATE_F):
                    gate(vec(0, GATE_F), gate_f)
                if i >= 4 and i % 2:
                    attn_out((i - 4) // 2, 0)
            squares(1)
            rsqrt(1)
            modulate(1)
            router(0)
            experts(0)

            squares(2)
            rsqrt(2)
            modulate(2)
            for u in range(12):
                if u < UNITS:
                    take(("kvq", u), kT[:, 2 * u:2 * u + 2, :])
                elif u < 2 * UNITS:
                    take(("kvq", u), v[:, :, (u - UNITS) * COLS:(u - UNITS + 1) * COLS])
                else:
                    take(("kvq", u), qT[:, 2 * (u - 2 * UNITS):2 * (u - 2 * UNITS) + 2, :])
                if SUM_AFTER_KVQ1.get(u) == vec(1, GATE_M):
                    gate(vec(1, GATE_M), gate_m)
            for i in range(HEADS + 4):
                if i < HEADS:
                    exps_b(i)
                if 2 <= i < HEADS + 2:
                    probs_b(i - 2)
                if SUM_AFTER_HEAD1.get(i) == vec(1, GATE_F):
                    gate(vec(1, GATE_F), gate_f)
                if i >= 4 and i % 2:
                    attn_out((i - 4) // 2, 1)
            squares(3)
            rsqrt(3)
            modulate(3)
            router(1)
            experts(1)
            squares(4)
            rsqrt(4)

        @block.vector
        def _(dve):
            counts = {}

            def step(semaphore, ins):
                ins.then_inc(semaphore, 1)
                counts[semaphore.name] = counts.get(semaphore.name, 0) + 1

            def settled(semaphore):
                dve.wait_ge(semaphore, counts[semaphore.name])

            def add_rows(n):
                vv, part = n // PARTS, n % PARTS
                dve.wait_ge(a_landed[n % ASLOTS], 16 * (n // ASLOTS + 1))
                if n == 0:
                    dve.wait_ge(s_c, 16)
                if part == 0 and vv >= 2:
                    dve.wait_ge(out_full, OUT[sum_items(vv - 2)[-1]] + 1)
                for r in range(ROWS):
                    k = part * ROWS + r
                    w = aring[:, n % ASLOTS, r, :]
                    a = acc[:, vv % 2, :]
                    if k == 0:
                        step(ada_rows, dve.tensor_scalar(a, w, cT[:, k:k + 1], None, ALU.mult))
                    else:
                        settled(ada_rows)
                        step(ada_rows, dve.scalar_tensor_tensor(out=a, in0=w, scalar=cT[:, k:k + 1], in1=a,
                                                                op0=ALU.mult, op1=ALU.add))

            def column(vv):
                i = OUT[("sum", vv, 0)]
                dve.wait_ge(out_full, i + 1)
                if is_scale(vv):
                    ins = dve.scalar_tensor_tensor(out=shift[:, vv, :], in0=out_bank[i % 2][:, 0:KC], scalar=1.0,
                                                   in1=gains[:, vv, :], op0=ALU.add, op1=ALU.mult)
                else:
                    ins = dve.tensor_copy(shift[:, vv, :], out_bank[i % 2][:, 0:KC])
                step(vec_ready, ins)

            def normalise(norm, last=False):
                dve.wait_ge(ss_ready, TT * (norm + 1))
                step(nrm, dve.tensor_scalar(ms[:, :], ss[:, :], 1.0 / D, EPS, ALU.mult, ALU.add))
                dve.wait_ge(rsqrt_ready, 2 * norm + 2)
                settled(nrm)
                step(nrm, dve.tensor_tensor(rtmp[:, 1, :], rtmp[:, 0, :], rtmp[:, 0, :], ALU.mult))
                settled(nrm)
                step(nrm, dve.tensor_tensor(rtmp[:, 2, :], rtmp[:, 1, :], ms[:, :], ALU.mult))
                settled(nrm)
                step(nrm, dve.tensor_scalar(rtmp[:, 3, :], rtmp[:, 2, :], -0.5, 1.5, ALU.mult, ALU.add))
                settled(nrm)
                step(nrm, dve.tensor_tensor(rstd[:, :], rtmp[:, 3, :], rtmp[:, 0, :], ALU.mult))
                settled(nrm)
                for t in range(TT):
                    if last:
                        step(o_step, dve.scalar_tensor_tensor(out=xn[:, t, :], in0=x[:, t, :], scalar=rstd[:, t:t + 1],
                                                              in1=gfin[:, :], op0=ALU.mult, op1=ALU.mult))
                    else:
                        step(nrm, dve.tensor_scalar(xn[:, t, :], x[:, t, :], rstd[:, t:t + 1], None, ALU.mult))

            def modulate(norm):
                settled(vec_ready)
                for j in (0, 2):
                    dve.wait_ge(turned, 4 * norm + j + 1)
                    for dst, sh, a in modulated(norm):
                        for n in range(2):
                            k = 2 * j + n
                            dve.tensor_scalar(dst[:, k, :], turn_bank[j][:, n * T:(n + 1) * T], shift[:, a, k:k + 1],
                                              shift[:, sh, k:k + 1], ALU.mult, ALU.add).then_inc(hT_dve, 1)

            def mask_a(h):
                dve.wait_ge(z_full, h + 1)
                if h >= 4:
                    dve.wait_ge(w_ready, h - 3)
                dve.scalar_tensor_tensor(out=zm[:, h % 4, :], in0=z_bank[h % 2][:, 0:CAUSAL], scalar=SCALE,
                                         in1=maskA[:, :], op0=ALU.mult, op1=ALU.add).then_inc(zm_ready, 1)

            def softplus_a(h):
                dve.wait_ge(soft_ready, h + 1)
                dve.wait_ge(zm_ready, h + 1)
                if h >= 2:
                    dve.wait_ge(s_full, h - 1)
                dve.scalar_tensor_tensor(out=sp[:, h % 2, :], in0=zm[:, h % 4, :], scalar=0.0, in1=soft[:, h % 2, :],
                                         op0=ALU.max, op1=ALU.add).then_inc(sp_ready, 1)

            def exponent_a(h):
                dve.wait_ge(s_full, h + 1)
                dve.wait_ge(sp_ready, h + 1)
                dve.tensor_tensor(zm[:, h % 4, :], s_bank[h % 2][:, 0:CAUSAL], zm[:, h % 4, :], ALU.add)\
                   .then_inc(t_ready, 1)

            def bias_max_b(h):
                dve.wait_ge(z_full, HEADS + h + 1)
                if h >= 4:
                    dve.wait_ge(s_full, HEADS + h - 3)
                slope = 2.0 ** (-8.0 * (h + 1) / HEADS)
                z = zm[:, h % 4, :]
                step(b_max, dve.scalar_tensor_tensor(out=z, in0=distB[:, :], scalar=slope / SCALE,
                                                     in1=z_bank[h % 2][:, 0:CAUSAL], op0=ALU.mult, op1=ALU.add))
                settled(b_max)
                if h >= 2:
                    dve.wait_ge(p_ready, 2 * (h - 1))
                dve.tensor_reduce(mx[:, h % 2, 0:1], z[:, 0:P], AX_X, ALU.max)
                step(b_max, dve.tensor_reduce(mx[:, h % 2, 1:2], z[:, P:CAUSAL], AX_X, ALU.max))
                settled(b_max)
                step(b_max, dve.tensor_scalar(nmx[:, h % 2, :], mx[:, h % 2, :], -SCALE, None, ALU.mult))

            def norm_b(h):
                dve.wait_ge(p_ready, 2 * (h + 1))
                step(b_norm, dve.reciprocal(rden[:, h % 2, :], den[:, h % 2, :]))
                settled(b_norm)
                for t, cols in ((0, slice(0, P)), (1, slice(P, CAUSAL))):
                    step(b_norm, dve.tensor_scalar(zm[:, h % 4, cols], zm[:, h % 4, cols], rden[:, h % 2, t:t + 1],
                                                   None, ALU.mult))

            def residual(item):
                i, u = OUT[item], item[1]
                cols = slice(u * COLS, (u + 1) * COLS)
                dve.wait_ge(out_full, i + 1)
                tmp = otmp[:, u % 2, :, :]
                step(o_step, dve.tensor_tensor(tmp, out_bank[i % 2][:, :].rearrange("p (t n) -> p t n", t=TT),
                                               gate_m[:, cols].unsqueeze(1).broadcast_to([P, TT, COLS]), ALU.mult))
                settled(o_step)
                step(o_step, dve.tensor_tensor(x[:, :, cols], x[:, :, cols], tmp, ALU.add))

            def first_max(src, peak, hit, score, best, dst):
                r(dve.tensor_reduce(peak, src, AX_X, ALU.max))
                r(dve.tensor_tensor(hit, src, peak.unsqueeze(2).broadcast_to([P, TT, 4]), ALU.is_equal))
                r(dve.tensor_tensor(score, hit, desc[:, :].unsqueeze(1).broadcast_to([P, TT, 4]), ALU.mult))
                r(dve.tensor_reduce(best, score, AX_X, ALU.max))
                r(dve.tensor_tensor(dst, score, best.unsqueeze(2).broadcast_to([P, TT, 4]), ALU.is_equal))

            def r(ins):
                step(route, ins)
                settled(route)

            def wide(row):
                return row.unsqueeze(2).broadcast_to([P, TT, 4])

            def router(layer):
                start = counts.get(route.name, 0)
                i = OUT[("route", layer)]
                dve.wait_ge(out_full, i + 1)
                n = GROUPS + EXPERTS
                r(dve.tensor_tensor(lg[:, :, :], out_bank[i % 2][:, 0:64].rearrange("p (t n) -> p t n", t=TT)[:, :, 0:n],
                                    b_r[:, layer, :].unsqueeze(1).broadcast_to([P, TT, n]), ALU.add))
                groups = lg[:, :, 0:GROUPS]
                in_group = rt[:, 0, :, :]
                first_max(groups, r1[:, 0, :], rt[:, 1, :, :], rt[:, 2, :, :], r1[:, 1, :], in_group)
                r(dve.tensor_tensor(rt[:, 4, :, :], groups, wide(r1[:, 0, :]), ALU.subtract))
                assert counts[route.name] - start == R_EXP1
                r(dve.tensor_tensor(le_sel[:, :, :].rearrange("p t (g j) -> p t g j", g=GROUPS),
                                    lg[:, :, GROUPS:].rearrange("p t (g j) -> p t g j", g=GROUPS),
                                    in_group.unsqueeze(3).broadcast_to([P, TT, GROUPS, PER_GROUP]), ALU.mult))
                le, first, rest, second = rt[:, 5, :, :], rt[:, 6, :, :], rt[:, 7, :, :], rt[:, 8, :, :]
                r(dve.tensor_reduce(le, le_sel[:, :, :].rearrange("p t (g j) -> p t j g", g=GROUPS), AX_X, ALU.add))
                first_max(le, r1[:, 2, :], rt[:, 9, :, :], rt[:, 10, :, :], r1[:, 3, :], first)
                r(dve.scalar_tensor_tensor(out=rest, in0=first, scalar=-3.0e38, in1=le, op0=ALU.mult, op1=ALU.add))
                first_max(rest, r1[:, 4, :], rt[:, 9, :, :], rt[:, 10, :, :], r1[:, 5, :], second)
                r(dve.tensor_tensor(r1[:, 6, :], r1[:, 4, :], r1[:, 2, :], ALU.subtract))
                assert counts[route.name] - start == R_EXP2
                dve.wait_ge(route_exp, 2 * layer + 1)
                r(dve.tensor_reduce(r1[:, 7, :], rt[:, 4, :, :], AX_X, ALU.add))
                r(dve.reciprocal(r1[:, 8, :], r1[:, 7, :]))
                dve.wait_ge(route_exp, 2 * layer + 2)
                r(dve.tensor_scalar(r1[:, 9, :], r1[:, 6, :], 1.0, None, ALU.add))
                r(dve.reciprocal(r1[:, 10, :], r1[:, 9, :]))
                r(dve.tensor_tensor(r1[:, 11, :], r1[:, 10, :], r1[:, 8, :], ALU.mult))
                r(dve.tensor_tensor(r1[:, 0, :], r1[:, 6, :], r1[:, 11, :], ALU.mult))
                r(dve.tensor_tensor(rt[:, 9, :, :], first, wide(r1[:, 11, :]), ALU.mult))
                r(dve.tensor_tensor(rt[:, 10, :, :], second, wide(r1[:, 0, :]), ALU.mult))
                r(dve.tensor_tensor(rt[:, 11, :, :], rt[:, 9, :, :], rt[:, 10, :, :], ALU.add))
                r(dve.tensor_tensor(comb[:, :, :].rearrange("p t (g j) -> p t g j", g=GROUPS),
                                    in_group.unsqueeze(3).broadcast_to([P, TT, GROUPS, PER_GROUP]),
                                    rt[:, 11, :, :].unsqueeze(2).broadcast_to([P, TT, GROUPS, PER_GROUP]), ALU.mult))
                assert counts[route.name] - start == R_STEPS

            def experts(layer):
                with dve.Fori(0, GROUPS) as g:
                    y_base = layer * Y_GROUP * GROUPS

                    def hidden(j):
                        e = layer * EXPERTS + j
                        dve.wait_ge(silu_done, g * PER_GROUP + e + 1)
                        dve.wait_ge(gu_full, g * 2 * PER_GROUP + 2 * e + 2)
                        dve.tensor_tensor(hid[:, j % 2, :], sg[:, j % 2, :], gu_bank[j % 2][1][:, :], ALU.mult)\
                           .then_inc(gu_free, 1)

                    def add_output(j):
                        e = layer * EXPERTS + j
                        for q in range(4):
                            t, half = divmod(q, 2)
                            cols = slice(half * 512, half * 512 + 512)
                            dve.wait_ge(y_full, g * 4 * PER_GROUP + 4 * e + q + 1)
                            dve.wait_ge(y_sum, g * Y_GROUP + y_base + (1 if j == 0 else 4 * j + q - 2))
                            dve.scalar_tensor_tensor(out=ytmp[:, q, :], in0=y_bank[q][:, :],
                                                     scalar=comb_g[:, t, j:j + 1], in1=gate_f[:, cols],
                                                     op0=ALU.mult, op1=ALU.mult).then_inc(y_free, 1)
                            dve.wait_ge(y_free, g * 4 * PER_GROUP + 4 * e + q + 5)
                            dve.tensor_tensor(x[:, t, cols], x[:, t, cols], ytmp[:, q, :], ALU.add).then_inc(y_sum, 1)

                    dve.tensor_copy(comb_g[:, :, :], comb[:, :, bass.ds(g * PER_GROUP, PER_GROUP)]).then_inc(y_sum, 1)
                    hidden(0)
                    for j in range(PER_GROUP):
                        if j + 1 < PER_GROUP:
                            hidden(j + 1)
                        add_output(j)

            dve.sem_inc(gu_free, 2)
            dve.sem_inc(y_free, 4)
            dve.wait_ge(s_small, SMALL)
            dve.wait_ge(s_const, CONSTS)
            for n in range(PARTS):
                add_rows(n)
            normalise(0)
            for n in range(PARTS, 2 * PARTS):
                add_rows(n)
            column(0)
            column(1)
            modulate(0)
            for u in range(12):
                add_rows(2 * PARTS + u)
                if u in SUM_AFTER_QKV0 and not is_gate(SUM_AFTER_QKV0[u]):
                    column(SUM_AFTER_QKV0[u])
            for i in range(HEADS + 2):
                if i < HEADS:
                    mask_a(i)
                if 1 <= i <= HEADS:
                    softplus_a(i - 1)
                if i >= 2:
                    exponent_a(i - 2)
                if i < HEADS:
                    add_rows(20 + i)
                if i in SUM_AFTER_HEAD0 and not is_gate(SUM_AFTER_HEAD0[i]):
                    column(SUM_AFTER_HEAD0[i])
            column(8)
            dve.wait_ge(gate_ready, 2)
            for u in range(UNITS):
                residual(("o0", u))
                add_rows(36 + u)
            column(9)
            normalise(1)
            modulate(1)
            router(0)
            dve.wait_ge(gate_ready, 4)
            experts(0)

            normalise(2)
            modulate(2)
            for u in range(12):
                add_rows(40 + u)
                if u in SUM_AFTER_KVQ1 and not is_gate(SUM_AFTER_KVQ1[u]):
                    column(SUM_AFTER_KVQ1[u])
            for i in range(HEADS + 1):
                if i < HEADS:
                    bias_max_b(i)
                if i >= 1:
                    norm_b(i - 1)
                if i in (0, 3, 6, 9):
                    add_rows(52 + i // 3)
                if i in SUM_AFTER_HEAD1 and not is_gate(SUM_AFTER_HEAD1[i]):
                    column(SUM_AFTER_HEAD1[i])
            dve.wait_ge(gate_ready, 6)
            for u in range(UNITS):
                residual(("o1", u))
            normalise(3)
            modulate(3)
            router(1)
            dve.wait_ge(gate_ready, 8)
            experts(1)
            dve.wait_ge(s_gfin, 16)
            normalise(4, last=True)


_INS = ["x", "c", "w_ada", "b_ada", "g_attn", "g_ffn", "w_qkv_a", "w_o_a", "w_ada_kv", "b_ada_kv", "g_kv", "w_kv",
        "w_q_b", "w_o_b", "w_rg", "b_rg", "w_re", "b_re", "w_gate", "w_up", "w_down", "g_final"]


def kernel(**inputs):
    import numpy as np
    import concourse.bacc as bacc
    from concourse.bass_utils import run_bass_kernel_spmd

    nc = bacc.Bacc("TRN2", target_bir_lowering=False, num_devices=1)
    arrays, args = {}, []
    for name in _INS:
        a = np.ascontiguousarray(inputs[name])
        arrays[f"in_{name}"] = a
        args.append(nc.dram_tensor(f"in_{name}", a.shape, mybir.dt.from_np(a.dtype), kind="ExternalInput").ap())
    out = nc.dram_tensor("out_y", (1, T, D), F32, kind="ExternalOutput").ap()
    program(nc, *args, out)
    result = run_bass_kernel_spmd(nc, [arrays], core_ids=[0])
    return result.results[0]["out_y"]
```

```python
from contextlib import ExitStack

import concourse.bass as bass
from concourse import mybir

F32 = mybir.dt.float32
I32 = mybir.dt.int32
ALU = mybir.AluOpType
ACT = mybir.ActivationFunctionType
AX_X = mybir.AxisListType.X

P = 128
D = 1024
T = 256
TT = T // P
KC = D // P
HEADS = 16
HD = D // HEADS
PAIRS = HEADS // 2
GROUPS = 4
PER_GROUP = 4
EXPERTS = GROUPS * PER_GROUP
FF = 256
FC = FF // P
EPS = 1e-6
SCALE = HD ** -0.5
NEG = -1.0e30
CAUSAL = T + P
COLS = 256
UNITS = D // COLS
WSLOTS = 12
ASLOTS = 3
VECS = 14
PARTS = 4
ROWS = KC // PARTS
DEPTH = 2
CAP = 96

SHIFT_M, SCALE_M, GATE_M, SHIFT_F, SCALE_F, GATE_F = range(6)
KV_SHIFT, KV_SCALE = 6, 7


def vec(layer, which):
    return which if layer == 0 else 8 + which


def is_gate(v):
    return v in (vec(0, GATE_M), vec(0, GATE_F), vec(1, GATE_M), vec(1, GATE_F))


def is_scale(v):
    return v in (vec(0, SCALE_M), vec(0, SCALE_F), KV_SCALE, vec(1, SCALE_M), vec(1, SCALE_F))


GROUP_LOADS = [("gate", 0), ("up", 0), ("gate", 1), ("up", 1), ("down", 0), ("gate", 2), ("up", 2), ("down", 1),
               ("gate", 3), ("up", 3), ("down", 2), ("down", 3)]
assert len(GROUP_LOADS) == WSLOTS

QKV0 = [("qkv", u) for u in range(12)]
O0 = [("o0", u) for u in range(4)]
KVQ1 = [("kvq", u) for u in range(12)]
O1 = [("o1", u) for u in range(4)]


def sum_items(v):
    return [("sum", v, 0), ("sum", v, 1)] if is_gate(v) else [("sum", v, 0)]


SUM_AFTER_QKV0 = {6: 2, 10: 3}
SUM_AFTER_HEAD0 = {0: 4, 5: 5, 9: 6, 13: 7}
SUM_AFTER_KVQ1 = {6: 10, 10: 11}
SUM_AFTER_HEAD1 = {0: 12, 12: 13}


def out_items():
    items = sum_items(0) + sum_items(1)
    for u, item in enumerate(QKV0):
        items.append(item)
        if u in SUM_AFTER_QKV0:
            items += sum_items(SUM_AFTER_QKV0[u])
    for h in range(HEADS):
        if h in SUM_AFTER_HEAD0:
            items += sum_items(SUM_AFTER_HEAD0[h])
    items += sum_items(8)
    items += O0
    items += sum_items(9)
    items += [("route", 0), ("rank", 0)]
    for u, item in enumerate(KVQ1):
        items.append(item)
        if u in SUM_AFTER_KVQ1:
            items += sum_items(SUM_AFTER_KVQ1[u])
    for h in range(HEADS):
        if h in SUM_AFTER_HEAD1:
            items += sum_items(SUM_AFTER_HEAD1[h])
    items += O1
    items += [("route", 1), ("rank", 1)]
    return items


ITEMS = out_items()
OUT = {item: i for i, item in enumerate(ITEMS)}
VEC_ORDER = [vv for vv in range(VECS) if not is_gate(vv)]
GATE_ORDER = [vv for vv in range(VECS) if is_gate(vv)]
R_GROUP, R_EXP1, R_RANK, R_EXP2, R_STEPS = 6, 7, 10, 24, 34
F_STEPS = 3
Y_GROUP = 1 + 4 * PER_GROUP
O_STEPS = 2 * UNITS
assert sorted(v for k in OUT if k[0] == "sum" for v in [k[1]] if k[2] == 0) == list(range(VECS))

FIXED_LOADS = {0: QKV0 + O0, 1: KVQ1 + O1}
MOE_LOADS = GROUPS * WSLOTS
LOAD_BASE = {0: 0, 1: len(QKV0 + O0) + MOE_LOADS}
MOE_BASE = {l: LOAD_BASE[l] + len(FIXED_LOADS[l]) for l in range(DEPTH)}
LOAD = {}
for _l in range(DEPTH):
    for _i, _item in enumerate(FIXED_LOADS[_l]):
        LOAD[_item] = LOAD_BASE[_l] + _i


def program(nc, x_in, c_in, w_ada, b_ada, g_attn, g_ffn, w_qkv_a, w_o_a, w_ada_kv, b_ada_kv, g_kv, w_kv,
            w_q_b, w_o_b, w_rg, b_rg, w_re, b_re, w_gate, w_up, w_down, g_final, out):
    ctx = ExitStack()
    with ctx:
        def sb(name, shape, dt=F32):
            return ctx.enter_context(nc.sbuf_tensor(name, shape, dt))

        def sem(name):
            return ctx.enter_context(nc.semaphore(name))

        bank = [ctx.enter_context(nc.psum_tensor(f"bank{i}", [P, 512], F32)) for i in range(8)]
        out_bank = bank[0:2]
        av_bank = bank[2:4]
        z_bank = bank[4:6]
        s_bank = bank[6:8]
        turn_bank = bank[4:8]
        gu_bank = [bank[0:2], bank[6:8]]
        y_bank = bank[2:6]
        few_bank = bank[4:6]
        comb_bank = bank[0]
        place_bank = bank[1]
        few_y_bank = bank[2:4]
        back_bank = [bank[6], bank[7], bank[2], bank[3]]

        wring = sb("wring", [P, WSLOTS, 2048])
        aring = sb("aring", [P, ASLOTS, ROWS, D])
        x = sb("x", [P, TT, D])
        xn = sb("xn", [P, TT, D])
        hT = sb("hT", [P, KC, T])
        qT = sb("qT", [P, PAIRS, T])
        kT = sb("kT", [P, PAIRS, T])
        v = sb("v", [P, TT, D])
        attnT = sb("attnT", [P, PAIRS, T])
        hkvT = attnT
        cT = sb("cT", [P, KC])
        acc = sb("acc", [P, 2, D])
        bias14 = sb("bias14", [VECS, D])
        shift = sb("shift", [P, VECS, KC])
        gains = sb("gains", [P, VECS, KC])
        gate_m = sb("gate_m", [P, D])
        gate_f = sb("gate_f", [P, D])
        gfin = gate_m
        ident = sb("ident", [P, P])
        one = sb("one", [P, 1])
        negone = sb("negone", [P, 1])
        ones = one[:, :].broadcast_to([P, P])
        negones = negone[:, :].broadcast_to([P, P])
        negtri = sb("negtri", [P, P])
        maskA = sb("maskA", [P, CAUSAL])
        distB = sb("distB", [P, CAUSAL])
        distI = kT[:, 0:2, :].rearrange("p a t -> p (a t)")[:, 0:CAUSAL].bitcast(I32)
        desc = sb("desc", [P, GROUPS])
        before = sb("before", [P, P])
        places = sb("places", [P, CAP])
        placesI = qT[:, 0, 0:CAP].bitcast(I32)
        zm = hT[:, :, :].rearrange("p k t -> p (k t)")[:, 0:4 * CAUSAL].rearrange("p (i n) -> p i n", i=4)
        xn_flat = xn[:, :, :].rearrange("p t n -> p (t n)")
        soft = xn_flat[:, 0:2 * CAUSAL].rearrange("p (i n) -> p i n", i=2)
        sp = xn_flat[:, D:D + 2 * CAUSAL].rearrange("p (i n) -> p i n", i=2)
        prob = sb("prob", [P, 2, CAUSAL])
        mx = sb("mx", [P, 2, TT])
        nmx = sb("nmx", [P, 2, TT])
        den = sb("den", [P, 2, TT])
        rden = sb("rden", [P, 2, TT])
        ss = sb("ss", [P, TT])
        ms = sb("ms", [P, TT])
        rstd = sb("rstd", [P, TT])
        rtmp = sb("rtmp", [P, 4, TT])
        otmp = v[:, :, :].rearrange("p t n -> p (t n)")[:, 0:4 * COLS].rearrange("p (i t n) -> p i t n", i=2, t=TT)
        w_r = sb("w_r", [P, DEPTH, KC, GROUPS + EXPERTS])
        b_r = sb("b_r", [P, DEPTH, GROUPS + EXPERTS])
        lg = sb("lg", [P, TT, GROUPS + EXPERTS])
        rt = sb("rt", [P, 12, TT, 4])
        r1 = sb("r1", [P, 12, TT])
        le_sel = sb("le_sel", [P, TT, EXPERTS])
        comb = sb("comb", [P, TT, EXPERTS])
        comb_g = sb("comb_g", [P, TT, PER_GROUP])
        where = sb("where", [P, 2, TT, GROUPS + 1])
        where_g = sb("where_g", [P, 2, TT])
        largest = sb("largest", [P, 2])
        largestI = sb("largestI", [P, 2], I32)
        q_flat = qT[:, :, :].rearrange("p c t -> p (c t)")
        sg = q_flat[:, 0:2 * FC * T].rearrange("p (i n) -> p i n", i=2)
        hid = q_flat[:, 2 * FC * T:4 * FC * T].rearrange("p (i n) -> p i n", i=2)
        ytmp = kT[:, :, :].rearrange("p c t -> p (c t)").rearrange("p (q n) -> p q n", q=4)
        few_sg = q_flat[:, 0:2 * FC * CAP].rearrange("p (i n) -> p i n", i=2)
        few_uc = q_flat[:, 512:512 + 2 * FC * CAP].rearrange("p (i n) -> p i n", i=2)
        few_hid = q_flat[:, D:D + 2 * FC * CAP].rearrange("p (i n) -> p i n", i=2)
        k_flat = kT[:, :, :].rearrange("p c t -> p (c t)")
        few_y = k_flat[0:CAP, 0:D]
        few_comb = k_flat[:, D:D + PER_GROUP * CAP]
        v_flat = v[:, :, :].rearrange("p t n -> p (t n)")
        onehot = v_flat[:, 0:TT * CAP].rearrange("p (t s) -> p t s", t=TT)
        onehotT = v_flat[0:CAP, D:D + T]
        few_hT = attnT[:, :, :].rearrange("p c t -> p (c t)")[:, 0:KC * CAP].rearrange("p (k s) -> p k s", k=KC)

        s_x = sem("s_x")
        s_c = sem("s_c")
        s_small = sem("s_small")
        s_route = sem("s_route")
        s_gfin = sem("s_gfin")
        s_const = sem("s_const")
        w_landed = [sem(f"w_landed{i}") for i in range(WSLOTS)]
        a_landed = [sem(f"a_landed{i}") for i in range(ASLOTS)]
        ada_rows = sem("ada_rows")
        out_full = sem("out_full")
        vec_ready = sem("vec_ready")
        gate_ready = sem("gate_ready")
        ss_ready = sem("ss_ready")
        rsqrt_ready = sem("rsqrt_ready")
        nrm = sem("nrm")
        turned = sem("turned")
        hT_dve = sem("hT_dve")
        hT_act = sem("hT_act")
        qkv_ready = sem("qkv_ready")
        z_full = sem("z_full")
        zm_ready = sem("zm_ready")
        act_step = sem("act_step")
        soft_ready = sem("soft_ready")
        sp_ready = sem("sp_ready")
        s_full = sem("s_full")
        t_ready = sem("t_ready")
        w_ready = sem("w_ready")
        av_full = sem("av_full")
        attn_ready = sem("attn_ready")
        b_max = sem("b_max")
        p_ready = sem("p_ready")
        b_norm = sem("b_norm")
        pT_ready = sem("pT_ready")
        o_step = sem("o_step")
        route = sem("route")
        route_exp = sem("route_exp")
        gu_full = sem("gu_full")
        silu_done = sem("silu_done")
        gu_free = sem("gu_free")
        y_full = sem("y_full")
        y_free = sem("y_free")
        y_sum = sem("y_sum")
        largest_ready = sem("largest_ready")
        placed = sem("placed")
        few_full = sem("few_full")
        few_hT_dve = sem("few_hT_dve")
        few_hT_act = sem("few_hT_act")
        few_comb_ready = sem("few_comb_ready")
        few_turned = sem("few_turned")
        few_turn_ready = sem("few_turn_ready")
        few_up = sem("few_up")
        few_y_ready = sem("few_y_ready")
        few_back = sem("few_back")
        few_added = sem("few_added")
        comb_ready = sem("comb_ready")
        moe_done = sem("moe_done")
        s_out = sem("s_out")

        wslot = [wring[:, i, :] for i in range(WSLOTS)]

        def w_cols(slot):
            return wslot[slot].rearrange("p (k n) -> p k n", k=KC)

        def w_rows(slot):
            return wslot[slot].rearrange("p (k n) -> p k n", k=FC)

        def wait_weights(eng, load, extra=0):
            eng.wait_ge(w_landed[load % WSLOTS], (extra + load // WSLOTS + 1) * 16)

        def wait_out_read(eng, i):
            kind, n = ITEMS[i][0:2]
            if kind in ("qkv", "kvq"):
                eng.wait_ge(qkv_ready, n + 1 + 12 * (kind == "kvq"))
            elif kind in ("o0", "o1"):
                eng.wait_ge(o_step, 2 * (n + UNITS * (kind == "o1")) + 1)
            elif kind == "route":
                eng.wait_ge(route, R_STEPS * n + 1)
            elif kind == "rank":
                eng.wait_ge(route, R_STEPS * n + R_RANK)
            elif is_gate(n):
                eng.wait_ge(gate_ready, 2 * GATE_ORDER.index(n) + ITEMS[i][2] + 1)
            else:
                eng.wait_ge(vec_ready, VEC_ORDER.index(n) + 1)

        def wait_out_free(pe, i):
            if i >= 2:
                wait_out_read(pe, i - 2)

        def pk(w):
            return w.rearrange("(p k) n -> p k n", k=KC)

        def cp(w):
            return w.rearrange("(c p) n -> p c n", p=P)

        def unit_source(item):
            kind, u = item
            cols = slice(u * COLS, (u + 1) * COLS)
            if kind == "qkv":
                return pk(w_qkv_a[0])[:, :, cols]
            if kind == "o0":
                return cp(w_o_a[0])[:, :, cols]
            if kind == "kvq" and u < 2 * UNITS:
                return pk(w_kv)[:, :, cols]
            if kind == "kvq":
                cols = slice((u - 2 * UNITS) * COLS, (u - 2 * UNITS + 1) * COLS)
                return pk(w_q_b[0])[:, :, cols]
            return cp(w_o_b[0])[:, :, cols]

        def ada_source(n):
            vv, part = n // PARTS, n % PARTS
            if vv in (KV_SHIFT, KV_SCALE):
                w, j = w_ada_kv, vv - KV_SHIFT
            else:
                l, j = (0, vv) if vv < 6 else (1, vv - 8)
                w = w_ada[l]
            return pk(w)[:, part * ROWS:(part + 1) * ROWS, j * D:(j + 1) * D]

        HT_COUNT = {0: 4, 1: 8, 2: 16, 3: 20}

        def modulated(norm):
            if norm == 2:
                return [(hkvT, KV_SHIFT, KV_SCALE), (hT, vec(1, SHIFT_M), vec(1, SCALE_M))]
            return [(hT, *{0: (vec(0, SHIFT_M), vec(0, SCALE_M)), 1: (vec(0, SHIFT_F), vec(0, SCALE_F)),
                           3: (vec(1, SHIFT_F), vec(1, SCALE_F))}[norm])]

        CONSTS = 23
        SMALL = 16 * (3 + 5)
        ROUTE = 16 * 4 * DEPTH

        block = ctx.enter_context(nc.Block())

        @block.sync
        def _(sp_eng):
            sp_eng.dma_start(cT[:, :], c_in[0].rearrange("(p k) -> p k", k=KC)).then_inc(s_c, 16)
            for t in range(TT):
                sp_eng.dma_start(x[:, t, :], x_in[0, t * P:(t + 1) * P, :]).then_inc(s_x, 16)

            def released(load):
                for item, i in LOAD.items():
                    if i == load:
                        sp_eng.wait_ge(out_full, OUT[item] + 1)
                        return
                layer = 0 if load < LOAD_BASE[1] else 1
                g, j = divmod(load - MOE_BASE[layer], WSLOTS)
                moe_released(layer, j, g)

            def moe_released(layer, j, g):
                kind, e = GROUP_LOADS[j]
                if kind == "down":
                    sp_eng.wait_ge(y_full, g * 4 * PER_GROUP + (layer * EXPERTS + e) * 4 + 4)
                else:
                    sp_eng.wait_ge(gu_full, g * 2 * PER_GROUP + (layer * EXPERTS + e) * 2 + 1 + (kind == "up"))

            def expert_load(layer, j, g):
                kind, e = GROUP_LOADS[j]
                load = MOE_BASE[layer] + j
                src = {"gate": w_gate, "up": w_up, "down": w_down}[kind]
                one = src[layer, bass.ds(g * PER_GROUP + e, 1)].rearrange("o r n -> (o r) n")
                slot = load % WSLOTS
                if kind == "down":
                    sp_eng.dma_start(w_rows(slot), cp(one)).then_inc(w_landed[slot], 16)
                else:
                    sp_eng.dma_start(w_cols(slot), pk(one)).then_inc(w_landed[slot], 16)

            sp_eng.wait_ge(ada_rows, 8)
            for layer in range(DEPTH):
                for item in FIXED_LOADS[layer]:
                    load = LOAD[item]
                    if load >= WSLOTS:
                        released(load - WSLOTS)
                    sp_eng.dma_start(w_cols(load % WSLOTS), unit_source(item)).then_inc(w_landed[load % WSLOTS], 16)
                for j in range(WSLOTS):
                    released(MOE_BASE[layer] + j - WSLOTS)
                    expert_load(layer, j, 0)
                with sp_eng.Fori(1, GROUPS) as g:
                    for j in range(WSLOTS):
                        moe_released(layer, j, g - 1)
                        expert_load(layer, j, g)

            for t in range(TT):
                sp_eng.wait_ge(o_step, DEPTH * O_STEPS + t + 1)
                sp_eng.dma_start(out[0, t * P:(t + 1) * P, :], xn[:, t, :]).then_inc(s_out, 16)
            sp_eng.wait_ge(s_out, 16 * TT)

        @block.gpsimd
        def _(pool):
            def load_ada(n):
                if n >= ASLOTS:
                    pool.wait_ge(ada_rows, ROWS * (n - ASLOTS + 1))
                pool.dma_start(aring[:, n % ASLOTS, :, :], ada_source(n)).then_inc(a_landed[n % ASLOTS], 16)

            for n in range(ASLOTS):
                load_ada(n)
            pool.memset(ident[:, :], 0.0).then_inc(s_const, 1)
            pool.memset(one[:, :], 1.0).then_inc(s_const, 1)
            pool.memset(negone[:, :], -1.0).then_inc(s_const, 1)
            pool.memset(negtri[:, :], -1.0).then_inc(s_const, 1)
            pool.memset(maskA[:, :], 0.0).then_inc(s_const, 1)
            for j in range(GROUPS):
                pool.memset(desc[:, j:j + 1], float(GROUPS - j)).then_inc(s_const, 1)
            pool.iota(distI[:, 0:P], pattern=[[1, P]], base=0, channel_multiplier=-1).then_inc(s_const, 1)
            pool.iota(distI[:, P:], pattern=[[1, T]], base=-P, channel_multiplier=-1).then_inc(s_const, 1)
            pool.iota(placesI, pattern=[[1, CAP]], base=0, channel_multiplier=0).then_inc(s_const, 1)
            pool.memset(before[:, :], 1.0).then_inc(s_const, 1)
            pool.memset(where[:, :, :, :], 0.0).then_inc(s_const, 1)
            pool.wait_ge(s_const, 14)
            pool.affine_select(out=ident[:, :], in_=ident[:, :], compare_op=ALU.not_equal, fill=1.0, base=0,
                               pattern=[[-1, P]], channel_multiplier=1).then_inc(s_const, 1)
            pool.affine_select(out=negtri[:, :], in_=negtri[:, :], compare_op=ALU.is_ge, fill=0.0, base=0,
                               pattern=[[-1, P]], channel_multiplier=1).then_inc(s_const, 1)
            for lo, n in ((0, T), (T, P)):
                pool.affine_select(out=maskA[:, lo:lo + n], in_=maskA[:, lo:lo + n], compare_op=ALU.is_ge, fill=NEG,
                                   base=-1, pattern=[[1, n]], channel_multiplier=-1).then_inc(s_const, 1)
            pool.tensor_copy(distB[:, :], distI[:, :]).then_inc(s_const, 1)
            pool.tensor_copy(places[:, :], placesI).then_inc(s_const, 1)
            pool.affine_select(out=before[:, :], in_=before[:, :], compare_op=ALU.is_ge, fill=0.0, base=-1,
                               pattern=[[1, P]], channel_multiplier=-1).then_inc(s_const, 1)
            pool.wait_ge(s_const, 21)
            for lo, n, off in ((0, P, 0), (P, T, P)):
                pool.affine_select(out=distB[:, lo:lo + n], in_=distB[:, lo:lo + n], compare_op=ALU.is_ge, fill=NEG,
                                   base=off, pattern=[[-1, n]], channel_multiplier=1).then_inc(s_const, 1)
            for n in range(ASLOTS, VECS * PARTS):
                load_ada(n)
            pool.wait_ge(o_step, DEPTH * O_STEPS)
            pool.dma_start(gfin[:, :], g_final.rearrange("(o n) -> o n", o=1).broadcast_to([P, D])).then_inc(s_gfin, 16)

        @block.tensor
        def _(pe):
            mm = pe.matmul

            def sum_vector(vv):
                pe.wait_ge(ada_rows, KC * (vv + 1))
                rows = acc[:, vv % 2, :]
                if not is_gate(vv):
                    i = OUT[("sum", vv, 0)]
                    wait_out_free(pe, i)
                    b = out_bank[i % 2]
                    by_chunk = rows.rearrange("p (q k) -> p k q", k=KC)
                    bias_by_chunk = bias14[:, :].rearrange("p (q k) -> p k q", k=KC)
                    for k in range(KC):
                        mm(b[:, k:k + 1], by_chunk[:, k, :], one[:, 0:1], start=True, stop=False)
                        last = mm(b[:, k:k + 1], bias_by_chunk[:, k, :], ident[0:VECS, vv:vv + 1],
                                  start=False, stop=True)
                    last.then_inc(out_full, 1)
                    return
                for half in range(2):
                    i = OUT[("sum", vv, half)]
                    wait_out_free(pe, i)
                    cols = slice(half * 512, half * 512 + 512)
                    mm(out_bank[i % 2][:, :], ones, rows[:, cols], start=True, stop=False)
                    mm(out_bank[i % 2][:, :], ident[0:VECS, vv:vv + 1].broadcast_to([VECS, P]), bias14[:, cols],
                       start=False, stop=True).then_inc(out_full, 1)

            def turn(norm):
                by_chunk = xn[:, :, :].rearrange("p t (q k) -> p t k q", k=KC)
                for j in range(4):
                    for a in range(2):
                        for t in range(TT):
                            pe.wait_ge(nrm, 7 * norm + 6 + t)
                            col = a * T + t * P
                            last = pe.transpose(turn_bank[j][:, col:col + P], by_chunk[:, t, 2 * j + a, :], ident[:, :])
                    last.then_inc(turned, 1)

            def feature_unit(item, rhsT):
                i, load = OUT[item], LOAD[item]
                wait_out_free(pe, i)
                wait_weights(pe, load)
                w = w_cols(load % WSLOTS)
                for half in range(2):
                    for k in range(KC):
                        last = mm(out_bank[i % 2][:, half * T:(half + 1) * T], w[:, k, half * P:(half + 1) * P],
                                  rhsT[:, k, :], start=(k == 0), stop=(k == KC - 1))
                last.then_inc(out_full, 1)

            def token_unit(item, lhsT):
                i, load = OUT[item], LOAD[item]
                wait_out_free(pe, i)
                wait_weights(pe, load)
                w = w_cols(load % WSLOTS)
                for t in range(TT):
                    for k in range(KC):
                        last = mm(out_bank[i % 2][:, t * COLS:(t + 1) * COLS], lhsT[:, k, t * P:(t + 1) * P],
                                  w[:, k, :], start=(k == 0), stop=(k == KC - 1))
                last.then_inc(out_full, 1)

            def head_rows(h):
                return slice(HD * (h % 2), HD * (h % 2) + HD), h // 2

            def scores_a(h):
                if h >= 2:
                    pe.wait_ge(zm_ready, h - 1)
                r, c = head_rows(h)
                z = z_bank[h % 2]
                mm(z[:, 0:T], kT[r, c, 0:P], qT[r, c, :], start=True, stop=True)
                mm(z[:, T:CAUSAL], kT[r, c, P:T], qT[r, c, P:T], start=True, stop=True).then_inc(z_full, 1)

            def suffix_a(h):
                pe.wait_ge(sp_ready, h + 1)
                if h >= 2:
                    pe.wait_ge(t_ready, h - 1)
                s, w = s_bank[h % 2], sp[:, h % 2, :]
                mm(s[:, 0:P], negtri[:, :], w[:, 0:P], start=True, stop=True)
                mm(s[:, P:T], negtri[:, :], w[:, P:T], start=True, stop=False)
                mm(s[:, P:T], negones, w[:, T:CAUSAL], start=False, stop=True)
                mm(s[:, T:CAUSAL], negtri[:, :], w[:, T:CAUSAL], start=True, stop=True).then_inc(s_full, 1)

            def values(h, ready, count, layer):
                pe.wait_ge(ready, count)
                r, c = head_rows(h)
                if h % 2 == 0 and c + layer * PAIRS >= 2:
                    pe.wait_ge(attn_ready, c + layer * PAIRS - 1)
                o, w = av_bank[c % 2], prob[:, h % 2, :]
                vh = v[:, :, h * HD:(h + 1) * HD]
                mm(o[r, 0:P], vh[:, 0, :], w[:, 0:P], start=True, stop=True)
                mm(o[r, P:T], vh[:, 0, :], w[:, P:T], start=True, stop=False)
                mm(o[r, P:T], vh[:, 1, :], w[:, T:CAUSAL], start=False, stop=True).then_inc(av_full, 1)

            def scores_b(h):
                if h >= 2:
                    pe.wait_ge(b_max, 3 * (h - 2) + 1)
                r, c = head_rows(h)
                z = z_bank[h % 2]
                mm(z[:, 0:P], qT[r, c, 0:P], kT[r, c, 0:P], start=True, stop=True)
                mm(z[:, P:CAUSAL], qT[r, c, P:T], kT[r, c, :], start=True, stop=True).then_inc(z_full, 1)

            def turn_b(h):
                pe.wait_ge(b_norm, 3 * h + 3)
                if h >= 2:
                    pe.wait_ge(pT_ready, h - 1)
                s, p = s_bank[h % 2], zm[:, h % 4, :]
                pe.transpose(s[:, 0:P], p[:, 0:P], ident[:, :])
                pe.transpose(s[:, P:T], p[:, P:T], ident[:, :])
                pe.transpose(s[:, T:CAUSAL], p[:, T:CAUSAL], ident[:, :]).then_inc(s_full, 1)

            def router(layer):
                i = OUT[("route", layer)]
                wait_out_free(pe, i)
                for t in range(TT):
                    for k in range(KC):
                        last = mm(out_bank[i % 2][:, t * 32:t * 32 + GROUPS + EXPERTS], hT[:, k, t * P:(t + 1) * P],
                                  w_r[:, layer, k, :], start=(k == 0), stop=(k == KC - 1))
                last.then_inc(out_full, 1)

            def gate_up(layer, j, g):
                e = layer * EXPERTS + j
                pe.wait_ge(gu_free, g * PER_GROUP + e + 1)
                for n, kind in enumerate(("gate", "up")):
                    load = MOE_BASE[layer] + GROUP_LOADS.index((kind, j))
                    wait_weights(pe, load, g)
                    w = w_cols(load % WSLOTS)
                    b = gu_bank[j % 2][n]
                    for f in range(FC):
                        for k in range(KC):
                            last = mm(b[:, f * T:(f + 1) * T], w[:, k, f * P:(f + 1) * P], hT[:, k, :],
                                      start=(k == 0), stop=(k == KC - 1))
                    last.then_inc(gu_full, 1)

            def down(layer, j, g):
                e = layer * EXPERTS + j
                load = MOE_BASE[layer] + GROUP_LOADS.index(("down", j))
                wait_weights(pe, load, g)
                pe.wait_ge(gu_free, g * PER_GROUP + e + 3)
                w = w_rows(load % WSLOTS)
                hT_e = hid[:, j % 2, :].rearrange("p (f t) -> p f t", f=FC)
                for q in range(4):
                    t, half = divmod(q, 2)
                    pe.wait_ge(y_free, g * 4 * PER_GROUP + 4 * e + q + 1)
                    for f in range(FC):
                        last = mm(y_bank[q][:, :], hT_e[:, f, t * P:(t + 1) * P], w[:, f, half * 512:half * 512 + 512],
                                  start=(f == 0), stop=(f == FC - 1))
                    last.then_inc(y_full, 1)

            def rank(layer):
                i = OUT[("rank", layer)]
                wait_out_free(pe, i)
                pe.wait_ge(route, R_STEPS * layer + R_GROUP)
                b = out_bank[i % 2]
                n = GROUPS
                member = [rt[:, 0, t, :] for t in range(TT)]
                mm(b[:, 0:n], before[:, :], member[0], start=True, stop=True)
                mm(b[:, n:2 * n], ones, member[0], start=True, stop=False)
                mm(b[:, n:2 * n], before[:, :], member[1], start=False, stop=True)
                mm(b[:, 2 * n:3 * n], ones, member[0], start=True, stop=False)
                mm(b[:, 2 * n:3 * n], ones, member[1], start=False, stop=True).then_inc(out_full, 1)

            def dense_experts(layer):
                with pe.Fori(0, GROUPS) as g:
                    gate_up(layer, 0, g)
                    for j in range(PER_GROUP):
                        if j + 1 < PER_GROUP:
                            gate_up(layer, j + 1, g)
                        down(layer, j, g)

            def gather(layer, g):
                n = layer * GROUPS
                pe.wait_ge(placed, g * F_STEPS + F_STEPS * (n + 1))
                by_chunk = xn[:, :, :].rearrange("p t (q k) -> p t k q", k=KC)
                for half in range(2):
                    for a in range(KC // 2):
                        for t in range(TT):
                            last = mm(few_bank[half][:, a * CAP:(a + 1) * CAP], by_chunk[:, t, half * KC // 2 + a, :],
                                      onehot[:, t, :], start=(t == 0), stop=(t == TT - 1))
                    last.then_inc(few_full, 1)

            def gather_comb(layer, g):
                n = layer * GROUPS
                pe.wait_ge(comb_ready, g + n + 1)
                for j in range(PER_GROUP):
                    for t in range(TT):
                        last = mm(comb_bank[:, j * CAP:(j + 1) * CAP], comb_g[:, t, j:j + 1].broadcast_to([P, P]),
                                  onehot[:, t, :], start=(t == 0), stop=(t == TT - 1))
                last.then_inc(few_full, 1)

            def turn_places(layer, g):
                for t in range(TT):
                    last = pe.transpose(place_bank[0:CAP, t * P:(t + 1) * P], onehot[:, t, :], ident[:, :])
                last.then_inc(few_turned, 1)

            def few_gate_up(layer, j, g):
                e = layer * EXPERTS + j
                n = layer * GROUPS
                pe.wait_ge(gu_free, g * PER_GROUP + e + 1)
                if j == 0:
                    pe.wait_ge(few_hT_dve, g * (KC // 2) + (n + 1) * (KC // 2))
                    pe.wait_ge(few_hT_act, g * (KC // 2) + (n + 1) * (KC // 2))
                    pe.wait_ge(few_comb_ready, g + n + 1)
                    pe.wait_ge(few_turn_ready, g + n + 1)
                if j == 1:
                    pe.wait_ge(few_added, g * 4 + 4 * n + 2)
                for m, kind in enumerate(("gate", "up")):
                    load = MOE_BASE[layer] + GROUP_LOADS.index((kind, j))
                    wait_weights(pe, load, g)
                    w = w_cols(load % WSLOTS)
                    b = gu_bank[j % 2][m]
                    for f in range(FC):
                        for k in range(KC):
                            last = mm(b[:, f * CAP:(f + 1) * CAP], w[:, k, f * P:(f + 1) * P], few_hT[:, k, :],
                                      start=(k == 0), stop=(k == KC - 1))
                    last.then_inc(gu_full, 1)

            def few_down(layer, j, g):
                e = layer * EXPERTS + j
                load = MOE_BASE[layer] + GROUP_LOADS.index(("down", j))
                wait_weights(pe, load, g)
                pe.wait_ge(gu_free, g * PER_GROUP + e + 3)
                if j == 0:
                    pe.wait_ge(few_added, g * 4 + 4 * layer * GROUPS + 4)
                w = w_rows(load % WSLOTS)
                hT_e = few_hid[:, j % 2, :].rearrange("p (f s) -> p f s", f=FC)
                for half in range(2):
                    for f in range(FC):
                        mm(few_y_bank[half][0:CAP, :], hT_e[:, f, :], w[:, f, half * 512:half * 512 + 512],
                           start=(j == 0 and f == 0), stop=(j == PER_GROUP - 1 and f == FC - 1)).then_inc(y_full, 1)

            def scatter(layer, g):
                n = layer * GROUPS
                for q in range(4):
                    t, half = divmod(q, 2)
                    pe.wait_ge(few_y_ready, g * 2 + 2 * n + (half + 1 if q < 2 else 2))
                    mm(back_bank[q][:, :], onehotT[:, t * P:(t + 1) * P], few_y[:, half * 512:half * 512 + 512],
                       start=True, stop=True).then_inc(few_back, 1)

            def few_group(layer, g, last):
                few_gate_up(layer, 0, g)
                for j in range(PER_GROUP):
                    if j + 1 < PER_GROUP:
                        few_gate_up(layer, j + 1, g)
                    few_down(layer, j, g)
                if not last:
                    gather(layer, g + 1)
                    gather_comb(layer, g + 1)
                scatter(layer, g)
                if not last:
                    turn_places(layer, g + 1)

            def routed_experts(layer):
                gather(layer, 0)
                gather_comb(layer, 0)
                turn_places(layer, 0)
                with pe.Fori(0, GROUPS - 1) as g:
                    few_group(layer, g, False)
                few_group(layer, GROUPS - 1, True)

            def experts(layer):
                pe.wait_ge(largest_ready, 2 * (layer + 1))
                size = pe.value_load(largestI[0:1, layer:layer + 1], min_val=0, max_val=T)
                wait_out_read(pe, OUT[("route", layer)])
                wait_out_read(pe, OUT[("rank", layer)])
                with pe.If(size <= CAP):
                    routed_experts(layer)
                with pe.Else():
                    pe.sem_inc(few_full, 3 * GROUPS)
                    pe.sem_inc(few_turned, GROUPS)
                    pe.sem_inc(few_back, 4 * GROUPS)
                    dense_experts(layer)

            def wait_hT(norm):
                pe.wait_ge(hT_dve, HT_COUNT[norm])
                pe.wait_ge(hT_act, HT_COUNT[norm])

            pe.wait_ge(s_const, CONSTS)
            pe.wait_ge(s_small, SMALL)
            sum_vector(0)
            sum_vector(1)
            turn(0)
            wait_hT(0)
            pe.wait_ge(s_route, ROUTE)
            for u in range(12):
                if u < 2 * UNITS:
                    feature_unit(("qkv", u), hT)
                else:
                    token_unit(("qkv", u), hT)
                if u in SUM_AFTER_QKV0:
                    sum_vector(SUM_AFTER_QKV0[u])
            pe.wait_ge(qkv_ready, 12)
            for i in range(HEADS + 3):
                if i < HEADS:
                    scores_a(i)
                if 1 <= i <= HEADS:
                    suffix_a(i - 1)
                if i in SUM_AFTER_HEAD0:
                    sum_vector(SUM_AFTER_HEAD0[i])
                if i >= 3:
                    values(i - 3, w_ready, i - 2, 0)
            sum_vector(8)
            pe.wait_ge(attn_ready, PAIRS)
            for u in range(UNITS):
                token_unit(("o0", u), attnT)
            sum_vector(9)
            turn(1)
            wait_hT(1)
            router(0)
            rank(0)
            experts(0)

            turn(2)
            wait_hT(2)
            for u in range(12):
                if u < UNITS:
                    feature_unit(("kvq", u), hkvT)
                elif u < 2 * UNITS:
                    token_unit(("kvq", u), hkvT)
                else:
                    feature_unit(("kvq", u), hT)
                if u in SUM_AFTER_KVQ1:
                    sum_vector(SUM_AFTER_KVQ1[u])
            pe.wait_ge(qkv_ready, 24)
            for i in range(HEADS + 3):
                if i < HEADS:
                    scores_b(i)
                if 2 <= i < HEADS + 2:
                    turn_b(i - 2)
                if i in SUM_AFTER_HEAD1:
                    sum_vector(SUM_AFTER_HEAD1[i])
                if i >= 3:
                    values(i - 3, pT_ready, i - 2, 1)
            pe.wait_ge(attn_ready, 2 * PAIRS)
            for u in range(UNITS):
                token_unit(("o1", u), attnT)
            turn(3)
            wait_hT(3)
            router(1)
            rank(1)
            experts(1)

        @block.scalar
        def _(act):
            steps = [0]

            def own(ins):
                ins.then_inc(act_step, 1)
                steps[0] += 1
                act.wait_ge(act_step, steps[0])

            def squares(norm):
                for t in range(TT):
                    if norm == 0:
                        act.wait_ge(s_x, 16 * TT)
                    elif norm in (1, 3):
                        act.wait_ge(o_step, O_STEPS * (norm // 2 + 1))
                    else:
                        act.wait_ge(moe_done, norm // 2)
                    act.activation(xn[:, t, :], x[:, t, :], ACT.Square, accum_out=ss[:, t:t + 1]).then_inc(ss_ready, 1)

            def rsqrt(norm):
                act.wait_ge(nrm, 7 * norm + 1)
                act.activation(rtmp[:, 0, :], ms[:, :], ACT.Ln).then_inc(rsqrt_ready, 1)
                act.wait_ge(rsqrt_ready, 2 * norm + 1)
                act.activation(rtmp[:, 0, :], rtmp[:, 0, :], ACT.Exp, scale=-0.5).then_inc(rsqrt_ready, 1)

            def modulate(norm):
                act.wait_ge(vec_ready, 1 + max(VEC_ORDER.index(a) for _, sh, a in modulated(norm)))
                for j in (1, 3):
                    act.wait_ge(turned, 4 * norm + j + 1)
                    for dst, sh, a in modulated(norm):
                        for n in range(2):
                            k = 2 * j + n
                            act.activation(dst[:, k, :], turn_bank[j][:, n * T:(n + 1) * T], ACT.Identity,
                                           bias=shift[:, sh, k:k + 1], scale=shift[:, a, k:k + 1]).then_inc(hT_act, 1)

            def take(item, dst):
                i = OUT[item]
                act.wait_ge(out_full, i + 1)
                act.activation(dst, out_bank[i % 2][:, :].rearrange("p (a n) -> p a n", a=2), ACT.Copy)\
                   .then_inc(qkv_ready, 1)

            def gate(vv, dst):
                for half in range(2):
                    i = OUT[("sum", vv, half)]
                    act.wait_ge(out_full, i + 1)
                    act.activation(dst[:, half * 512:half * 512 + 512], out_bank[i % 2][:, :], ACT.Copy, bias=1.0)\
                       .then_inc(gate_ready, 1)

            def attn_out(c, layer):
                act.wait_ge(av_full, 2 * (c + 1) + layer * HEADS)
                act.activation(attnT[:, c, :], av_bank[c % 2][:, 0:T], ACT.Copy).then_inc(attn_ready, 1)

            def soft_a(h):
                act.wait_ge(zm_ready, h + 1)
                if h >= 2:
                    act.wait_ge(sp_ready, h - 1)
                s = soft[:, h % 2, :]
                own(act.activation(s, zm[:, h % 4, :], ACT.Abs))
                own(act.activation(s, s, ACT.Exp, scale=-1.0))
                act.activation(s, s, ACT.Ln, bias=1.0).then_inc(soft_ready, 1)

            def weights_a(h):
                act.wait_ge(t_ready, h + 1)
                if h >= 2:
                    act.wait_ge(av_full, h - 1)
                act.activation(prob[:, h % 2, :], zm[:, h % 4, :], ACT.Exp).then_inc(w_ready, 1)

            def exps_b(h):
                act.wait_ge(b_max, 3 * h + 3)
                for t, cols in ((0, slice(0, P)), (1, slice(P, CAUSAL))):
                    act.activation(zm[:, h % 4, cols], zm[:, h % 4, cols], ACT.Exp, scale=SCALE,
                                   bias=nmx[:, h % 2, t:t + 1], accum_out=den[:, h % 2, t:t + 1]).then_inc(p_ready, 1)

            def probs_b(h):
                act.wait_ge(s_full, HEADS + h + 1)
                if h >= 2:
                    act.wait_ge(av_full, HEADS + h - 1)
                act.activation(prob[:, h % 2, :], s_bank[h % 2][:, 0:CAUSAL], ACT.Copy).then_inc(pT_ready, 1)

            def router(layer):
                act.wait_ge(route, R_STEPS * layer + R_EXP1)
                act.activation(rt[:, 4, :, :], rt[:, 4, :, :], ACT.Exp).then_inc(route_exp, 1)
                act.wait_ge(route, R_STEPS * layer + R_EXP2)
                act.activation(r1[:, 6, :], r1[:, 6, :], ACT.Exp).then_inc(route_exp, 1)

            def few_modulate(layer, g):
                act.wait_ge(few_full, g * 3 + 3 * layer * GROUPS + 2)
                for a in range(KC // 2):
                    k = KC // 2 + a
                    act.activation(few_hT[:, k, :], few_bank[1][:, a * CAP:(a + 1) * CAP], ACT.Identity,
                                   bias=shift[:, vec(layer, SHIFT_F), k:k + 1],
                                   scale=shift[:, vec(layer, SCALE_F), k:k + 1]).then_inc(few_hT_act, 1)

            def few_places(layer, g):
                act.wait_ge(few_turned, g + layer * GROUPS + 1)
                act.activation(onehotT, place_bank[0:CAP, 0:T], ACT.Copy).then_inc(few_turn_ready, 1)

            def few_group(layer, g, last):
                for j in range(PER_GROUP):
                    e = layer * EXPERTS + j
                    act.wait_ge(gu_full, g * 2 * PER_GROUP + 2 * e + 1)
                    act.wait_ge(gu_free, g * PER_GROUP + e + 1)
                    act.activation(few_sg[:, j % 2, :], gu_bank[j % 2][0][:, 0:FC * CAP], ACT.Silu)\
                       .then_inc(silu_done, 1)
                if not last:
                    few_modulate(layer, g + 1)
                    few_places(layer, g + 1)

            def experts(layer):
                act.wait_ge(largest_ready, 2 * (layer + 1))
                size = act.value_load(largestI[0:1, layer:layer + 1], min_val=0, max_val=T)
                with act.If(size <= CAP):
                    few_modulate(layer, 0)
                    router(layer)
                    few_places(layer, 0)
                    with act.Fori(0, GROUPS - 1) as g:
                        few_group(layer, g, False)
                    few_group(layer, GROUPS - 1, True)
                with act.Else():
                    act.sem_inc(few_hT_act, GROUPS * KC // 2)
                    act.sem_inc(few_turn_ready, GROUPS)
                    router(layer)
                    dense_experts(layer)

            def dense_experts(layer):
                with act.Fori(0, GROUPS) as g:
                    for j in range(PER_GROUP):
                        e = layer * EXPERTS + j
                        act.wait_ge(gu_full, g * 2 * PER_GROUP + 2 * e + 1)
                        act.wait_ge(gu_free, g * PER_GROUP + e + 1)
                        act.activation(sg[:, j % 2, :], gu_bank[j % 2][0][:, :], ACT.Silu).then_inc(silu_done, 1)

            act.dma_start(bias14[0:6, :], b_ada[0].rearrange("(j n) -> j n", n=D)).then_inc(s_small, 16)
            act.dma_start(bias14[6:8, :], b_ada_kv.rearrange("(j n) -> j n", n=D)).then_inc(s_small, 16)
            act.dma_start(bias14[8:14, :], b_ada[1].rearrange("(j n) -> j n", n=D)).then_inc(s_small, 16)
            for vv, g_ap in ((vec(0, SCALE_M), g_attn[0]), (vec(0, SCALE_F), g_ffn[0]), (KV_SCALE, g_kv),
                             (vec(1, SCALE_M), g_attn[1]), (vec(1, SCALE_F), g_ffn[1])):
                act.dma_start(gains[:, vv, :], g_ap.rearrange("(p k) -> p k", k=KC)).then_inc(s_small, 16)
            squares(0)
            rsqrt(0)
            for l in range(DEPTH):
                act.dma_start(w_r[:, l, :, 0:GROUPS], pk(w_rg[l])).then_inc(s_route, 16)
                act.dma_start(w_r[:, l, :, GROUPS:], pk(w_re[l])).then_inc(s_route, 16)
                act.dma_start(b_r[:, l, 0:GROUPS], b_rg[l:l + 1, :].broadcast_to([P, GROUPS])).then_inc(s_route, 16)
                act.dma_start(b_r[:, l, GROUPS:], b_re[l:l + 1, :].broadcast_to([P, EXPERTS])).then_inc(s_route, 16)

            modulate(0)
            for u in range(12):
                if u < 2 * UNITS:
                    dst = qT if u < UNITS else kT
                    take(("qkv", u), dst[:, 2 * (u % UNITS):2 * (u % UNITS) + 2, :])
                else:
                    take(("qkv", u), v[:, :, (u - 2 * UNITS) * COLS:(u - 2 * UNITS + 1) * COLS])
                if SUM_AFTER_QKV0.get(u) == vec(0, GATE_M):
                    gate(vec(0, GATE_M), gate_m)
            for i in range(HEADS + 4):
                if i < HEADS:
                    soft_a(i)
                if 2 <= i < HEADS + 2:
                    weights_a(i - 2)
                if SUM_AFTER_HEAD0.get(i) == vec(0, GATE_F):
                    gate(vec(0, GATE_F), gate_f)
                if i >= 4 and i % 2:
                    attn_out((i - 4) // 2, 0)
            squares(1)
            rsqrt(1)
            modulate(1)
            experts(0)

            squares(2)
            rsqrt(2)
            modulate(2)
            for u in range(12):
                if u < UNITS:
                    take(("kvq", u), kT[:, 2 * u:2 * u + 2, :])
                elif u < 2 * UNITS:
                    take(("kvq", u), v[:, :, (u - UNITS) * COLS:(u - UNITS + 1) * COLS])
                else:
                    take(("kvq", u), qT[:, 2 * (u - 2 * UNITS):2 * (u - 2 * UNITS) + 2, :])
                if SUM_AFTER_KVQ1.get(u) == vec(1, GATE_M):
                    gate(vec(1, GATE_M), gate_m)
            for i in range(HEADS + 4):
                if i < HEADS:
                    exps_b(i)
                if 2 <= i < HEADS + 2:
                    probs_b(i - 2)
                if SUM_AFTER_HEAD1.get(i) == vec(1, GATE_F):
                    gate(vec(1, GATE_F), gate_f)
                if i >= 4 and i % 2:
                    attn_out((i - 4) // 2, 1)
            squares(3)
            rsqrt(3)
            modulate(3)
            experts(1)
            squares(4)
            rsqrt(4)

        @block.vector
        def _(dve):
            counts = {}

            def step(semaphore, ins):
                ins.then_inc(semaphore, 1)
                counts[semaphore.name] = counts.get(semaphore.name, 0) + 1

            def settled(semaphore):
                dve.wait_ge(semaphore, counts[semaphore.name])

            def add_rows(n):
                vv, part = n // PARTS, n % PARTS
                dve.wait_ge(a_landed[n % ASLOTS], 16 * (n // ASLOTS + 1))
                if n == 0:
                    dve.wait_ge(s_c, 16)
                if part == 0 and vv >= 2:
                    dve.wait_ge(out_full, OUT[sum_items(vv - 2)[-1]] + 1)
                for r in range(ROWS):
                    k = part * ROWS + r
                    w = aring[:, n % ASLOTS, r, :]
                    a = acc[:, vv % 2, :]
                    if k == 0:
                        step(ada_rows, dve.tensor_scalar(a, w, cT[:, k:k + 1], None, ALU.mult))
                    else:
                        settled(ada_rows)
                        step(ada_rows, dve.scalar_tensor_tensor(out=a, in0=w, scalar=cT[:, k:k + 1], in1=a,
                                                                op0=ALU.mult, op1=ALU.add))

            def column(vv):
                i = OUT[("sum", vv, 0)]
                dve.wait_ge(out_full, i + 1)
                if is_scale(vv):
                    ins = dve.scalar_tensor_tensor(out=shift[:, vv, :], in0=out_bank[i % 2][:, 0:KC], scalar=1.0,
                                                   in1=gains[:, vv, :], op0=ALU.add, op1=ALU.mult)
                else:
                    ins = dve.tensor_copy(shift[:, vv, :], out_bank[i % 2][:, 0:KC])
                step(vec_ready, ins)

            def normalise(norm, last=False):
                dve.wait_ge(ss_ready, TT * (norm + 1))
                step(nrm, dve.tensor_scalar(ms[:, :], ss[:, :], 1.0 / D, EPS, ALU.mult, ALU.add))
                dve.wait_ge(rsqrt_ready, 2 * norm + 2)
                settled(nrm)
                step(nrm, dve.tensor_tensor(rtmp[:, 1, :], rtmp[:, 0, :], rtmp[:, 0, :], ALU.mult))
                settled(nrm)
                step(nrm, dve.tensor_tensor(rtmp[:, 2, :], rtmp[:, 1, :], ms[:, :], ALU.mult))
                settled(nrm)
                step(nrm, dve.tensor_scalar(rtmp[:, 3, :], rtmp[:, 2, :], -0.5, 1.5, ALU.mult, ALU.add))
                settled(nrm)
                step(nrm, dve.tensor_tensor(rstd[:, :], rtmp[:, 3, :], rtmp[:, 0, :], ALU.mult))
                settled(nrm)
                for t in range(TT):
                    if last:
                        step(o_step, dve.scalar_tensor_tensor(out=xn[:, t, :], in0=x[:, t, :], scalar=rstd[:, t:t + 1],
                                                              in1=gfin[:, :], op0=ALU.mult, op1=ALU.mult))
                    else:
                        step(nrm, dve.tensor_scalar(xn[:, t, :], x[:, t, :], rstd[:, t:t + 1], None, ALU.mult))

            def modulate(norm):
                settled(vec_ready)
                for j in (0, 2):
                    dve.wait_ge(turned, 4 * norm + j + 1)
                    for dst, sh, a in modulated(norm):
                        for n in range(2):
                            k = 2 * j + n
                            dve.tensor_scalar(dst[:, k, :], turn_bank[j][:, n * T:(n + 1) * T], shift[:, a, k:k + 1],
                                              shift[:, sh, k:k + 1], ALU.mult, ALU.add).then_inc(hT_dve, 1)

            def mask_a(h):
                dve.wait_ge(z_full, h + 1)
                if h >= 4:
                    dve.wait_ge(w_ready, h - 3)
                dve.scalar_tensor_tensor(out=zm[:, h % 4, :], in0=z_bank[h % 2][:, 0:CAUSAL], scalar=SCALE,
                                         in1=maskA[:, :], op0=ALU.mult, op1=ALU.add).then_inc(zm_ready, 1)

            def softplus_a(h):
                dve.wait_ge(soft_ready, h + 1)
                dve.wait_ge(zm_ready, h + 1)
                if h >= 2:
                    dve.wait_ge(s_full, h - 1)
                dve.scalar_tensor_tensor(out=sp[:, h % 2, :], in0=zm[:, h % 4, :], scalar=0.0, in1=soft[:, h % 2, :],
                                         op0=ALU.max, op1=ALU.add).then_inc(sp_ready, 1)

            def exponent_a(h):
                dve.wait_ge(s_full, h + 1)
                dve.wait_ge(sp_ready, h + 1)
                dve.tensor_tensor(zm[:, h % 4, :], s_bank[h % 2][:, 0:CAUSAL], zm[:, h % 4, :], ALU.add)\
                   .then_inc(t_ready, 1)

            def bias_max_b(h):
                dve.wait_ge(z_full, HEADS + h + 1)
                if h >= 4:
                    dve.wait_ge(s_full, HEADS + h - 3)
                slope = 2.0 ** (-8.0 * (h + 1) / HEADS)
                z = zm[:, h % 4, :]
                step(b_max, dve.scalar_tensor_tensor(out=z, in0=distB[:, :], scalar=slope / SCALE,
                                                     in1=z_bank[h % 2][:, 0:CAUSAL], op0=ALU.mult, op1=ALU.add))
                settled(b_max)
                if h >= 2:
                    dve.wait_ge(p_ready, 2 * (h - 1))
                dve.tensor_reduce(mx[:, h % 2, 0:1], z[:, 0:P], AX_X, ALU.max)
                step(b_max, dve.tensor_reduce(mx[:, h % 2, 1:2], z[:, P:CAUSAL], AX_X, ALU.max))
                settled(b_max)
                step(b_max, dve.tensor_scalar(nmx[:, h % 2, :], mx[:, h % 2, :], -SCALE, None, ALU.mult))

            def norm_b(h):
                dve.wait_ge(p_ready, 2 * (h + 1))
                step(b_norm, dve.reciprocal(rden[:, h % 2, :], den[:, h % 2, :]))
                settled(b_norm)
                for t, cols in ((0, slice(0, P)), (1, slice(P, CAUSAL))):
                    step(b_norm, dve.tensor_scalar(zm[:, h % 4, cols], zm[:, h % 4, cols], rden[:, h % 2, t:t + 1],
                                                   None, ALU.mult))

            def residual(item):
                i, u = OUT[item], item[1]
                cols = slice(u * COLS, (u + 1) * COLS)
                dve.wait_ge(out_full, i + 1)
                tmp = otmp[:, u % 2, :, :]
                step(o_step, dve.tensor_tensor(tmp, out_bank[i % 2][:, :].rearrange("p (t n) -> p t n", t=TT),
                                               gate_m[:, cols].unsqueeze(1).broadcast_to([P, TT, COLS]), ALU.mult))
                settled(o_step)
                step(o_step, dve.tensor_tensor(x[:, :, cols], x[:, :, cols], tmp, ALU.add))

            def first_max(src, peak, hit, score, best, dst):
                r(dve.tensor_reduce(peak, src, AX_X, ALU.max))
                r(dve.tensor_tensor(hit, src, peak.unsqueeze(2).broadcast_to([P, TT, 4]), ALU.is_equal))
                r(dve.tensor_tensor(score, hit, desc[:, :].unsqueeze(1).broadcast_to([P, TT, 4]), ALU.mult))
                r(dve.tensor_reduce(best, score, AX_X, ALU.max))
                r(dve.tensor_tensor(dst, score, best.unsqueeze(2).broadcast_to([P, TT, 4]), ALU.is_equal))

            def r(ins):
                step(route, ins)
                settled(route)

            def wide(row):
                return row.unsqueeze(2).broadcast_to([P, TT, 4])

            def router(layer):
                start = R_STEPS * layer
                i = OUT[("route", layer)]
                dve.wait_ge(out_full, i + 1)
                n = GROUPS + EXPERTS
                r(dve.tensor_tensor(lg[:, :, :], out_bank[i % 2][:, 0:64].rearrange("p (t n) -> p t n", t=TT)[:, :, 0:n],
                                    b_r[:, layer, :].unsqueeze(1).broadcast_to([P, TT, n]), ALU.add))
                groups = lg[:, :, 0:GROUPS]
                in_group = rt[:, 0, :, :]
                first_max(groups, r1[:, 0, :], rt[:, 1, :, :], rt[:, 2, :, :], r1[:, 1, :], in_group)
                r(dve.tensor_tensor(rt[:, 4, :, :], groups, wide(r1[:, 0, :]), ALU.subtract))
                assert counts[route.name] - start == R_EXP1

            def ranks(layer):
                i = OUT[("rank", layer)]
                dve.wait_ge(out_full, i + 1)
                b = out_bank[i % 2]
                r(dve.tensor_copy(where[:, 0, :, 0:GROUPS], b[:, 0:TT * GROUPS].rearrange("p (t g) -> p t g", t=TT)))
                r(dve.tensor_copy(where[:, 1, :, 0:GROUPS], rt[:, 0, :, :]))
                r(dve.tensor_reduce(largest[:, layer:layer + 1], b[:, TT * GROUPS:(TT + 1) * GROUPS], AX_X, ALU.max))
                dve.tensor_copy(largestI[:, layer:layer + 1], largest[:, layer:layer + 1]).then_inc(largest_ready, 2)

            def experts_router(layer):
                start = R_STEPS * layer
                in_group = rt[:, 0, :, :]
                r(dve.tensor_tensor(le_sel[:, :, :].rearrange("p t (g j) -> p t g j", g=GROUPS),
                                    lg[:, :, GROUPS:].rearrange("p t (g j) -> p t g j", g=GROUPS),
                                    in_group.unsqueeze(3).broadcast_to([P, TT, GROUPS, PER_GROUP]), ALU.mult))
                le, first, rest, second = rt[:, 5, :, :], rt[:, 6, :, :], rt[:, 7, :, :], rt[:, 8, :, :]
                r(dve.tensor_reduce(le, le_sel[:, :, :].rearrange("p t (g j) -> p t j g", g=GROUPS), AX_X, ALU.add))
                first_max(le, r1[:, 2, :], rt[:, 9, :, :], rt[:, 10, :, :], r1[:, 3, :], first)
                r(dve.scalar_tensor_tensor(out=rest, in0=first, scalar=-3.0e38, in1=le, op0=ALU.mult, op1=ALU.add))
                first_max(rest, r1[:, 4, :], rt[:, 9, :, :], rt[:, 10, :, :], r1[:, 5, :], second)
                r(dve.tensor_tensor(r1[:, 6, :], r1[:, 4, :], r1[:, 2, :], ALU.subtract))
                assert counts[route.name] - start == R_EXP2
                dve.wait_ge(route_exp, 2 * layer + 1)
                r(dve.tensor_reduce(r1[:, 7, :], rt[:, 4, :, :], AX_X, ALU.add))
                r(dve.reciprocal(r1[:, 8, :], r1[:, 7, :]))
                dve.wait_ge(route_exp, 2 * layer + 2)
                r(dve.tensor_scalar(r1[:, 9, :], r1[:, 6, :], 1.0, None, ALU.add))
                r(dve.reciprocal(r1[:, 10, :], r1[:, 9, :]))
                r(dve.tensor_tensor(r1[:, 11, :], r1[:, 10, :], r1[:, 8, :], ALU.mult))
                r(dve.tensor_tensor(r1[:, 0, :], r1[:, 6, :], r1[:, 11, :], ALU.mult))
                r(dve.tensor_tensor(rt[:, 9, :, :], first, wide(r1[:, 11, :]), ALU.mult))
                r(dve.tensor_tensor(rt[:, 10, :, :], second, wide(r1[:, 0, :]), ALU.mult))
                r(dve.tensor_tensor(rt[:, 11, :, :], rt[:, 9, :, :], rt[:, 10, :, :], ALU.add))
                r(dve.tensor_tensor(comb[:, :, :].rearrange("p t (g j) -> p t g j", g=GROUPS),
                                    in_group.unsqueeze(3).broadcast_to([P, TT, GROUPS, PER_GROUP]),
                                    rt[:, 11, :, :].unsqueeze(2).broadcast_to([P, TT, GROUPS, PER_GROUP]), ALU.mult))
                assert counts[route.name] - start == R_STEPS

            def place(layer, g):
                n = F_STEPS * layer * GROUPS
                if not (isinstance(g, int) and g == 0):
                    dve.wait_ge(few_turned, g + layer * GROUPS)
                dve.tensor_copy(where_g[:, :, :], where[:, :, :, bass.ds(g, 1)].rearrange("p a t o -> p a (t o)"))\
                   .then_inc(placed, 1)
                dve.wait_ge(placed, g * F_STEPS + n + 1)
                for t in range(TT):
                    dve.tensor_scalar(onehot[:, t, :], places[:, :], where_g[:, 0, t:t + 1], where_g[:, 1, t:t + 1],
                                      ALU.is_equal, ALU.mult).then_inc(placed, 1)

            def combine(layer, g):
                dve.tensor_copy(comb_g[:, :, :], comb[:, :, bass.ds(g * PER_GROUP, PER_GROUP)]).then_inc(comb_ready, 1)

            def few_gathered(layer, g):
                n = layer * GROUPS
                dve.wait_ge(few_full, g * 3 + 3 * n + 1)
                for k in range(KC // 2):
                    dve.tensor_scalar(few_hT[:, k, :], few_bank[0][:, k * CAP:(k + 1) * CAP],
                                      shift[:, vec(layer, SCALE_F), k:k + 1], shift[:, vec(layer, SHIFT_F), k:k + 1],
                                      ALU.mult, ALU.add).then_inc(few_hT_dve, 1)

            def few_combine(layer, g):
                dve.wait_ge(few_full, g * 3 + 3 * layer * GROUPS + 3)
                dve.tensor_copy(few_comb, comb_bank[:, 0:PER_GROUP * CAP]).then_inc(few_comb_ready, 1)

            def few_hidden(layer, j, g):
                e = layer * EXPERTS + j
                weight = few_comb[:, j * CAP:(j + 1) * CAP].unsqueeze(1).broadcast_to([P, FC, CAP])
                dve.wait_ge(gu_full, g * 2 * PER_GROUP + 2 * e + 2)
                if j == 0:
                    dve.wait_ge(few_comb_ready, g + layer * GROUPS + 1)
                dve.tensor_tensor(few_uc[:, j % 2, :].rearrange("p (f s) -> p f s", f=FC),
                                  gu_bank[j % 2][1][:, 0:FC * CAP].rearrange("p (f s) -> p f s", f=FC),
                                  weight, ALU.mult).then_inc(few_up, 1)
                if j >= 2:
                    dve.wait_ge(y_full, g * 4 * PER_GROUP + 4 * (e - 1))
                dve.wait_ge(silu_done, g * PER_GROUP + e + 1)
                dve.wait_ge(few_up, g * PER_GROUP + e + 1)
                dve.tensor_tensor(few_hid[:, j % 2, :], few_sg[:, j % 2, :], few_uc[:, j % 2, :], ALU.mult)\
                   .then_inc(gu_free, 1)

            def few_output(layer, g):
                for half in range(2):
                    cols = slice(half * 512, half * 512 + 512)
                    dve.wait_ge(y_full, g * 4 * PER_GROUP + 4 * PER_GROUP * (layer * GROUPS + 1) - 2 + 2 * half)
                    dve.tensor_tensor(few_y[:, cols], few_y_bank[half][0:CAP, :], gate_f[0:CAP, cols], ALU.mult)\
                       .then_inc(few_y_ready, 1)

            def few_add(layer, g, last):
                n = 4 * layer * GROUPS
                for q in range(4):
                    t, half = divmod(q, 2)
                    cols = slice(half * 512, half * 512 + 512)
                    dve.wait_ge(few_back, g * 4 + n + q + 1)
                    dve.wait_ge(few_added, g * 4 + n + q + 1)
                    ins = dve.tensor_tensor(x[:, t, cols], x[:, t, cols], back_bank[q][:, :], ALU.add)
                    ins.then_inc(few_added, 1)
                if last:
                    dve.wait_ge(few_added, n + 4 * GROUPS + 4)
                    dve.sem_inc(moe_done, 1)

            def few_group(layer, g, last):
                for j in range(PER_GROUP):
                    few_hidden(layer, j, g)
                    if j == 0 and not last:
                        place(layer, g + 1)
                        combine(layer, g + 1)
                few_output(layer, g)
                if not last:
                    few_gathered(layer, g + 1)
                    few_combine(layer, g + 1)
                few_add(layer, g, last)

            def experts(layer):
                settled_value = 2 * (layer + 1)
                dve.wait_ge(largest_ready, settled_value)
                size = dve.value_load(largestI[0:1, layer:layer + 1], min_val=0, max_val=T)
                with dve.If(size <= CAP):
                    dve.sem_inc(y_free, 4 * EXPERTS)
                    dve.sem_inc(y_sum, Y_GROUP * GROUPS)
                    place(layer, 0)
                    few_gathered(layer, 0)
                    experts_router(layer)
                    dve.wait_ge(gate_ready, 4 * (layer + 1))
                    combine(layer, 0)
                    few_combine(layer, 0)
                    with dve.Fori(0, GROUPS - 1) as g:
                        few_group(layer, g, False)
                    few_group(layer, GROUPS - 1, True)
                with dve.Else():
                    for semaphore, n in ((placed, F_STEPS * GROUPS), (comb_ready, GROUPS), (few_hT_dve, GROUPS * KC // 2),
                                         (few_comb_ready, GROUPS), (few_up, EXPERTS), (few_y_ready, 2 * GROUPS),
                                         (few_added, 4 * GROUPS)):
                        dve.sem_inc(semaphore, n)
                    counts[route.name] = R_STEPS * layer + R_RANK
                    experts_router(layer)
                    dve.wait_ge(gate_ready, 4 * (layer + 1))
                    dense_experts(layer)
                    dve.wait_ge(y_sum, Y_GROUP * GROUPS * (layer + 1))
                    dve.sem_inc(moe_done, 1)

            def dense_experts(layer):
                with dve.Fori(0, GROUPS) as g:
                    y_base = layer * Y_GROUP * GROUPS

                    def hidden(j):
                        e = layer * EXPERTS + j
                        dve.wait_ge(silu_done, g * PER_GROUP + e + 1)
                        dve.wait_ge(gu_full, g * 2 * PER_GROUP + 2 * e + 2)
                        dve.tensor_tensor(hid[:, j % 2, :], sg[:, j % 2, :], gu_bank[j % 2][1][:, :], ALU.mult)\
                           .then_inc(gu_free, 1)

                    def add_output(j):
                        e = layer * EXPERTS + j
                        for q in range(4):
                            t, half = divmod(q, 2)
                            cols = slice(half * 512, half * 512 + 512)
                            dve.wait_ge(y_full, g * 4 * PER_GROUP + 4 * e + q + 1)
                            dve.wait_ge(y_sum, g * Y_GROUP + y_base + (1 if j == 0 else 4 * j + q - 2))
                            dve.scalar_tensor_tensor(out=ytmp[:, q, :], in0=y_bank[q][:, :],
                                                     scalar=comb_g[:, t, j:j + 1], in1=gate_f[:, cols],
                                                     op0=ALU.mult, op1=ALU.mult).then_inc(y_free, 1)
                            dve.wait_ge(y_free, g * 4 * PER_GROUP + 4 * e + q + 5)
                            dve.tensor_tensor(x[:, t, cols], x[:, t, cols], ytmp[:, q, :], ALU.add).then_inc(y_sum, 1)

                    dve.tensor_copy(comb_g[:, :, :], comb[:, :, bass.ds(g * PER_GROUP, PER_GROUP)]).then_inc(y_sum, 1)
                    hidden(0)
                    for j in range(PER_GROUP):
                        if j + 1 < PER_GROUP:
                            hidden(j + 1)
                        add_output(j)

            dve.sem_inc(gu_free, 2)
            dve.sem_inc(y_free, 4)
            dve.sem_inc(few_added, 4)
            for n in range(PARTS):
                add_rows(n)
            normalise(0)
            for n in range(PARTS, 2 * PARTS):
                add_rows(n)
            dve.wait_ge(s_small, SMALL)
            dve.wait_ge(s_const, CONSTS)
            dve.wait_ge(s_route, ROUTE)
            column(0)
            column(1)
            modulate(0)
            for u in range(12):
                add_rows(2 * PARTS + u)
                if u in SUM_AFTER_QKV0 and not is_gate(SUM_AFTER_QKV0[u]):
                    column(SUM_AFTER_QKV0[u])
            for i in range(HEADS + 2):
                if i < HEADS:
                    mask_a(i)
                if 1 <= i <= HEADS:
                    softplus_a(i - 1)
                if i >= 2:
                    exponent_a(i - 2)
                if i < HEADS:
                    add_rows(20 + i)
                if i in SUM_AFTER_HEAD0 and not is_gate(SUM_AFTER_HEAD0[i]):
                    column(SUM_AFTER_HEAD0[i])
            column(8)
            dve.wait_ge(gate_ready, 2)
            for u in range(UNITS):
                residual(("o0", u))
                add_rows(36 + u)
            column(9)
            normalise(1)
            modulate(1)
            router(0)
            ranks(0)
            experts(0)

            normalise(2)
            modulate(2)
            for u in range(12):
                add_rows(40 + u)
                if u in SUM_AFTER_KVQ1 and not is_gate(SUM_AFTER_KVQ1[u]):
                    column(SUM_AFTER_KVQ1[u])
            for i in range(HEADS + 1):
                if i < HEADS:
                    bias_max_b(i)
                if i >= 1:
                    norm_b(i - 1)
                if i in (0, 3, 6, 9):
                    add_rows(52 + i // 3)
                if i in SUM_AFTER_HEAD1 and not is_gate(SUM_AFTER_HEAD1[i]):
                    column(SUM_AFTER_HEAD1[i])
            dve.wait_ge(gate_ready, 6)
            for u in range(UNITS):
                residual(("o1", u))
            normalise(3)
            modulate(3)
            router(1)
            ranks(1)
            experts(1)
            dve.wait_ge(s_gfin, 16)
            normalise(4, last=True)


_INS = ["x", "c", "w_ada", "b_ada", "g_attn", "g_ffn", "w_qkv_a", "w_o_a", "w_ada_kv", "b_ada_kv", "g_kv", "w_kv",
        "w_q_b", "w_o_b", "w_rg", "b_rg", "w_re", "b_re", "w_gate", "w_up", "w_down", "g_final"]


def kernel(**inputs):
    import numpy as np
    import concourse.bacc as bacc
    from concourse.bass_utils import run_bass_kernel_spmd

    nc = bacc.Bacc("TRN2", target_bir_lowering=False, num_devices=1)
    arrays, args = {}, []
    for name in _INS:
        a = np.ascontiguousarray(inputs[name])
        arrays[f"in_{name}"] = a
        args.append(nc.dram_tensor(f"in_{name}", a.shape, mybir.dt.from_np(a.dtype), kind="ExternalInput").ap())
    out = nc.dram_tensor("out_y", (1, T, D), F32, kind="ExternalOutput").ap()
    program(nc, *args, out)
    result = run_bass_kernel_spmd(nc, [arrays], core_ids=[0])
    return result.results[0]["out_y"]
```

```python
from contextlib import ExitStack

import concourse.bass as bass
from concourse import mybir

F32 = mybir.dt.float32
I32 = mybir.dt.int32
BF16 = mybir.dt.bfloat16
ALU = mybir.AluOpType
ACT = mybir.ActivationFunctionType
AX_X = mybir.AxisListType.X

P = 128
D = 1024
T = 256
TT = T // P
KC = D // P
HEADS = 16
HD = D // HEADS
PAIRS = HEADS // 2
GROUPS = 4
PER_GROUP = 4
EXPERTS = GROUPS * PER_GROUP
FF = 256
FC = FF // P
EPS = 1e-6
SCALE = HD ** -0.5
NEG = -1.0e30
CAUSAL = T + P
COLS = 256
UNITS = D // COLS
WSLOTS = 12
ASLOTS = 3
VECS = 14
PARTS = 4
LATE = range(6, 9)
ROWS = KC // PARTS
DEPTH = 2
CAP = 96

SHIFT_M, SCALE_M, GATE_M, SHIFT_F, SCALE_F, GATE_F = range(6)
KV_SHIFT, KV_SCALE = 6, 7


def vec(layer, which):
    return which if layer == 0 else 8 + which


def is_gate(v):
    return v in (vec(0, GATE_M), vec(0, GATE_F), vec(1, GATE_M), vec(1, GATE_F))


def is_scale(v):
    return v in (vec(0, SCALE_M), vec(0, SCALE_F), KV_SCALE, vec(1, SCALE_M), vec(1, SCALE_F))


GROUP_LOADS = [("gate", 0), ("up", 0), ("gate", 1), ("up", 1), ("down", 0), ("gate", 2), ("up", 2), ("down", 1),
               ("gate", 3), ("up", 3), ("down", 2), ("down", 3)]
assert len(GROUP_LOADS) == WSLOTS

QKV0 = [("qkv", b + UNITS * kind) for b in range(UNITS) for kind in range(3)]
O0 = [("o0", u) for u in range(4)]
KVQ1 = [("kvq", u) for u in range(12)]
O1 = [("o1", u) for u in range(4)]


def sum_items(v):
    return [("sum", v, 0), ("sum", v, 1)] if is_gate(v) else [("sum", v, 0)]


AHEAD = {0: 3, 1: 2 * UNITS + 1}
PIECES = {0: 3, 1: 1}
LAST = {0: HEADS + 2, 1: HEADS + 3}
PIECE_STEPS = 12
PROJ = {0: QKV0, 1: KVQ1}
for _l in range(2):
    assert AHEAD[_l] * 4 + PIECES[_l] * PIECE_STEPS == len(PROJ[_l]) * 4
O_CHUNKS = {0: {12: (0, 1), 13: (2, 3), 14: (4,), 16: (5,), 17: (6,)},
            1: {12: (0, 1), 13: (2,), 14: (3,), 15: (4,), 17: (5,), 18: (6,)}}
SUM_AFTER_UNIT = {0: {2: 2}, 1: {2: 10, 4: 11, 6: 12}}
SUM_IN_STEP = {0: {5: 3, 9: 4}, 1: {}}
ADA_AT_UNIT = {0: {0: [8], 1: [9, 10], 2: [11]}, 1: {u: [40 + 2 * u, 41 + 2 * u] for u in range(8)}}
ADA_IN_STEP = {0: {i: [12 + i] for i in range(12)}, 1: {}}


def piece_units(layer, step):
    if step >= PIECE_STEPS:
        return []
    at = range(PIECES[layer] * step, PIECES[layer] * (step + 1))
    return [(AHEAD[layer] + n // 4, n % 4) for n in at]


def units_done(layer, step):
    return [u for u, piece in piece_units(layer, step) if piece == 3]


def step_work(layer, step):
    pieces = piece_units(layer, step)
    vv = SUM_IN_STEP[layer].get(step)
    if vv is None:
        return pieces
    at = [piece for _, piece in pieces].index(3) + 1 if pieces else 0
    return pieces[:at] + [(None, vv)] + pieces[at:]


def out_items():
    items = sum_items(0) + sum_items(1)
    for layer, o in ((0, O0), (1, O1)):
        if layer == 1:
            items += sum_items(9)
        for u in range(AHEAD[layer]):
            items.append(PROJ[layer][u])
            if u in SUM_AFTER_UNIT[layer]:
                items += sum_items(SUM_AFTER_UNIT[layer][u])
        for i in range(LAST[layer]):
            for u, n in step_work(layer, i):
                if u is None:
                    items += sum_items(n)
                elif n == 0:
                    items.append(PROJ[layer][u])
        items += o + sum_items(vec(layer, GATE_F))
        items += [("route", layer), ("rank", layer)]
    return items


ITEMS = out_items()
OUT = {item: i for i, item in enumerate(ITEMS)}
VEC_ORDER = [vv for vv in range(VECS) if not is_gate(vv) and (vv not in LATE or is_scale(vv))]
GATE_ORDER = [vv for vv in range(VECS) if is_gate(vv)]
R_GROUP, R_EXP1, R_RANK, R_EXP2, R_STEPS = 6, 7, 18, 24, 34
N_STEPS = 6
F_STEPS = 3
Y_GROUP = 1 + 4 * PER_GROUP
O_STEPS = 2 * UNITS
assert sorted([v for k in OUT if k[0] == "sum" for v in [k[1]] if k[2] == 0] + list(LATE)) == list(range(VECS))

FIXED_LOADS = {0: QKV0 + O0, 1: KVQ1 + O1}
MOE_LOADS = GROUPS * WSLOTS
LOAD_BASE = {0: 0, 1: len(QKV0 + O0) + MOE_LOADS}
MOE_BASE = {l: LOAD_BASE[l] + len(FIXED_LOADS[l]) for l in range(DEPTH)}
LOAD = {}
for _l in range(DEPTH):
    for _i, _item in enumerate(FIXED_LOADS[_l]):
        LOAD[_item] = LOAD_BASE[_l] + _i


_W = [("w", n) for n in range(len(FIXED_LOADS[0]) + WSLOTS)]
_A = [("ada", n) for n in range(VECS * PARTS)]
EARLY = LATE[-1] * PARTS + PARTS


def layer0_stream():
    out = _A[:8] + _W[:2] + _A[8:9] + _W[2:3] + _A[9:11] + _W[3:4] + _A[11:12]
    w = 4
    for i in range(12):
        if i % 4 < 3:
            out.append(_W[w])
            w += 1
        out += _A[12 + i:13 + i]
    return out + _W[w:]


def late_stream(a, w):
    return a[0:2] + w[0:2] + a[2:3] + w[2:4] + a[3:4] + w[4:]


def layer1_stream():
    out = _A[EARLY:EARLY + 3] + _W[:2] + _A[EARLY + 3:EARLY + PARTS] + _W[2:WSLOTS]
    for n in range(4):
        out += _A[40 + 4 * n:44 + 4 * n] + _W[WSLOTS + n:WSLOTS + n + 1]
    return out + _W[WSLOTS + 4:]


STREAM = {0: layer0_stream(), 1: layer1_stream()}
for _l in range(DEPTH):
    assert [x for x in STREAM[_l] if x[0] == "w"] == _W
assert [x for _l in range(DEPTH) for x in STREAM[_l] if x[0] == "ada"] == _A[:LATE[0] * PARTS] + _A[EARLY:]


def ada_slot(n):
    return n % 2 if n // PARTS in LATE else n % ASLOTS


def ada_landings(n):
    return sum(ada_slot(m) == ada_slot(n) for m in range(n + 1))


def ada_before(n):
    return max([m for m in range(n) if ada_slot(m) == ada_slot(n)], default=None)


def program(nc, x_in, c_in, w_ada, b_ada, g_attn, g_ffn, w_qkv_a, w_o_a, w_ada_kv, b_ada_kv, g_kv, w_kv,
            w_q_b, w_o_b, w_rg, b_rg, w_re, b_re, w_gate, w_up, w_down, g_final, out):
    ctx = ExitStack()
    with ctx:
        def sb(name, shape, dt=F32):
            return ctx.enter_context(nc.sbuf_tensor(name, shape, dt))

        def sem(name):
            return ctx.enter_context(nc.semaphore(name))

        bank = [ctx.enter_context(nc.psum_tensor(f"bank{i}", [P, 512], F32)) for i in range(8)]
        out_bank = bank[0:2]
        av_bank = bank[2:4]
        za_bank = bank[4:8]
        z_bank = bank[4:6]
        s_bank = bank[6:8]
        turn_bank = bank[4:8]
        gu_bank = [bank[0:2], bank[6:8]]
        y_bank = bank[2:6]
        few_bank = bank[4:6]
        comb_bank = bank[0]
        place_bank = bank[1]
        late_bank = bank[4][:, 512 - KC:512]
        few_y_bank = bank[2:4]
        back_bank = [bank[6], bank[7], bank[2], bank[3]]

        wring = sb("wring", [P, WSLOTS, 2048])
        aring = sb("aring", [P, ASLOTS, ROWS, D])
        x = sb("x", [P, TT, D])
        xn = sb("xn", [P, TT, D])
        hT = sb("hT", [P, KC, T])
        qT = sb("qT", [P, PAIRS, T])
        kT = sb("kT", [P, PAIRS, T])
        v = sb("v", [P, TT, D])
        attnT = sb("attnT", [P, PAIRS, T])
        hkvT = attnT
        cT = sb("cT", [P, KC])
        acc = sb("acc", [P, 2, D])
        gate_bias = sb("gate_bias", [P, D])
        shift = sb("shift", [P, VECS, KC])
        gains = sb("gains", [P, VECS, KC])
        gate_m = sb("gate_m", [P, D])
        gate_f = sb("gate_f", [P, D])
        gfin = gate_m
        ident = sb("ident", [P, P])
        one = sb("one", [P, 1])
        negone = sb("negone", [P, 1])
        ones = one[:, :].broadcast_to([P, P])
        negones = negone[:, :].broadcast_to([P, P])
        negtri = sb("negtri", [P, P])
        mask = sb("mask", [P, P], BF16)
        identb = sb("identb", [P, P], BF16)
        distB = sb("distB", [P, CAUSAL])
        distI = kT[:, 0:2, :].rearrange("p a t -> p (a t)")[:, 0:CAUSAL].bitcast(I32)
        desc = sb("desc", [P, GROUPS])
        before = sb("before", [P, P])
        places = sb("places", [P, CAP])
        placesI = qT[:, 0, 0:CAP].bitcast(I32)
        xn_flat = xn[:, :, :].rearrange("p t n -> p (t n)")
        soft = xn_flat[:, 0:2 * CAUSAL].rearrange("p (i n) -> p i n", i=2)
        sp = xn_flat[:, D:D + 2 * CAUSAL].rearrange("p (i n) -> p i n", i=2)
        zb = xn_flat[:, 0:4 * CAUSAL].rearrange("p (i n) -> p i n", i=4)
        prob = sb("prob", [P, 2, CAUSAL])
        mx = sb("mx", [P, 2, TT])
        nmx = sb("nmx", [P, 2, TT])
        den = sb("den", [P, 2, TT])
        rden = sb("rden", [P, 2, TT])
        ss = sb("ss", [P, TT])
        ss4 = sb("ss4", [P, TT, UNITS])
        ms = sb("ms", [P, TT])
        rstd = sb("rstd", [P, TT])
        rtmp = sb("rtmp", [P, 3, TT])
        diag = sb("diag", [P, TT, P])
        otmp = v[:, :, :].rearrange("p t n -> p (t n)")[:, 0:4 * COLS].rearrange("p (i t n) -> p i t n", i=2, t=TT)
        w_r = sb("w_r", [P, DEPTH, KC, GROUPS + EXPERTS])
        b_r = sb("b_r", [P, DEPTH, GROUPS + EXPERTS])
        lg = sb("lg", [P, TT, GROUPS + EXPERTS])
        rt = sb("rt", [P, 12, TT, 4])
        r1 = sb("r1", [P, 12, TT])
        le_sel = sb("le_sel", [P, TT, EXPERTS])
        comb = sb("comb", [P, TT, EXPERTS])
        comb_g = sb("comb_g", [P, TT, PER_GROUP])
        where = sb("where", [P, 2, TT, GROUPS + 1])
        where_g = sb("where_g", [P, 2, TT])
        largest = sb("largest", [P, 2])
        largestI = sb("largestI", [P, 2], I32)
        q_flat = qT[:, :, :].rearrange("p c t -> p (c t)")
        sg = q_flat[:, 0:2 * FC * T].rearrange("p (i n) -> p i n", i=2)
        hid = q_flat[:, 2 * FC * T:4 * FC * T].rearrange("p (i n) -> p i n", i=2)
        ytmp = kT[:, :, :].rearrange("p c t -> p (c t)").rearrange("p (q n) -> p q n", q=4)
        few_sg = q_flat[:, 0:2 * FC * CAP].rearrange("p (i n) -> p i n", i=2)
        few_uc = q_flat[:, 512:512 + 2 * FC * CAP].rearrange("p (i n) -> p i n", i=2)
        few_hid = q_flat[:, D:D + 2 * FC * CAP].rearrange("p (i n) -> p i n", i=2)
        k_flat = kT[:, :, :].rearrange("p c t -> p (c t)")
        few_y = k_flat[0:CAP, 0:D]
        few_comb = k_flat[:, D:D + PER_GROUP * CAP]
        v_flat = v[:, :, :].rearrange("p t n -> p (t n)")
        onehot = v_flat[:, 0:TT * CAP].rearrange("p (t s) -> p t s", t=TT)
        onehotT = v_flat[0:CAP, D:D + T]
        few_hT = attnT[:, :, :].rearrange("p c t -> p (c t)")[:, 0:KC * CAP].rearrange("p (k s) -> p k s", k=KC)

        s_x = sem("s_x")
        s_c = sem("s_c")
        s_small = sem("s_small")
        s_route = sem("s_route")
        s_gfin = sem("s_gfin")
        s_const = sem("s_const")
        late_sum = sem("late_sum")
        late_ready = sem("late_ready")
        w_landed = [sem(f"w_landed{i}") for i in range(WSLOTS)]
        a_landed = [sem(f"a_landed{i}") for i in range(ASLOTS)]
        bias_added = sem("bias_added")
        ada_rows = sem("ada_rows")
        out_full = sem("out_full")
        scale_step = sem("scale_step")
        vec_ready = sem("vec_ready")
        gate_ready = sem("gate_ready")
        ss_ready = sem("ss_ready")
        ss_sum = sem("ss_sum")
        rsqrt_ready = sem("rsqrt_ready")
        nrm = sem("nrm")
        xn_ready = sem("xn_ready")
        turned = sem("turned")
        hT_dve = sem("hT_dve")
        hT_act = sem("hT_act")
        qkv_ready = sem("qkv_ready")
        z_full = sem("z_full")
        act_step = sem("act_step")
        soft_ready = sem("soft_ready")
        sp_ready = sem("sp_ready")
        s_full = sem("s_full")
        w_ready = sem("w_ready")
        av_full = sem("av_full")
        attn_ready = sem("attn_ready")
        b_max = sem("b_max")
        p_ready = sem("p_ready")
        b_norm = sem("b_norm")
        pT_ready = sem("pT_ready")
        o_step = sem("o_step")
        route = sem("route")
        route_exp = sem("route_exp")
        gu_full = sem("gu_full")
        silu_done = sem("silu_done")
        gu_free = sem("gu_free")
        y_full = sem("y_full")
        y_free = sem("y_free")
        y_sum = sem("y_sum")
        largest_ready = sem("largest_ready")
        placed = sem("placed")
        few_full = sem("few_full")
        few_hT_dve = sem("few_hT_dve")
        few_hT_act = sem("few_hT_act")
        few_comb_ready = sem("few_comb_ready")
        few_turned = sem("few_turned")
        few_turn_ready = sem("few_turn_ready")
        few_up = sem("few_up")
        few_y_ready = sem("few_y_ready")
        few_back = sem("few_back")
        few_added = sem("few_added")
        comb_ready = sem("comb_ready")
        moe_done = sem("moe_done")
        s_out = sem("s_out")

        wslot = [wring[:, i, :] for i in range(WSLOTS)]

        def w_cols(slot):
            return wslot[slot].rearrange("p (k n) -> p k n", k=KC)

        def w_rows(slot):
            return wslot[slot].rearrange("p (k n) -> p k n", k=FC)

        def wait_weights(eng, load, extra=0):
            eng.wait_ge(w_landed[load % WSLOTS], (extra + load // WSLOTS + 1) * 16)

        def wait_out_read(eng, i):
            kind, n = ITEMS[i][0:2]
            if kind in ("qkv", "kvq"):
                layer = int(kind == "kvq")
                eng.wait_ge(qkv_ready, 12 * layer + PROJ[layer].index(ITEMS[i]) + 1)
            elif kind in ("o0", "o1"):
                eng.wait_ge(o_step, 2 * (n + UNITS * (kind == "o1")) + 1)
            elif kind == "route":
                eng.wait_ge(route, R_STEPS * n + 1)
            elif kind == "rank":
                eng.wait_ge(route, R_STEPS * n + R_RANK)
            elif is_gate(n):
                eng.wait_ge(gate_ready, 2 * GATE_ORDER.index(n) + ITEMS[i][2] + 1)
            else:
                eng.wait_ge(vec_ready, VEC_ORDER.index(n) + 1)

        def wait_out_free(pe, i):
            if i >= 2:
                wait_out_read(pe, i - 2)

        def pk(w):
            return w.rearrange("(p k) n -> p k n", k=KC)

        def cp(w):
            return w.rearrange("(c p) n -> p c n", p=P)

        def unit_source(item):
            kind, u = item
            cols = slice(u * COLS, (u + 1) * COLS)
            if kind == "qkv":
                return pk(w_qkv_a[0])[:, :, cols]
            if kind == "o0":
                return cp(w_o_a[0])[:, :, cols]
            if kind == "kvq" and u < 2 * UNITS:
                return pk(w_kv)[:, :, cols]
            if kind == "kvq":
                cols = slice((u - 2 * UNITS) * COLS, (u - 2 * UNITS + 1) * COLS)
                return pk(w_q_b[0])[:, :, cols]
            return cp(w_o_b[0])[:, :, cols]

        def ada_source(n):
            vv, part = n // PARTS, n % PARTS
            if vv in (KV_SHIFT, KV_SCALE):
                return ada_part(w_ada_kv, vv - KV_SHIFT, part)
            l, j = (0, vv) if vv < 6 else (1, vv - 8)
            return ada_part(w_ada[l], j, part)

        def ada_part(w, j, part):
            return pk(w)[:, part * ROWS:(part + 1) * ROWS, bass.ds(j * D, D)]

        HT_COUNT = {0: 4, 1: 8, 2: 16, 3: 20}

        def modulated(norm):
            if norm == 2:
                return [(hkvT, KV_SHIFT, KV_SCALE), (hT, vec(1, SHIFT_M), vec(1, SCALE_M))]
            return [(hT, *{0: (vec(0, SHIFT_M), vec(0, SCALE_M)), 1: (vec(0, SHIFT_F), vec(0, SCALE_F)),
                           3: (vec(1, SHIFT_F), vec(1, SCALE_F))}[norm])]

        CONSTS = 23
        SMALL = 16 * (3 + len(GATE_ORDER) + 5)
        ROUTE = 16 * 4 * DEPTH

        block = ctx.enter_context(nc.Block())

        @block.sync
        def _(sp_eng):
            sp_eng.dma_start(cT[:, :], c_in[0].rearrange("(p k) -> p k", k=KC)).then_inc(s_c, 16)
            for t in range(TT):
                sp_eng.dma_start(x[:, t, :], x_in[0, t * P:(t + 1) * P, :]).then_inc(s_x, 16)

            def released(load):
                for item, i in LOAD.items():
                    if i == load:
                        sp_eng.wait_ge(out_full, OUT[item] + 1)
                        return
                layer = 0 if load < LOAD_BASE[1] else 1
                g, j = divmod(load - MOE_BASE[layer], WSLOTS)
                moe_released(layer, j, g)

            def moe_released(layer, j, g):
                kind, e = GROUP_LOADS[j]
                if kind == "down":
                    sp_eng.wait_ge(y_full, g * 4 * PER_GROUP + (layer * EXPERTS + e) * 4 + 4)
                else:
                    sp_eng.wait_ge(gu_full, g * 2 * PER_GROUP + (layer * EXPERTS + e) * 2 + 1 + (kind == "up"))

            def expert_load(layer, j, g):
                kind, e = GROUP_LOADS[j]
                load = MOE_BASE[layer] + j
                src = {"gate": w_gate, "up": w_up, "down": w_down}[kind]
                one = src[layer, bass.ds(g * PER_GROUP + e, 1)].rearrange("o r n -> (o r) n")
                slot = load % WSLOTS
                if kind == "down":
                    sp_eng.dma_start(w_rows(slot), cp(one)).then_inc(w_landed[slot], 16)
                else:
                    sp_eng.dma_start(w_cols(slot), pk(one)).then_inc(w_landed[slot], 16)

            def load_ada(n):
                before_it = ada_before(n)
                if before_it is not None:
                    sp_eng.wait_ge(ada_rows, ROWS * (before_it + 1))
                sp_eng.dma_start(aring[:, ada_slot(n), :, :], ada_source(n)).then_inc(a_landed[ada_slot(n)], 16)

            def load_late(w, j, part, g):
                n = LATE[0] * PARTS + part
                sp_eng.wait_ge(ada_rows, g * KC + ROWS * (n - 1))
                sp_eng.dma_start(aring[:, ada_slot(n), :, :], ada_part(w, j, part)).then_inc(a_landed[ada_slot(n)], 16)

            group_items = _W[:WSLOTS]
            late_items = (_A[:PARTS], group_items)

            def group_loads(layer, g, late):
                for kind, n in late_stream(*late_items) if late else group_items:
                    if kind == "ada":
                        load_late(*late, n, g - 1)
                    else:
                        moe_released(layer, n, g - 1)
                        expert_load(layer, n, g)

            def load_weights(layer, n):
                load = LOAD_BASE[layer] + n
                if load >= WSLOTS:
                    released(load - WSLOTS)
                if n < len(FIXED_LOADS[layer]):
                    item = FIXED_LOADS[layer][n]
                    sp_eng.dma_start(w_cols(load % WSLOTS), unit_source(item)).then_inc(w_landed[load % WSLOTS], 16)
                else:
                    expert_load(layer, n - len(FIXED_LOADS[layer]), 0)

            for layer in range(DEPTH):
                for kind, n in STREAM[layer]:
                    if kind == "ada":
                        load_ada(n)
                    else:
                        load_weights(layer, n)
                if layer == 0:
                    with sp_eng.Fori(1, 3) as g:
                        group_loads(layer, g, (w_ada_kv, g - 1))
                    group_loads(layer, 3, (w_ada[1], 0))
                else:
                    with sp_eng.Fori(1, GROUPS) as g:
                        group_loads(layer, g, None)

            for t in range(TT):
                sp_eng.wait_ge(o_step, DEPTH * O_STEPS + t + 1)
                sp_eng.dma_start(out[0, t * P:(t + 1) * P, :], xn[:, t, :]).then_inc(s_out, 16)
            sp_eng.wait_ge(s_out, 16 * TT)

        @block.gpsimd
        def _(pool):
            pool.memset(ident[:, :], 0.0).then_inc(s_const, 1)
            pool.memset(one[:, :], 1.0).then_inc(s_const, 1)
            pool.memset(negone[:, :], -1.0).then_inc(s_const, 1)
            pool.memset(negtri[:, :], -1.0).then_inc(s_const, 1)
            pool.memset(mask[:, :], 0.0).then_inc(s_const, 1)
            for j in range(GROUPS):
                pool.memset(desc[:, j:j + 1], float(GROUPS - j)).then_inc(s_const, 1)
            pool.iota(distI[:, 0:P], pattern=[[1, P]], base=0, channel_multiplier=-1).then_inc(s_const, 1)
            pool.iota(distI[:, P:], pattern=[[1, T]], base=-P, channel_multiplier=-1).then_inc(s_const, 1)
            pool.iota(placesI, pattern=[[1, CAP]], base=0, channel_multiplier=0).then_inc(s_const, 1)
            pool.memset(before[:, :], 1.0).then_inc(s_const, 1)
            pool.memset(where[:, :, :, :], 0.0).then_inc(s_const, 1)
            pool.wait_ge(s_const, 14)
            pool.affine_select(out=ident[:, :], in_=ident[:, :], compare_op=ALU.not_equal, fill=1.0, base=0,
                               pattern=[[-1, P]], channel_multiplier=1).then_inc(s_const, 1)
            pool.affine_select(out=negtri[:, :], in_=negtri[:, :], compare_op=ALU.is_ge, fill=0.0, base=0,
                               pattern=[[-1, P]], channel_multiplier=1).then_inc(s_const, 1)
            pool.affine_select(out=mask[:, :], in_=mask[:, :], compare_op=ALU.is_ge, fill=NEG, base=-1,
                               pattern=[[1, P]], channel_multiplier=-1).then_inc(s_const, 1)
            pool.tensor_copy(distB[:, :], distI[:, :]).then_inc(s_const, 1)
            pool.tensor_copy(places[:, :], placesI).then_inc(s_const, 1)
            pool.affine_select(out=before[:, :], in_=before[:, :], compare_op=ALU.is_ge, fill=0.0, base=-1,
                               pattern=[[1, P]], channel_multiplier=-1).then_inc(s_const, 1)
            pool.wait_ge(s_const, 20)
            pool.tensor_copy(identb[:, :], ident[:, :]).then_inc(s_const, 1)
            for lo, n, off in ((0, P, 0), (P, T, P)):
                pool.affine_select(out=distB[:, lo:lo + n], in_=distB[:, lo:lo + n], compare_op=ALU.is_ge, fill=NEG,
                                   base=off, pattern=[[-1, n]], channel_multiplier=1).then_inc(s_const, 1)
            pool.wait_ge(o_step, DEPTH * O_STEPS)
            pool.dma_start(gfin[:, :], g_final.rearrange("(o n) -> o n", o=1).broadcast_to([P, D])).then_inc(s_gfin, 16)

        @block.tensor
        def _(pe):
            mm = pe.matmul

            def sum_vector(vv):
                pe.wait_ge(ada_rows, KC * (vv + 1))
                rows = acc[:, vv % 2, :]
                if not is_gate(vv):
                    i = OUT[("sum", vv, 0)]
                    wait_out_free(pe, i)
                    b = out_bank[i % 2]
                    by_chunk = rows.rearrange("p (q k) -> p k q", k=KC)
                    for k in range(KC):
                        last = mm(b[:, k:k + 1], by_chunk[:, k, :], one[:, 0:1], start=True, stop=True)
                    last.then_inc(out_full, 1)
                    return
                pe.wait_ge(bias_added, GATE_ORDER.index(vv) + 1)
                for half in range(2):
                    i = OUT[("sum", vv, half)]
                    wait_out_free(pe, i)
                    cols = slice(half * 512, half * 512 + 512)
                    mm(out_bank[i % 2][:, :], ones, rows[:, cols], start=True, stop=True).then_inc(out_full, 1)

            def sum_late(g):
                pe.wait_ge(ada_rows, g * KC + KC * (LATE[0] + 1))
                pe.wait_ge(late_ready, g + 1)
                by_chunk = acc[:, 0, :].rearrange("p (q k) -> p k q", k=KC)
                for k in range(KC):
                    last = mm(late_bank[:, k:k + 1], by_chunk[:, k, :], one[:, 0:1], start=True, stop=True)
                last.then_inc(late_sum, 1)

            def turn(norm):
                by_chunk = x[:, :, :].rearrange("p t (q k) -> p t k q", k=KC)
                for j in range(4):
                    for a in range(2):
                        for t in range(TT):
                            pe.wait_ge(nrm, N_STEPS * norm + 5 + t)
                            col = a * T + t * P
                            last = mm(turn_bank[j][:, col:col + P], by_chunk[:, t, 2 * j + a, :], diag[:, t, :],
                                      start=True, stop=True)
                    last.then_inc(turned, 1)

            def project(item, src, by_feature, pieces, norm=None):
                i, load = OUT[item], LOAD[item]
                if 0 in pieces:
                    wait_out_free(pe, i)
                    wait_weights(pe, load)
                w = w_cols(load % WSLOTS)
                for piece in pieces:
                    half = piece // 2
                    dst = out_bank[i % 2][:, half * COLS:(half + 1) * COLS]
                    for k in range(KC // 2 * (piece % 2), KC // 2 * (piece % 2 + 1)):
                        if norm is not None and piece < 2:
                            wait_chunk(norm, k)
                        if by_feature:
                            last = mm(dst, w[:, k, half * P:(half + 1) * P], src[:, k, :],
                                      start=(k == 0), stop=(k == KC - 1))
                        else:
                            last = mm(dst, src[:, k, half * P:(half + 1) * P], w[:, k, :],
                                      start=(k == 0), stop=(k == KC - 1))
                if 3 in pieces:
                    last.then_inc(out_full, 1)

            def begin_output(layer, chunks):
                for u in range(2):
                    item = (f"o{layer}", u)
                    i, load = OUT[item], LOAD[item]
                    if 0 in chunks:
                        wait_out_free(pe, i)
                        wait_weights(pe, load)
                    for c in chunks:
                        pe.wait_ge(attn_ready, PAIRS * layer + c + 1)
                        mm(out_bank[i % 2][:, 0:COLS], attnT[:, c, 0:P], w_cols(load % WSLOTS)[:, c, :],
                           start=(c == 0), stop=(c == PAIRS - 1))

            def project_output(layer):
                begin_output(layer, (PAIRS - 1,))
                for u in range(2):
                    project((f"o{layer}", u), attnT, False, (2, 3))
                for u in range(2, UNITS):
                    project((f"o{layer}", u), attnT, False, range(4))

            def project_qkv(layer, u, pieces):
                item = PROJ[layer][u]
                norm = 2 * layer if u == 0 else None
                if layer == 0:
                    project(item, hT, item[1] < 2 * UNITS, pieces, norm)
                else:
                    if u == 2 * UNITS:
                        wait_hT(2)
                    project(item, hkvT if item[1] < 2 * UNITS else hT, item[1] // UNITS != 1, pieces, norm)

            def wait_qkv(layer, h):
                if h % 4 == 0:
                    pe.wait_ge(qkv_ready, 3 * (h // 4 + 1) if layer == 0 else 12 + 2 * UNITS + h // 4 + 1)

            def head_rows(h):
                return slice(HD * (h % 2), HD * (h % 2) + HD), h // 2

            def scores_a(h):
                wait_qkv(0, h)
                if h >= 4:
                    pe.wait_ge(w_ready, h - 3)
                r, c = head_rows(h)
                z = za_bank[h % 4]
                mm(z[:, 0:T], kT[r, c, 0:P], qT[r, c, :], start=True, stop=False, skip_group_check=True)
                mm(z[:, T:CAUSAL], kT[r, c, P:T], qT[r, c, P:T], start=False, stop=False, skip_group_check=True)
                mm(z[:, 0:P], identb[:, :], mask[:, :], start=False, stop=False, skip_group_check=True)
                mm(z[:, T:CAUSAL], identb[:, :], mask[:, :], start=False, stop=True, skip_group_check=True)\
                    .then_inc(z_full, 1)

            def suffix_a(h):
                pe.wait_ge(sp_ready, h + 1)
                z, w = za_bank[h % 4], sp[:, h % 2, :]
                mm(z[:, 0:T], negtri[:, :], w[:, 0:T], start=False, stop=False, skip_group_check=True)
                mm(z[:, P:T], negones, w[:, T:CAUSAL], start=False, stop=False, skip_group_check=True)
                mm(z[:, T:CAUSAL], negtri[:, :], w[:, T:CAUSAL], start=False, stop=True, skip_group_check=True)\
                    .then_inc(s_full, 1)

            def values(h, ready, count, layer):
                pe.wait_ge(ready, count)
                r, c = head_rows(h)
                if h % 2 == 0 and c + layer * PAIRS >= 2:
                    pe.wait_ge(attn_ready, c + layer * PAIRS - 1)
                o, w = av_bank[c % 2], prob[:, h % 2, :]
                vh = v[:, :, h * HD:(h + 1) * HD]
                mm(o[r, 0:P], vh[:, 0, :], w[:, 0:P], start=True, stop=True)
                mm(o[r, P:T], vh[:, 0, :], w[:, P:T], start=True, stop=False)
                mm(o[r, P:T], vh[:, 1, :], w[:, T:CAUSAL], start=False, stop=True).then_inc(av_full, 1)

            def scores_b(h):
                wait_qkv(1, h)
                if h >= 2:
                    pe.wait_ge(b_max, 3 * (h - 2) + 1)
                r, c = head_rows(h)
                z = z_bank[h % 2]
                mm(z[:, 0:P], qT[r, c, 0:P], kT[r, c, 0:P], start=True, stop=True)
                mm(z[:, P:CAUSAL], qT[r, c, P:T], kT[r, c, :], start=True, stop=True).then_inc(z_full, 1)

            def turn_b(h):
                pe.wait_ge(b_norm, 3 * h + 3)
                if h >= 2:
                    pe.wait_ge(pT_ready, h - 1)
                s, p = s_bank[h % 2], zb[:, h % 4, :]
                pe.transpose(s[:, 0:P], p[:, 0:P], ident[:, :])
                pe.transpose(s[:, P:T], p[:, P:T], ident[:, :])
                pe.transpose(s[:, T:CAUSAL], p[:, T:CAUSAL], ident[:, :]).then_inc(s_full, 1)

            def router(layer):
                i = OUT[("route", layer)]
                wait_out_free(pe, i)
                for t in range(TT):
                    for k in range(KC):
                        if t == 0:
                            wait_chunk(2 * layer + 1, k)
                        last = mm(out_bank[i % 2][:, t * 32:t * 32 + GROUPS + EXPERTS], hT[:, k, t * P:(t + 1) * P],
                                  w_r[:, layer, k, :], start=(k == 0), stop=(k == KC - 1))
                last.then_inc(out_full, 1)

            def gate_up(layer, j, g):
                e = layer * EXPERTS + j
                pe.wait_ge(gu_free, g * PER_GROUP + e + 1)
                for n, kind in enumerate(("gate", "up")):
                    load = MOE_BASE[layer] + GROUP_LOADS.index((kind, j))
                    wait_weights(pe, load, g)
                    w = w_cols(load % WSLOTS)
                    b = gu_bank[j % 2][n]
                    for f in range(FC):
                        for k in range(KC):
                            last = mm(b[:, f * T:(f + 1) * T], w[:, k, f * P:(f + 1) * P], hT[:, k, :],
                                      start=(k == 0), stop=(k == KC - 1))
                    last.then_inc(gu_full, 1)

            def down(layer, j, g):
                e = layer * EXPERTS + j
                load = MOE_BASE[layer] + GROUP_LOADS.index(("down", j))
                wait_weights(pe, load, g)
                pe.wait_ge(gu_free, g * PER_GROUP + e + 3)
                w = w_rows(load % WSLOTS)
                hT_e = hid[:, j % 2, :].rearrange("p (f t) -> p f t", f=FC)
                for q in range(4):
                    t, half = divmod(q, 2)
                    pe.wait_ge(y_free, g * 4 * PER_GROUP + 4 * e + q + 1)
                    for f in range(FC):
                        last = mm(y_bank[q][:, :], hT_e[:, f, t * P:(t + 1) * P], w[:, f, half * 512:half * 512 + 512],
                                  start=(f == 0), stop=(f == FC - 1))
                    last.then_inc(y_full, 1)

            def rank(layer):
                i = OUT[("rank", layer)]
                wait_out_free(pe, i)
                pe.wait_ge(route, R_STEPS * layer + R_GROUP)
                b = out_bank[i % 2]
                n = GROUPS
                member = [rt[:, 0, t, :] for t in range(TT)]
                mm(b[:, 0:n], before[:, :], member[0], start=True, stop=True)
                mm(b[:, n:2 * n], ones, member[0], start=True, stop=False)
                mm(b[:, n:2 * n], before[:, :], member[1], start=False, stop=True)
                mm(b[:, 2 * n:3 * n], ones, member[0], start=True, stop=False)
                mm(b[:, 2 * n:3 * n], ones, member[1], start=False, stop=True).then_inc(out_full, 1)

            def dense_experts(layer):
                with pe.Fori(0, GROUPS - 1) as g:
                    dense_group(layer, g, False)
                dense_group(layer, GROUPS - 1, True)

            def dense_group(layer, g, last):
                gate_up(layer, 0, g)
                for j in range(PER_GROUP):
                    if j + 1 < PER_GROUP:
                        gate_up(layer, j + 1, g)
                    down(layer, j, g)
                if layer == 0 and not last:
                    pe.wait_ge(y_free, g * 4 * PER_GROUP + 4 * PER_GROUP + 4)
                    sum_late(g)
                    pe.wait_ge(late_ready, g + 2)

            def gather(layer, g):
                n = layer * GROUPS
                pe.wait_ge(placed, g * F_STEPS + F_STEPS * (n + 1))
                if layer == 0 and not (isinstance(g, int) and g == 0):
                    pe.wait_ge(late_ready, g)
                by_chunk = xn[:, :, :].rearrange("p t (q k) -> p t k q", k=KC)
                for half in range(2):
                    for a in range(KC // 2):
                        for t in range(TT):
                            last = mm(few_bank[half][:, a * CAP:(a + 1) * CAP], by_chunk[:, t, half * KC // 2 + a, :],
                                      onehot[:, t, :], start=(t == 0), stop=(t == TT - 1))
                    last.then_inc(few_full, 1)

            def gather_comb(layer, g):
                n = layer * GROUPS
                pe.wait_ge(comb_ready, g + n + 1)
                for j in range(PER_GROUP):
                    for t in range(TT):
                        last = mm(comb_bank[:, j * CAP:(j + 1) * CAP], comb_g[:, t, j:j + 1].broadcast_to([P, P]),
                                  onehot[:, t, :], start=(t == 0), stop=(t == TT - 1))
                last.then_inc(few_full, 1)

            def turn_places(layer, g):
                for t in range(TT):
                    last = pe.transpose(place_bank[0:CAP, t * P:(t + 1) * P], onehot[:, t, :], ident[:, :])
                last.then_inc(few_turned, 1)

            def few_gate_up(layer, j, g):
                e = layer * EXPERTS + j
                n = layer * GROUPS
                pe.wait_ge(gu_free, g * PER_GROUP + e + 1)
                if j == 0:
                    pe.wait_ge(few_hT_dve, g * (KC // 2) + (n + 1) * (KC // 2))
                    pe.wait_ge(few_hT_act, g * (KC // 2) + (n + 1) * (KC // 2))
                    pe.wait_ge(few_comb_ready, g + n + 1)
                    pe.wait_ge(few_turn_ready, g + n + 1)
                if j == 1:
                    pe.wait_ge(few_added, g * 4 + 4 * n + 2)
                for m, kind in enumerate(("gate", "up")):
                    load = MOE_BASE[layer] + GROUP_LOADS.index((kind, j))
                    wait_weights(pe, load, g)
                    w = w_cols(load % WSLOTS)
                    b = gu_bank[j % 2][m]
                    for f in range(FC):
                        for k in range(KC):
                            last = mm(b[:, f * CAP:(f + 1) * CAP], w[:, k, f * P:(f + 1) * P], few_hT[:, k, :],
                                      start=(k == 0), stop=(k == KC - 1))
                    last.then_inc(gu_full, 1)

            def few_down(layer, j, g):
                e = layer * EXPERTS + j
                load = MOE_BASE[layer] + GROUP_LOADS.index(("down", j))
                wait_weights(pe, load, g)
                pe.wait_ge(gu_free, g * PER_GROUP + e + 3)
                if j == 0:
                    pe.wait_ge(few_added, g * 4 + 4 * layer * GROUPS + 4)
                w = w_rows(load % WSLOTS)
                hT_e = few_hid[:, j % 2, :].rearrange("p (f s) -> p f s", f=FC)
                for half in range(2):
                    for f in range(FC):
                        mm(few_y_bank[half][0:CAP, :], hT_e[:, f, :], w[:, f, half * 512:half * 512 + 512],
                           start=(j == 0 and f == 0), stop=(j == PER_GROUP - 1 and f == FC - 1)).then_inc(y_full, 1)

            def scatter(layer, g):
                n = layer * GROUPS
                for q in range(4):
                    t, half = divmod(q, 2)
                    pe.wait_ge(few_y_ready, g * 2 + 2 * n + (half + 1 if q < 2 else 2))
                    mm(back_bank[q][:, :], onehotT[:, t * P:(t + 1) * P], few_y[:, half * 512:half * 512 + 512],
                       start=True, stop=True).then_inc(few_back, 1)

            def few_group(layer, g, last):
                few_gate_up(layer, 0, g)
                for j in range(PER_GROUP):
                    if j + 1 < PER_GROUP:
                        few_gate_up(layer, j + 1, g)
                    if j == PER_GROUP - 1 and not last:
                        gather(layer, g + 1)
                    few_down(layer, j, g)
                if not last:
                    gather_comb(layer, g + 1)
                scatter(layer, g)
                if layer == 0 and not last:
                    sum_late(g)
                if not last:
                    turn_places(layer, g + 1)

            def routed_experts(layer):
                gather_comb(layer, 0)
                turn_places(layer, 0)
                with pe.Fori(0, GROUPS - 1) as g:
                    few_group(layer, g, False)
                few_group(layer, GROUPS - 1, True)

            def experts(layer):
                pe.wait_ge(xn_ready, TT * (layer + 1))
                gather(layer, 0)
                pe.wait_ge(largest_ready, 2 * (layer + 1))
                size = pe.value_load(largestI[0:1, layer:layer + 1], min_val=0, max_val=T)
                wait_out_read(pe, OUT[("route", layer)])
                wait_out_read(pe, OUT[("rank", layer)])
                with pe.If(size <= CAP):
                    routed_experts(layer)
                with pe.Else():
                    pe.sem_inc(few_full, 3 * GROUPS - 2)
                    pe.sem_inc(few_turned, GROUPS)
                    pe.sem_inc(few_back, 4 * GROUPS)
                    dense_experts(layer)

            def wait_chunk(norm, k):
                done = HT_COUNT[norm] - 4 * len(modulated(norm)) + 2 * (k // 4) + k % 2 + 1
                pe.wait_ge(hT_act if k % 4 >= 2 else hT_dve, done)

            def wait_hT(norm):
                pe.wait_ge(hT_dve, HT_COUNT[norm])
                pe.wait_ge(hT_act, HT_COUNT[norm])

            def attention(layer):
                for u in range(AHEAD[layer]):
                    project_qkv(layer, u, range(4))
                    if u in SUM_AFTER_UNIT[layer]:
                        sum_vector(SUM_AFTER_UNIT[layer][u])
                for i in range(LAST[layer]):
                    for u, n in step_work(layer, i):
                        if u is None:
                            sum_vector(n)
                        else:
                            project_qkv(layer, u, [n])
                    if layer == 0:
                        if i < HEADS:
                            scores_a(i)
                        if 1 <= i <= HEADS:
                            suffix_a(i - 1)
                        if i >= 2:
                            values(i - 2, w_ready, i - 1, 0)
                    else:
                        if i < HEADS:
                            scores_b(i)
                        if 2 <= i < HEADS + 2:
                            turn_b(i - 2)
                        if i >= 3:
                            values(i - 3, pT_ready, i - 2, 1)
                    if i in O_CHUNKS[layer]:
                        begin_output(layer, O_CHUNKS[layer][i])

            pe.sem_inc(late_sum, 1)
            pe.wait_ge(s_const, CONSTS)
            pe.wait_ge(s_small, SMALL)
            sum_vector(0)
            turn(0)
            sum_vector(1)
            attention(0)
            project_output(0)
            sum_vector(vec(0, GATE_F))
            turn(1)
            pe.wait_ge(s_route, ROUTE)
            router(0)
            rank(0)
            experts(0)

            sum_vector(9)
            turn(2)
            attention(1)
            project_output(1)
            sum_vector(vec(1, GATE_F))
            turn(3)
            router(1)
            rank(1)
            experts(1)

        @block.scalar
        def _(act):
            steps = [0]

            def own(ins):
                ins.then_inc(act_step, 1)
                steps[0] += 1
                act.wait_ge(act_step, steps[0])

            def squares(norm):
                if norm in (1, 3):
                    for u in range(UNITS):
                        cols = slice(u * COLS, (u + 1) * COLS)
                        act.wait_ge(o_step, 2 * (UNITS * (norm // 2) + u + 1))
                        for t in range(TT):
                            act.activation(xn[:, t, cols], x[:, t, cols], ACT.Square,
                                           accum_out=ss4[:, t, u:u + 1]).then_inc(ss_ready, 1)
                    return
                for t in range(TT):
                    if norm == 0:
                        act.wait_ge(s_x, 16 * TT)
                    else:
                        act.wait_ge(moe_done, TT * (norm // 2 - 1) + t + 1)
                    act.activation(xn[:, t, :], x[:, t, :], ACT.Square, accum_out=ss[:, t:t + 1]).then_inc(ss_ready, 1)

            def rsqrt(norm):
                act.wait_ge(nrm, N_STEPS * norm + 1)
                act.activation(rtmp[:, 0, :], ms[:, :], ACT.Ln).then_inc(rsqrt_ready, 1)
                act.wait_ge(rsqrt_ready, 2 * norm + 1)
                act.activation(rtmp[:, 0, :], rtmp[:, 0, :], ACT.Exp, scale=-0.5).then_inc(rsqrt_ready, 1)

            def modulate(norm, stream=0):
                dst, sh, a = modulated(norm)[stream]
                act.wait_ge(vec_ready, 1 + VEC_ORDER.index(a))
                for j in (1, 3):
                    act.wait_ge(turned, 4 * norm + j + 1)
                    for n in range(2):
                        k = 2 * j + n
                        act.activation(dst[:, k, :], turn_bank[j][:, n * T:(n + 1) * T], ACT.Identity,
                                       bias=shift[:, sh, k:k + 1], scale=shift[:, a, k:k + 1]).then_inc(hT_act, 1)

            def take(layer, u):
                item = PROJ[layer][u]
                kind, b = divmod(item[1], UNITS)
                what = ("qkv" if layer == 0 else "kvq")[kind]
                i = OUT[item]
                if what == "v":
                    dst = v[:, :, b * COLS:(b + 1) * COLS]
                else:
                    dst = (qT if what == "q" else kT)[:, 2 * b:2 * b + 2, :]
                act.wait_ge(out_full, i + 1)
                act.activation(dst, out_bank[i % 2][:, :].rearrange("p (a n) -> p a n", a=2), ACT.Copy,
                               scale=SCALE if layer == 0 and what == "q" else 1.0).then_inc(qkv_ready, 1)

            def gate(vv, dst):
                for half in range(2):
                    i = OUT[("sum", vv, half)]
                    act.wait_ge(out_full, i + 1)
                    act.activation(dst[:, half * 512:half * 512 + 512], out_bank[i % 2][:, :], ACT.Copy, bias=1.0)\
                       .then_inc(gate_ready, 1)

            def attn_out(c, layer):
                act.wait_ge(av_full, 2 * (c + 1) + layer * HEADS)
                act.activation(attnT[:, c, :], av_bank[c % 2][:, 0:T], ACT.Copy).then_inc(attn_ready, 1)

            def soft_a(h):
                act.wait_ge(z_full, h + 1)
                if h >= 2:
                    act.wait_ge(sp_ready, h - 1)
                s = soft[:, h % 2, :]
                own(act.activation(s, za_bank[h % 4][:, 0:CAUSAL], ACT.Abs))
                own(act.activation(s, s, ACT.Exp, scale=-1.0))
                act.activation(s, s, ACT.Ln, bias=1.0).then_inc(soft_ready, 1)

            def weights_a(h):
                act.wait_ge(s_full, h + 1)
                if h >= 2:
                    act.wait_ge(av_full, h - 1)
                act.activation(prob[:, h % 2, :], za_bank[h % 4][:, 0:CAUSAL], ACT.Exp).then_inc(w_ready, 1)

            def exps_b(h):
                act.wait_ge(b_max, 3 * h + 3)
                for t, cols in ((0, slice(0, P)), (1, slice(P, CAUSAL))):
                    act.activation(zb[:, h % 4, cols], zb[:, h % 4, cols], ACT.Exp, scale=SCALE,
                                   bias=nmx[:, h % 2, t:t + 1], accum_out=den[:, h % 2, t:t + 1]).then_inc(p_ready, 1)

            def probs_b(h):
                act.wait_ge(s_full, HEADS + h + 1)
                if h >= 2:
                    act.wait_ge(av_full, HEADS + h - 1)
                act.activation(prob[:, h % 2, :], s_bank[h % 2][:, 0:CAUSAL], ACT.Copy).then_inc(pT_ready, 1)

            def router(layer):
                act.wait_ge(route, R_STEPS * layer + R_EXP1)
                act.activation(rt[:, 4, :, :], rt[:, 4, :, :], ACT.Exp).then_inc(route_exp, 1)
                act.wait_ge(route, R_STEPS * layer + R_EXP2)
                act.activation(r1[:, 6, :], r1[:, 6, :], ACT.Exp).then_inc(route_exp, 1)

            def few_modulate(layer, g):
                act.wait_ge(few_full, g * 3 + 3 * layer * GROUPS + 2)
                for a in range(KC // 2):
                    k = KC // 2 + a
                    act.activation(few_hT[:, k, :], few_bank[1][:, a * CAP:(a + 1) * CAP], ACT.Identity,
                                   bias=shift[:, vec(layer, SHIFT_F), k:k + 1],
                                   scale=shift[:, vec(layer, SCALE_F), k:k + 1]).then_inc(few_hT_act, 1)

            def few_places(layer, g):
                act.wait_ge(few_turned, g + layer * GROUPS + 1)
                act.activation(onehotT, place_bank[0:CAP, 0:T], ACT.Copy).then_inc(few_turn_ready, 1)

            def few_group(layer, g, last):
                for j in range(PER_GROUP):
                    e = layer * EXPERTS + j
                    act.wait_ge(gu_full, g * 2 * PER_GROUP + 2 * e + 1)
                    act.wait_ge(gu_free, g * PER_GROUP + e + 1)
                    act.activation(few_sg[:, j % 2, :], gu_bank[j % 2][0][:, 0:FC * CAP], ACT.Silu)\
                       .then_inc(silu_done, 1)
                if not last:
                    few_modulate(layer, g + 1)
                    few_places(layer, g + 1)

            def experts(layer):
                act.wait_ge(largest_ready, 2 * (layer + 1))
                size = act.value_load(largestI[0:1, layer:layer + 1], min_val=0, max_val=T)
                with act.If(size <= CAP):
                    router(layer)
                    few_modulate(layer, 0)
                    few_places(layer, 0)
                    with act.Fori(0, GROUPS - 1) as g:
                        few_group(layer, g, False)
                    few_group(layer, GROUPS - 1, True)
                with act.Else():
                    act.sem_inc(few_hT_act, GROUPS * KC // 2)
                    act.sem_inc(few_turn_ready, GROUPS)
                    router(layer)
                    dense_experts(layer)

            def dense_experts(layer):
                with act.Fori(0, GROUPS) as g:
                    for j in range(PER_GROUP):
                        e = layer * EXPERTS + j
                        act.wait_ge(gu_full, g * 2 * PER_GROUP + 2 * e + 1)
                        act.wait_ge(gu_free, g * PER_GROUP + e + 1)
                        act.activation(sg[:, j % 2, :], gu_bank[j % 2][0][:, :], ACT.Silu).then_inc(silu_done, 1)

            for b, vv, n in ((b_ada[0], 0, 6), (b_ada_kv, 6, 2), (b_ada[1], 8, 6)):
                act.dma_start(shift[:, vv:vv + n, :], b.rearrange("(j p k) -> p j k", j=n, k=KC)).then_inc(s_small, 16)
            for n, vv in enumerate(GATE_ORDER):
                l, j = divmod(n, 2)
                act.dma_start(gate_bias[32 * n:32 * n + 1, :],
                              b_ada[l].rearrange("(j n) -> j n", n=D)[(GATE_M, GATE_F)[j]:(GATE_M, GATE_F)[j] + 1, :])\
                   .then_inc(s_small, 16)
            for vv, g_ap in ((vec(0, SCALE_M), g_attn[0]), (vec(0, SCALE_F), g_ffn[0]), (KV_SCALE, g_kv),
                             (vec(1, SCALE_M), g_attn[1]), (vec(1, SCALE_F), g_ffn[1])):
                act.dma_start(gains[:, vv, :], g_ap.rearrange("(p k) -> p k", k=KC)).then_inc(s_small, 16)
            def gates(layer, vv):
                if vv == vec(layer, GATE_M):
                    gate(vv, gate_m)

            def attention(layer):
                for u in range(AHEAD[layer]):
                    take(layer, u)
                    gates(layer, SUM_AFTER_UNIT[layer].get(u))
                    if layer == 1 and u == 1:
                        modulate(2, 1)
                for i in range(HEADS + 4):
                    for u in units_done(layer, i):
                        take(layer, u)
                    gates(layer, SUM_IN_STEP[layer].get(i))
                    if layer == 0:
                        if i < HEADS:
                            soft_a(i)
                        if 1 <= i <= HEADS:
                            weights_a(i - 1)
                        if i >= 4 and i % 2 == 0:
                            attn_out((i - 4) // 2, 0)
                    else:
                        if i < HEADS:
                            exps_b(i)
                        if 2 <= i < HEADS + 2:
                            probs_b(i - 2)
                        if i >= 5 and i % 2:
                            attn_out((i - 4) // 2, 1)

            act.preload_act_table_set("natural_log_exp_and_others")
            squares(0)
            rsqrt(0)
            modulate(0)
            for l in range(DEPTH):
                act.dma_start(w_r[:, l, :, 0:GROUPS], pk(w_rg[l])).then_inc(s_route, 16)
                act.dma_start(w_r[:, l, :, GROUPS:], pk(w_re[l])).then_inc(s_route, 16)
                act.dma_start(b_r[:, l, 0:GROUPS], b_rg[l:l + 1, :].broadcast_to([P, GROUPS])).then_inc(s_route, 16)
                act.dma_start(b_r[:, l, GROUPS:], b_re[l:l + 1, :].broadcast_to([P, EXPERTS])).then_inc(s_route, 16)
            attention(0)
            squares(1)
            rsqrt(1)
            gate(vec(0, GATE_F), gate_f)
            modulate(1)
            experts(0)

            act.preload_act_table_set("natural_log_exp_and_others")
            squares(2)
            rsqrt(2)
            modulate(2)
            attention(1)
            squares(3)
            rsqrt(3)
            gate(vec(1, GATE_F), gate_f)
            modulate(3)
            experts(1)
            act.preload_act_table_set("natural_log_exp_and_others")
            squares(4)
            rsqrt(4)

        @block.vector
        def _(dve):
            counts = {}

            def step(semaphore, ins):
                ins.then_inc(semaphore, 1)
                counts[semaphore.name] = counts.get(semaphore.name, 0) + 1

            def settled(semaphore):
                dve.wait_ge(semaphore, counts[semaphore.name])

            def add_part(part, slot, landings, buffer, n):
                dve.wait_ge(a_landed[slot], landings * 16)
                for r in range(ROWS):
                    k = part * ROWS + r
                    w = aring[:, slot, r, :]
                    a = acc[:, buffer, :]
                    if k == 0:
                        ins = dve.tensor_scalar(a, w, cT[:, k:k + 1], None, ALU.mult)
                    else:
                        dve.wait_ge(ada_rows, n * ROWS + r)
                        ins = dve.scalar_tensor_tensor(out=a, in0=w, scalar=cT[:, k:k + 1], in1=a,
                                                       op0=ALU.mult, op1=ALU.add)
                    ins.then_inc(ada_rows, 1)

            def add_rows(n):
                vv, part = n // PARTS, n % PARTS
                if n == 0:
                    dve.wait_ge(s_c, 16)
                if part == 0 and vv >= 2 and vv - 2 not in LATE:
                    dve.wait_ge(out_full, OUT[sum_items(vv - 2)[-1]] + 1)
                if part == 0 and vv - 2 in LATE:
                    dve.wait_ge(late_sum, len(LATE) + 1)
                add_part(part, ada_slot(n), ada_landings(n), vv % 2, n)
                if is_gate(vv) and part == PARTS - 1:
                    row = slice(32 * GATE_ORDER.index(vv), 32 * GATE_ORDER.index(vv) + 1)
                    dve.wait_ge(ada_rows, KC * (vv + 1))
                    dve.tensor_tensor(acc[row, vv % 2, :], acc[row, vv % 2, :], gate_bias[row, :], ALU.add)\
                       .then_inc(bias_added, 1)

            def add_late(part, g):
                n = LATE[0] * PARTS + part
                if part == 0:
                    dve.wait_ge(late_sum, g + 1)
                add_part(part, ada_slot(n), g * 2 + ada_landings(n), 0, g * PARTS + n)

            def late_column(g):
                dve.wait_ge(late_sum, g + 2)
                to = shift[:, bass.ds(g + LATE[0], 1), :].rearrange("p o k -> p (o k)")
                dve.tensor_tensor(to, late_bank, to, ALU.add).then_inc(late_ready, 1)

            def late_scales():
                dve.wait_ge(late_ready, len(LATE) + 1)
                for vv in LATE:
                    if is_scale(vv):
                        step(vec_ready, dve.scalar_tensor_tensor(out=shift[:, vv, :], in0=shift[:, vv, :], scalar=1.0,
                                                                 in1=gains[:, vv, :], op0=ALU.add, op1=ALU.mult))

            def column(vv):
                i = OUT[("sum", vv, 0)]
                dve.wait_ge(out_full, i + 1)
                if is_scale(vv):
                    scale_sum(vv, out_bank[i % 2][:, 0:KC])
                else:
                    step(vec_ready, dve.tensor_tensor(shift[:, vv, :], out_bank[i % 2][:, 0:KC], shift[:, vv, :],
                                                      ALU.add))

            def scale_sum(vv, total):
                step(scale_step, dve.scalar_tensor_tensor(out=shift[:, vv, :], in0=total, scalar=1.0,
                                                          in1=shift[:, vv, :], op0=ALU.add, op1=ALU.add))
                settled(scale_step)
                step(vec_ready, dve.tensor_tensor(shift[:, vv, :], shift[:, vv, :], gains[:, vv, :], ALU.mult))

            def normalise(norm, last=False):
                parts = [TT * UNITS if m in (1, 3) else TT for m in range(norm + 1)]
                dve.wait_ge(ss_ready, sum(parts))
                if norm in (1, 3):
                    step(ss_sum, dve.tensor_reduce(ss[:, :], ss4[:, :, :], AX_X, ALU.add))
                    settled(ss_sum)
                step(nrm, dve.tensor_scalar(ms[:, :], ss[:, :], 1.0 / D, EPS, ALU.mult, ALU.add))
                dve.wait_ge(rsqrt_ready, 2 * norm + 2)
                settled(nrm)
                step(nrm, dve.tensor_tensor(rtmp[:, 1, :], rtmp[:, 0, :], rtmp[:, 0, :], ALU.mult))
                settled(nrm)
                step(nrm, dve.scalar_tensor_tensor(out=rtmp[:, 2, :], in0=rtmp[:, 1, :], scalar=-0.5, in1=ms[:, :],
                                                   op0=ALU.mult, op1=ALU.mult))
                settled(nrm)
                step(nrm, dve.scalar_tensor_tensor(out=rstd[:, :], in0=rtmp[:, 2, :], scalar=1.5, in1=rtmp[:, 0, :],
                                                   op0=ALU.add, op1=ALU.mult))
                settled(nrm)
                for t in range(TT):
                    if last:
                        step(o_step, dve.scalar_tensor_tensor(out=xn[:, t, :], in0=x[:, t, :], scalar=rstd[:, t:t + 1],
                                                              in1=gfin[:, :], op0=ALU.mult, op1=ALU.mult))
                    else:
                        step(nrm, dve.tensor_scalar(diag[:, t, :], ident[:, :], rstd[:, t:t + 1], None, ALU.mult))
                if norm in (1, 3):
                    for t in range(TT):
                        dve.tensor_scalar(xn[:, t, :], x[:, t, :], rstd[:, t:t + 1], None, ALU.mult).then_inc(xn_ready, 1)

            def modulate(norm, stream=0):
                dst, sh, a = modulated(norm)[stream]
                settled(vec_ready)
                for j in (0, 2):
                    dve.wait_ge(turned, 4 * norm + j + 1)
                    for n in range(2):
                        k = 2 * j + n
                        dve.tensor_scalar(dst[:, k, :], turn_bank[j][:, n * T:(n + 1) * T], shift[:, a, k:k + 1],
                                          shift[:, sh, k:k + 1], ALU.mult, ALU.add).then_inc(hT_dve, 1)

            def softplus_a(h):
                dve.wait_ge(soft_ready, h + 1)
                if h >= 2:
                    dve.wait_ge(s_full, h - 1)
                dve.scalar_tensor_tensor(out=sp[:, h % 2, :], in0=za_bank[h % 4][:, 0:CAUSAL], scalar=0.0,
                                         in1=soft[:, h % 2, :], op0=ALU.max, op1=ALU.add).then_inc(sp_ready, 1)

            def bias_max_b(h):
                dve.wait_ge(z_full, HEADS + h + 1)
                if h >= 4:
                    dve.wait_ge(s_full, HEADS + h - 3)
                slope = 2.0 ** (-8.0 * (h + 1) / HEADS)
                z = zb[:, h % 4, :]
                step(b_max, dve.scalar_tensor_tensor(out=z, in0=distB[:, :], scalar=slope / SCALE,
                                                     in1=z_bank[h % 2][:, 0:CAUSAL], op0=ALU.mult, op1=ALU.add))
                settled(b_max)
                if h >= 2:
                    dve.wait_ge(p_ready, 2 * (h - 1))
                dve.tensor_reduce(mx[:, h % 2, 0:1], z[:, 0:P], AX_X, ALU.max)
                step(b_max, dve.tensor_reduce(mx[:, h % 2, 1:2], z[:, P:CAUSAL], AX_X, ALU.max))
                settled(b_max)
                step(b_max, dve.tensor_scalar(nmx[:, h % 2, :], mx[:, h % 2, :], -SCALE, None, ALU.mult))

            def norm_b(h):
                dve.wait_ge(p_ready, 2 * (h + 1))
                step(b_norm, dve.reciprocal(rden[:, h % 2, :], den[:, h % 2, :]))
                settled(b_norm)
                for t, cols in ((0, slice(0, P)), (1, slice(P, CAUSAL))):
                    step(b_norm, dve.tensor_scalar(zb[:, h % 4, cols], zb[:, h % 4, cols], rden[:, h % 2, t:t + 1],
                                                   None, ALU.mult))

            def residual(item):
                i, u = OUT[item], item[1]
                cols = slice(u * COLS, (u + 1) * COLS)
                dve.wait_ge(out_full, i + 1)
                tmp = otmp[:, u % 2, :, :]
                step(o_step, dve.tensor_tensor(tmp, out_bank[i % 2][:, :].rearrange("p (t n) -> p t n", t=TT),
                                               gate_m[:, cols].unsqueeze(1).broadcast_to([P, TT, COLS]), ALU.mult))
                settled(o_step)
                step(o_step, dve.tensor_tensor(x[:, :, cols], x[:, :, cols], tmp, ALU.add))

            def first_max(src, peak, hit, score, best, dst):
                r(dve.tensor_reduce(peak, src, AX_X, ALU.max))
                r(dve.tensor_tensor(hit, src, peak.unsqueeze(2).broadcast_to([P, TT, 4]), ALU.is_equal))
                r(dve.tensor_tensor(score, hit, desc[:, :].unsqueeze(1).broadcast_to([P, TT, 4]), ALU.mult))
                r(dve.tensor_reduce(best, score, AX_X, ALU.max))
                r(dve.tensor_tensor(dst, score, best.unsqueeze(2).broadcast_to([P, TT, 4]), ALU.is_equal))

            le, first, rest, second = rt[:, 5, :, :], rt[:, 6, :, :], rt[:, 7, :, :], rt[:, 8, :, :]

            def r(ins):
                step(route, ins)
                settled(route)

            def wide(row):
                return row.unsqueeze(2).broadcast_to([P, TT, 4])

            def router(layer):
                start = R_STEPS * layer
                i = OUT[("route", layer)]
                dve.wait_ge(out_full, i + 1)
                n = GROUPS + EXPERTS
                r(dve.tensor_tensor(lg[:, :, :], out_bank[i % 2][:, 0:64].rearrange("p (t n) -> p t n", t=TT)[:, :, 0:n],
                                    b_r[:, layer, :].unsqueeze(1).broadcast_to([P, TT, n]), ALU.add))
                groups = lg[:, :, 0:GROUPS]
                in_group = rt[:, 0, :, :]
                first_max(groups, r1[:, 0, :], rt[:, 1, :, :], rt[:, 2, :, :], r1[:, 1, :], in_group)
                r(dve.tensor_tensor(rt[:, 4, :, :], groups, wide(r1[:, 0, :]), ALU.subtract))
                assert counts[route.name] - start == R_EXP1
                r(dve.tensor_tensor(le_sel[:, :, :].rearrange("p t (g j) -> p t g j", g=GROUPS),
                                    lg[:, :, GROUPS:].rearrange("p t (g j) -> p t g j", g=GROUPS),
                                    in_group.unsqueeze(3).broadcast_to([P, TT, GROUPS, PER_GROUP]), ALU.mult))
                r(dve.tensor_reduce(le, le_sel[:, :, :].rearrange("p t (g j) -> p t j g", g=GROUPS), AX_X, ALU.add))
                first_max(le, r1[:, 2, :], rt[:, 9, :, :], rt[:, 10, :, :], r1[:, 3, :], first)
                r(dve.scalar_tensor_tensor(out=rest, in0=first, scalar=-3.0e38, in1=le, op0=ALU.mult, op1=ALU.add))

            def ranks(layer):
                i = OUT[("rank", layer)]
                dve.wait_ge(out_full, i + 1)
                b = out_bank[i % 2]
                r(dve.tensor_copy(where[:, 0, :, 0:GROUPS], b[:, 0:TT * GROUPS].rearrange("p (t g) -> p t g", t=TT)))
                r(dve.tensor_copy(where[:, 1, :, 0:GROUPS], rt[:, 0, :, :]))
                place(layer, 0)
                r(dve.tensor_reduce(largest[:, layer:layer + 1], b[:, TT * GROUPS:(TT + 1) * GROUPS], AX_X, ALU.max))
                dve.tensor_copy(largestI[:, layer:layer + 1], largest[:, layer:layer + 1]).then_inc(largest_ready, 2)

            def experts_router(layer):
                start = R_STEPS * layer
                in_group = rt[:, 0, :, :]
                first_max(rest, r1[:, 4, :], rt[:, 9, :, :], rt[:, 10, :, :], r1[:, 5, :], second)
                r(dve.tensor_tensor(r1[:, 6, :], r1[:, 4, :], r1[:, 2, :], ALU.subtract))
                assert counts[route.name] - start == R_EXP2
                dve.wait_ge(route_exp, 2 * layer + 1)
                r(dve.tensor_reduce(r1[:, 7, :], rt[:, 4, :, :], AX_X, ALU.add))
                r(dve.reciprocal(r1[:, 8, :], r1[:, 7, :]))
                dve.wait_ge(route_exp, 2 * layer + 2)
                r(dve.tensor_scalar(r1[:, 9, :], r1[:, 6, :], 1.0, None, ALU.add))
                r(dve.reciprocal(r1[:, 10, :], r1[:, 9, :]))
                r(dve.tensor_tensor(r1[:, 11, :], r1[:, 10, :], r1[:, 8, :], ALU.mult))
                r(dve.tensor_tensor(r1[:, 0, :], r1[:, 6, :], r1[:, 11, :], ALU.mult))
                r(dve.tensor_tensor(rt[:, 9, :, :], first, wide(r1[:, 11, :]), ALU.mult))
                r(dve.tensor_tensor(rt[:, 10, :, :], second, wide(r1[:, 0, :]), ALU.mult))
                r(dve.tensor_tensor(rt[:, 11, :, :], rt[:, 9, :, :], rt[:, 10, :, :], ALU.add))
                r(dve.tensor_tensor(comb[:, :, :].rearrange("p t (g j) -> p t g j", g=GROUPS),
                                    in_group.unsqueeze(3).broadcast_to([P, TT, GROUPS, PER_GROUP]),
                                    rt[:, 11, :, :].unsqueeze(2).broadcast_to([P, TT, GROUPS, PER_GROUP]), ALU.mult))
                assert counts[route.name] - start == R_STEPS

            def place(layer, g):
                n = F_STEPS * layer * GROUPS
                if not (isinstance(g, int) and g == 0):
                    dve.wait_ge(few_turned, g + layer * GROUPS)
                dve.tensor_copy(where_g[:, :, :], where[:, :, :, bass.ds(g, 1)].rearrange("p a t o -> p a (t o)"))\
                   .then_inc(placed, 1)
                dve.wait_ge(placed, g * F_STEPS + n + 1)
                for t in range(TT):
                    dve.tensor_scalar(onehot[:, t, :], places[:, :], where_g[:, 0, t:t + 1], where_g[:, 1, t:t + 1],
                                      ALU.is_equal, ALU.mult).then_inc(placed, 1)

            def combine(layer, g):
                dve.tensor_copy(comb_g[:, :, :], comb[:, :, bass.ds(g * PER_GROUP, PER_GROUP)]).then_inc(comb_ready, 1)

            def few_gathered(layer, g):
                n = layer * GROUPS
                dve.wait_ge(few_full, g * 3 + 3 * n + 1)
                for k in range(KC // 2):
                    dve.tensor_scalar(few_hT[:, k, :], few_bank[0][:, k * CAP:(k + 1) * CAP],
                                      shift[:, vec(layer, SCALE_F), k:k + 1], shift[:, vec(layer, SHIFT_F), k:k + 1],
                                      ALU.mult, ALU.add).then_inc(few_hT_dve, 1)

            def few_combine(layer, g):
                dve.wait_ge(few_full, g * 3 + 3 * layer * GROUPS + 3)
                dve.tensor_copy(few_comb, comb_bank[:, 0:PER_GROUP * CAP]).then_inc(few_comb_ready, 1)

            def few_hidden(layer, j, g):
                e = layer * EXPERTS + j
                weight = few_comb[:, j * CAP:(j + 1) * CAP].unsqueeze(1).broadcast_to([P, FC, CAP])
                dve.wait_ge(gu_full, g * 2 * PER_GROUP + 2 * e + 2)
                if j == 0:
                    dve.wait_ge(few_comb_ready, g + layer * GROUPS + 1)
                dve.tensor_tensor(few_uc[:, j % 2, :].rearrange("p (f s) -> p f s", f=FC),
                                  gu_bank[j % 2][1][:, 0:FC * CAP].rearrange("p (f s) -> p f s", f=FC),
                                  weight, ALU.mult).then_inc(few_up, 1)
                if j >= 2:
                    dve.wait_ge(y_full, g * 4 * PER_GROUP + 4 * (e - 1))
                dve.wait_ge(silu_done, g * PER_GROUP + e + 1)
                dve.wait_ge(few_up, g * PER_GROUP + e + 1)
                dve.tensor_tensor(few_hid[:, j % 2, :], few_sg[:, j % 2, :], few_uc[:, j % 2, :], ALU.mult)\
                   .then_inc(gu_free, 1)

            def few_output(layer, g):
                for half in range(2):
                    cols = slice(half * 512, half * 512 + 512)
                    dve.wait_ge(y_full, g * 4 * PER_GROUP + 4 * PER_GROUP * (layer * GROUPS + 1) - 2 + 2 * half)
                    dve.tensor_tensor(few_y[:, cols], few_y_bank[half][0:CAP, :], gate_f[0:CAP, cols], ALU.mult)\
                       .then_inc(few_y_ready, 1)

            def few_add(layer, g, last):
                n = 4 * layer * GROUPS
                for q in range(4):
                    t, half = divmod(q, 2)
                    cols = slice(half * 512, half * 512 + 512)
                    dve.wait_ge(few_back, g * 4 + n + q + 1)
                    dve.wait_ge(few_added, g * 4 + n + q + 1)
                    ins = dve.tensor_tensor(x[:, t, cols], x[:, t, cols], back_bank[q][:, :], ALU.add)
                    ins.then_inc(few_added, 1)
                    if last and q >= 2:
                        dve.wait_ge(few_added, n + 4 * GROUPS + (2 if q == 2 else 4))
                        dve.sem_inc(moe_done, 1)

            def few_group(layer, g, last):
                for j in range(PER_GROUP):
                    few_hidden(layer, j, g)
                    if j == 0 and not last:
                        place(layer, g + 1)
                        combine(layer, g + 1)
                    if layer == 0 and last:
                        add_rows(EARLY + j)
                    elif layer == 0 and j < 3:
                        add_late(j, g)
                if not last:
                    few_gathered(layer, g + 1)
                few_output(layer, g)
                if not last:
                    few_combine(layer, g + 1)
                    if layer == 0:
                        add_late(3, g)
                few_add(layer, g, last)
                if layer == 0 and not last:
                    late_column(g)

            def experts(layer):
                dve.wait_ge(largest_ready, 2 * (layer + 1))
                size = dve.value_load(largestI[0:1, layer:layer + 1], min_val=0, max_val=T)
                with dve.If(size <= CAP):
                    dve.sem_inc(y_free, 4 * EXPERTS)
                    dve.sem_inc(y_sum, Y_GROUP * GROUPS)
                    experts_router(layer)
                    combine(layer, 0)
                    few_gathered(layer, 0)
                    dve.wait_ge(gate_ready, 4 * (layer + 1))
                    few_combine(layer, 0)
                    with dve.Fori(0, GROUPS - 1) as g:
                        few_group(layer, g, False)
                    few_group(layer, GROUPS - 1, True)
                with dve.Else():
                    for semaphore, n in ((placed, F_STEPS * (GROUPS - 1)), (comb_ready, GROUPS), (few_hT_dve, GROUPS * KC // 2),
                                         (few_comb_ready, GROUPS), (few_up, EXPERTS), (few_y_ready, 2 * GROUPS),
                                         (few_added, 4 * GROUPS)):
                        dve.sem_inc(semaphore, n)
                    counts[route.name] = R_STEPS * layer + R_RANK
                    experts_router(layer)
                    dve.wait_ge(gate_ready, 4 * (layer + 1))
                    dense_experts(layer)
                    if layer == 0:
                        for j in range(PARTS):
                            add_rows(EARLY + j)
                    dve.wait_ge(y_sum, Y_GROUP * GROUPS * (layer + 1))
                    dve.sem_inc(moe_done, TT)

            def dense_experts(layer):
                with dve.Fori(0, GROUPS - 1) as g:
                    dense_group(layer, g, False)
                dense_group(layer, GROUPS - 1, True)

            def dense_group(layer, g, last):
                y_base = layer * Y_GROUP * GROUPS

                def hidden(j):
                    e = layer * EXPERTS + j
                    dve.wait_ge(silu_done, g * PER_GROUP + e + 1)
                    dve.wait_ge(gu_full, g * 2 * PER_GROUP + 2 * e + 2)
                    dve.tensor_tensor(hid[:, j % 2, :], sg[:, j % 2, :], gu_bank[j % 2][1][:, :], ALU.mult)\
                       .then_inc(gu_free, 1)

                def add_output(j):
                    e = layer * EXPERTS + j
                    for q in range(4):
                        t, half = divmod(q, 2)
                        cols = slice(half * 512, half * 512 + 512)
                        dve.wait_ge(y_full, g * 4 * PER_GROUP + 4 * e + q + 1)
                        dve.wait_ge(y_sum, g * Y_GROUP + y_base + (1 if j == 0 else 4 * j + q - 2))
                        dve.scalar_tensor_tensor(out=ytmp[:, q, :], in0=y_bank[q][:, :],
                                                 scalar=comb_g[:, t, j:j + 1], in1=gate_f[:, cols],
                                                 op0=ALU.mult, op1=ALU.mult).then_inc(y_free, 1)
                        dve.wait_ge(y_free, g * 4 * PER_GROUP + 4 * e + q + 5)
                        dve.tensor_tensor(x[:, t, cols], x[:, t, cols], ytmp[:, q, :], ALU.add).then_inc(y_sum, 1)

                dve.tensor_copy(comb_g[:, :, :], comb[:, :, bass.ds(g * PER_GROUP, PER_GROUP)]).then_inc(y_sum, 1)
                hidden(0)
                for j in range(PER_GROUP):
                    if j + 1 < PER_GROUP:
                        hidden(j + 1)
                    add_output(j)
                    if layer == 0 and not last:
                        add_late(j, g)
                if layer == 0 and not last:
                    late_column(g)

            def columns(vv):
                if vv is not None and not is_gate(vv):
                    column(vv)

            def attention(layer):
                for u in range(AHEAD[layer]):
                    for n in ADA_AT_UNIT[layer].get(u, []):
                        add_rows(n)
                    columns(SUM_AFTER_UNIT[layer].get(u))
                    if layer == 1 and u == 0:
                        modulate(2, 1)
                for i in range(HEADS + 1):
                    if layer == 0 and i < HEADS:
                        softplus_a(i)
                    if layer == 1 and i < HEADS:
                        bias_max_b(i)
                    if layer == 1 and i >= 1:
                        norm_b(i - 1)
                    columns(SUM_IN_STEP[layer].get(i))
                    for n in ADA_IN_STEP[layer].get(i, []):
                        add_rows(n)

            dve.sem_inc(gu_free, 2)
            dve.sem_inc(y_free, 4)
            dve.sem_inc(few_added, 4)
            dve.sem_inc(late_ready, 1)
            for n in range(PARTS):
                add_rows(n)
            dve.wait_ge(s_const, CONSTS)
            normalise(0)
            for n in range(PARTS, 2 * PARTS):
                add_rows(n)
            dve.wait_ge(s_small, SMALL)
            column(0)
            column(1)
            modulate(0)
            attention(0)
            dve.wait_ge(gate_ready, 2)
            for u in range(UNITS):
                residual(("o0", u))
            normalise(1)
            modulate(1)
            dve.wait_ge(s_route, ROUTE)
            router(0)
            ranks(0)
            experts(0)

            late_scales()
            column(9)
            normalise(2)
            modulate(2)
            attention(1)
            dve.wait_ge(gate_ready, 6)
            for u in range(UNITS):
                residual(("o1", u))
            normalise(3)
            modulate(3)
            router(1)
            ranks(1)
            experts(1)
            dve.wait_ge(s_gfin, 16)
            normalise(4, last=True)


_INS = ["x", "c", "w_ada", "b_ada", "g_attn", "g_ffn", "w_qkv_a", "w_o_a", "w_ada_kv", "b_ada_kv", "g_kv", "w_kv",
        "w_q_b", "w_o_b", "w_rg", "b_rg", "w_re", "b_re", "w_gate", "w_up", "w_down", "g_final"]


def kernel(**inputs):
    import numpy as np
    import concourse.bacc as bacc
    from concourse.bass_utils import run_bass_kernel_spmd

    nc = bacc.Bacc("TRN2", target_bir_lowering=False, num_devices=1)
    arrays, args = {}, []
    for name in _INS:
        a = np.ascontiguousarray(inputs[name])
        arrays[f"in_{name}"] = a
        args.append(nc.dram_tensor(f"in_{name}", a.shape, mybir.dt.from_np(a.dtype), kind="ExternalInput").ap())
    out = nc.dram_tensor("out_y", (1, T, D), F32, kind="ExternalOutput").ap()
    program(nc, *args, out)
    result = run_bass_kernel_spmd(nc, [arrays], core_ids=[0])
    return result.results[0]["out_y"]
```
